# Optimizing a Trainium2 kernel written in Bass

```python
import math
import jax, jax.numpy as jnp
from jax import lax
import numpy as np
import jax
import jax.numpy as jnp

D_MODEL = 1024
BATCH = 1
SEQ = 256
DEPTH = 2

N_EVEN = (DEPTH + 1) // 2
N_ODD = DEPTH // 2
D_FF = 2816
N_MOD = 9
EPS = 1e-6

ATT_HEADS = 4
ATT_QK_DIM = 64
ATT_V_DIM = 2 * ATT_QK_DIM
QK_COLS = ATT_HEADS * 2 * ATT_QK_DIM
ATT_WIDTH = ATT_HEADS * ATT_V_DIM
Q_BLOCK = 128

POOL_WINDOWS = (2, 4, 8, 16)
POOL_GROUPS = len(POOL_WINDOWS)
POOL_WIDTH = D_MODEL // 2
POOL_GROUP_DIM = POOL_WIDTH // POOL_GROUPS

AB_IN_WIDTH = 2 * QK_COLS + ATT_WIDTH + POOL_WIDTH
MIX_WIDTH = ATT_WIDTH + POOL_WIDTH

CONV_WIDTH = D_MODEL
CONV_K = 3


def rmsnorm(x, g):
    xf = x.astype(jnp.float32)
    y = xf * lax.rsqrt(jnp.mean(xf * xf, axis=-1, keepdims=True) + EPS)
    return (y * g.astype(jnp.float32)).astype(x.dtype)

def modulated_norm(x, g, shift, scale):
    return rmsnorm(x, g) * (1 + scale) + shift

def swiglu(h, wg, wu, wd):
    return (jax.nn.silu(h @ wg) * (h @ wu)) @ wd

def diff_attention(q1, q2, k1, k2, v, lam):
    b, h, s, _ = q1.shape
    nb = s // Q_BLOCK
    scale = ATT_QK_DIM ** -0.5
    kpos = jnp.arange(s)

    def blocks(q):
        return q.reshape(b, h, nb, Q_BLOCK, q.shape[-1]).transpose(2, 0, 1, 3, 4)

    def one_block(args):
        qa, qb, i = args
        qpos = i * Q_BLOCK + jnp.arange(Q_BLOCK)
        mask = kpos[None, :] <= qpos[:, None]

        def probs(q, k):
            sc = jnp.einsum('bhqd,bhkd->bhqk', q, k).astype(jnp.float32) * scale
            sc = jnp.where(mask, sc, -jnp.inf)
            return jax.nn.softmax(sc, axis=-1)

        w = probs(qa, k1) - lam * probs(qb, k2)
        return jnp.einsum('bhqk,bhkd->bhqd', w.astype(v.dtype), v)

    out = lax.map(one_block, (blocks(q1), blocks(q2), jnp.arange(nb)))
    return out.transpose(1, 2, 0, 3, 4).reshape(b, h, s, v.shape[-1])

def multiscale_pool(u, pool_w, pool_scale):
    b, s, _ = u.shape
    uf = u.astype(jnp.float32).reshape(b, s, POOL_GROUPS, POOL_GROUP_DIM)
    cs = jnp.cumsum(uf, axis=1)
    t = jnp.arange(s)
    outs = []
    for g, w in enumerate(POOL_WINDOWS):
        csg = cs[:, :, g]
        lagged = jnp.pad(csg, ((0, 0), (w, 0), (0, 0)))[:, :s]
        cnt = jnp.minimum(t + 1, w).astype(jnp.float32)[None, :, None]
        outs.append((csg - lagged) / cnt - uf[:, :, g])
    d = jnp.stack(outs, axis=2)
    y = jnp.einsum('bsgc,gcd->bsgd', d, pool_w.astype(jnp.float32))
    y = y.reshape(b, s, POOL_WIDTH) * pool_scale.astype(jnp.float32)
    return y.astype(u.dtype)

def attn_pool_mixer(h, layer_idx, w_in, qk_g, lq1, lk1, lq2, lk2, subln_g, pool_w, pool_scale, w_out):
    b, s, _ = h.shape
    proj = h @ w_in
    q, k, v, u = jnp.split(proj, [QK_COLS, 2 * QK_COLS, 2 * QK_COLS + ATT_WIDTH], axis=-1)
    q = rmsnorm(q.reshape(b, s, ATT_HEADS, 2, ATT_QK_DIM), qk_g[0]).transpose(0, 2, 3, 1, 4)
    k = rmsnorm(k.reshape(b, s, ATT_HEADS, 2, ATT_QK_DIM), qk_g[1]).transpose(0, 2, 3, 1, 4)
    v = v.reshape(b, s, ATT_HEADS, ATT_V_DIM).transpose(0, 2, 1, 3)
    lam_init = 0.8 - 0.6 * math.exp(-0.3 * layer_idx)
    f32 = jnp.float32
    lam = (jnp.exp(jnp.sum(lq1.astype(f32) * lk1.astype(f32)))
           - jnp.exp(jnp.sum(lq2.astype(f32) * lk2.astype(f32))) + lam_init)
    o = diff_attention(q[:, :, 0], q[:, :, 1], k[:, :, 0], k[:, :, 1], v, lam)
    o = rmsnorm(o, subln_g) * (1 - lam_init)
    o = o.transpose(0, 2, 1, 3).reshape(b, s, ATT_WIDTH)
    p = multiscale_pool(u, pool_w, pool_scale)
    return jnp.concatenate([o, p], axis=-1) @ w_out

def short_conv_mixer(h, w_in, conv_w, w_out):
    b_gate, c_gate, xin = jnp.split(h @ w_in, 3, axis=-1)
    v = c_gate * xin
    s = v.shape[1]
    vp = jnp.pad(v, ((0, 0), (CONV_K - 1, 0), (0, 0)))
    y = conv_w[0] * vp[:, 0:s]
    for j in range(1, CONV_K):
        y = y + conv_w[j] * vp[:, j:j + s]
    return (b_gate * y) @ w_out

def first_inputs(seed: int = 0) -> dict:
    key = jax.random.key(seed)
    ks = jax.random.split(key, 24)
    f32 = jnp.float32

    def nrm(k, shape, scale):
        return jax.random.normal(k, shape, f32) * scale

    D = D_MODEL
    return {
        "x": nrm(ks[0], (BATCH, SEQ, D), 1.0),
        "c": nrm(ks[1], (BATCH, D), 1.0),
        "norm_g": 1.0 + nrm(ks[2], (DEPTH, 3, D), 0.05),
        "w_ada": nrm(ks[3], (DEPTH, D, N_MOD * D), D ** -0.5),
        "b_ada": nrm(ks[4], (DEPTH, N_MOD * D), 0.02),
        "ffn_wg": nrm(ks[5], (DEPTH, 2, D, D_FF), D ** -0.5),
        "ffn_wu": nrm(ks[6], (DEPTH, 2, D, D_FF), D ** -0.5),
        "ffn_wd": nrm(ks[7], (DEPTH, 2, D_FF, D), D_FF ** -0.5),
        "w_in_ab": nrm(ks[8], (N_EVEN, D, AB_IN_WIDTH), D ** -0.5),
        "qk_norm_g": 1.0 + nrm(ks[9], (N_EVEN, 2, ATT_QK_DIM), 0.05),
        "lambda_q1": nrm(ks[10], (N_EVEN, ATT_QK_DIM), 0.1),
        "lambda_k1": nrm(ks[11], (N_EVEN, ATT_QK_DIM), 0.1),
        "lambda_q2": nrm(ks[12], (N_EVEN, ATT_QK_DIM), 0.1),
        "lambda_k2": nrm(ks[13], (N_EVEN, ATT_QK_DIM), 0.1),
        "subln_g": 1.0 + nrm(ks[14], (N_EVEN, ATT_V_DIM), 0.05),
        "pool_w": nrm(ks[15], (N_EVEN, POOL_GROUPS, POOL_GROUP_DIM, POOL_GROUP_DIM), POOL_GROUP_DIM ** -0.5),
        "pool_scale": 1.0 + nrm(ks[16], (N_EVEN, POOL_WIDTH), 0.1),
        "w_out_ab": nrm(ks[17], (N_EVEN, MIX_WIDTH, D), MIX_WIDTH ** -0.5),
        "w_in_c": nrm(ks[18], (N_ODD, D, 3 * CONV_WIDTH), D ** -0.5),
        "conv_w": nrm(ks[19], (N_ODD, CONV_K, CONV_WIDTH), CONV_K ** -0.5),
        "w_out_c": nrm(ks[20], (N_ODD, CONV_WIDTH, D), CONV_WIDTH ** -0.5),
    }

def first_block(x, c, norm_g, w_ada, b_ada, ffn_wg, ffn_wu, ffn_wd, w_in_ab, qk_norm_g,
              lambda_q1, lambda_k1, lambda_q2, lambda_k2, subln_g, pool_w, pool_scale,
              w_out_ab, w_in_c, conv_w, w_out_c):
    b = x.shape[0]
    c_act = jax.nn.silu(c)
    for l in range(DEPTH):
        mod = (c_act @ w_ada[l] + b_ada[l]).reshape(b, N_MOD, 1, D_MODEL)
        sh1, sc1, g1, sh2, sc2, g2, sh3, sc3, g3 = [mod[:, i] for i in range(N_MOD)]
        h = modulated_norm(x, norm_g[l, 0], sh1, sc1)
        x = x + 0.5 * g1 * swiglu(h, ffn_wg[l, 0], ffn_wu[l, 0], ffn_wd[l, 0])
        h = modulated_norm(x, norm_g[l, 1], sh2, sc2)
        if l % 2 == 0:
            e = l // 2
            m = attn_pool_mixer(h, l, w_in_ab[e], qk_norm_g[e], lambda_q1[e], lambda_k1[e],
                                lambda_q2[e], lambda_k2[e], subln_g[e], pool_w[e],
                                pool_scale[e], w_out_ab[e])
        else:
            o = l // 2
            m = short_conv_mixer(h, w_in_c[o], conv_w[o], w_out_c[o])
        x = x + g2 * m
        h = modulated_norm(x, norm_g[l, 2], sh3, sc3)
        x = x + 0.5 * g3 * swiglu(h, ffn_wg[l, 1], ffn_wu[l, 1], ffn_wd[l, 1])
    return x


DN_HEADS = 4
DN_HEAD_DIM = 128
DN_KEY_DIM = DN_HEADS * DN_HEAD_DIM
DN_VAL_DIM = DN_HEADS * DN_HEAD_DIM
DN_CONV = 4
DN_CHUNK = 64
CV_CHANNELS = 512
CV_KERNEL = 31
MLA_HEADS = 4
MLA_Q_LORA = 384
MLA_KV_LORA = 256
MLA_NOPE = 128
MLA_ROPE = 64
MLA_V = 128
ATTN_BLOCK = 128
ROPE_THETA = 10000.0
N_BRANCHES = 3
DEEPNORM_ALPHA = (2 * DEPTH) ** 0.25
DEEPNORM_BETA = (8 * DEPTH) ** -0.25
NORM_EPS = 1e-5
IN_SIZES = (DN_KEY_DIM, DN_KEY_DIM, DN_VAL_DIM, DN_VAL_DIM, DN_HEADS, DN_HEADS,
            2 * CV_CHANNELS, MLA_Q_LORA, MLA_KV_LORA, MLA_ROPE, N_BRANCHES * D_MODEL)
D_IN = sum(IN_SIZES)


def _split_points():
    return [int(v) for v in np.cumsum(IN_SIZES)[:-1]]

def layer_norm(x, g, b):
    xf = x.astype(jnp.float32)
    mu = jnp.mean(xf, axis=-1, keepdims=True)
    var = jnp.mean(jnp.square(xf - mu), axis=-1, keepdims=True)
    return ((xf - mu) * lax.rsqrt(var + NORM_EPS) * g + b).astype(x.dtype)

def rms_norm(x, w):
    xf = x.astype(jnp.float32)
    return (xf * lax.rsqrt(jnp.mean(jnp.square(xf), axis=-1, keepdims=True) + NORM_EPS) * w).astype(x.dtype)

def l2_normalize(x):
    xf = x.astype(jnp.float32)
    return xf * lax.rsqrt(jnp.sum(jnp.square(xf), axis=-1, keepdims=True) + 1e-6)

def swiglu_2(x, w_gate, w_up, w_down):
    return (jax.nn.silu(x @ w_gate) * (x @ w_up)) @ w_down

def causal_depthwise_conv(x, w):
    k, c = w.shape
    return lax.conv_general_dilated(
        x, w[:, None, :].astype(x.dtype), window_strides=(1,), padding=[(k - 1, 0)],
        dimension_numbers=('NWC', 'WIO', 'NWC'), feature_group_count=c)

def rope_tables(positions):
    half = MLA_ROPE // 2
    inv_freq = ROPE_THETA ** (-jnp.arange(half, dtype=jnp.float32) / half)
    ang = positions.astype(jnp.float32)[..., None] * inv_freq
    return jnp.cos(ang), jnp.sin(ang)

def apply_rope(x, cos, sin):
    half = x.shape[-1] // 2
    xf = x.astype(jnp.float32)
    x1, x2 = xf[..., :half], xf[..., half:]
    return jnp.concatenate([x1 * cos - x2 * sin, x2 * cos + x1 * sin], axis=-1).astype(x.dtype)

def gated_delta_rule(q, k, v, g, beta):
    b, t, h, dk = q.shape
    dv = v.shape[-1]
    c = DN_CHUNK
    n = t // c
    f32 = jnp.float32

    def chunks(a):
        a = a.reshape(b, n, c, h, *a.shape[3:])
        return jnp.moveaxis(a, (1, 3), (0, 2))

    q = chunks(q.astype(f32)) * (dk ** -0.5)
    k = chunks(k.astype(f32))
    v = chunks(v.astype(f32))
    beta = chunks(beta.astype(f32))
    g = jnp.cumsum(chunks(g.astype(f32)), axis=-1)
    causal = jnp.tril(jnp.ones((c, c), dtype=bool))
    strict = jnp.tril(jnp.ones((c, c), dtype=bool), -1)
    decay = jnp.exp(jnp.where(causal, g[..., :, None] - g[..., None, :], -jnp.inf))
    kk = jnp.einsum('nbhik,nbhjk->nbhij', k, k)
    a_mat = jnp.where(strict, beta[..., None] * kk * decay, 0.0) + jnp.eye(c, dtype=f32)
    rhs = jnp.concatenate([v * beta[..., None], k * (beta * jnp.exp(g))[..., None]], axis=-1)
    sol = lax.linalg.triangular_solve(a_mat, rhs, left_side=True, lower=True, unit_diagonal=True)
    u, w = sol[..., :dv], sol[..., dv:]
    qk = jnp.where(causal, jnp.einsum('nbhik,nbhjk->nbhij', q, k) * decay, 0.0)
    q_dec = q * jnp.exp(g)[..., None]
    g_last = g[..., -1]
    k_dec = k * jnp.exp(g_last[..., None] - g)[..., None]

    def step(state, xs):
        u_i, w_i, qk_i, q_dec_i, k_dec_i, gl_i = xs
        v_new = u_i - jnp.einsum('bhck,bhkv->bhcv', w_i, state)
        o = jnp.einsum('bhck,bhkv->bhcv', q_dec_i, state) + jnp.einsum('bhij,bhjv->bhiv', qk_i, v_new)
        state = state * jnp.exp(gl_i)[..., None, None] + jnp.einsum('bhck,bhcv->bhkv', k_dec_i, v_new)
        return state, o

    s0 = jnp.zeros((b, h, dk, dv), f32)
    _, o = lax.scan(step, s0, (u, w, qk, q_dec, k_dec, g_last))
    return jnp.moveaxis(o, (0, 2), (1, 3)).reshape(b, t, h, dv)

def deltanet_branch(q, k, v, z, a, beta_logit, conv_w, a_log, dt_bias, norm_w, w_o):
    b, t, _ = q.shape
    qkv = jax.nn.silu(causal_depthwise_conv(jnp.concatenate([q, k, v], axis=-1), conv_w))
    q, k, v = jnp.split(qkv, [DN_KEY_DIM, 2 * DN_KEY_DIM], axis=-1)
    q = l2_normalize(q.reshape(b, t, DN_HEADS, DN_HEAD_DIM))
    k = l2_normalize(k.reshape(b, t, DN_HEADS, DN_HEAD_DIM))
    v = v.reshape(b, t, DN_HEADS, DN_HEAD_DIM)
    beta = jax.nn.sigmoid(beta_logit.astype(jnp.float32))
    g = -jnp.exp(a_log.astype(jnp.float32)) * jax.nn.softplus(a.astype(jnp.float32) + dt_bias.astype(jnp.float32))
    o = gated_delta_rule(q, k, v, g, beta)
    o = rms_norm(o, norm_w) * jax.nn.silu(z.reshape(b, t, DN_HEADS, DN_HEAD_DIM).astype(jnp.float32))
    return o.reshape(b, t, DN_VAL_DIM).astype(z.dtype) @ w_o

def conv_branch(u, glu_b, dw_w, dw_b, ln_g, ln_b, w_pw2, b_pw2):
    u = u + glu_b
    h = u[..., :CV_CHANNELS] * jax.nn.sigmoid(u[..., CV_CHANNELS:])
    h = causal_depthwise_conv(h, dw_w) + dw_b
    h = jax.nn.silu(layer_norm(h, ln_g, ln_b))
    return h @ w_pw2 + b_pw2

def causal_block_attention(q_nope, q_rope, k_nope, k_rope, v):
    t = q_nope.shape[1]
    scale = (MLA_NOPE + MLA_ROPE) ** -0.5
    outs = []
    for i in range(t // ATTN_BLOCK):
        q0, q1 = i * ATTN_BLOCK, (i + 1) * ATTN_BLOCK
        s = (jnp.einsum('bqhd,bkhd->bhqk', q_nope[:, q0:q1], k_nope[:, :q1])
             + jnp.einsum('bqhr,bkr->bhqk', q_rope[:, q0:q1], k_rope[:, :q1])).astype(jnp.float32) * scale
        mask = jnp.arange(q1)[None, :] <= jnp.arange(q0, q1)[:, None]
        p = jax.nn.softmax(jnp.where(mask, s, -jnp.inf), axis=-1).astype(v.dtype)
        outs.append(jnp.einsum('bhqk,bkhv->bqhv', p, v[:, :q1]))
    return jnp.concatenate(outs, axis=1)

def mla_branch(c_q, c_kv, k_r, cos, sin, q_norm_w, w_uq, kv_norm_w, w_ukv, w_o):
    b, t, _ = c_q.shape
    q = (rms_norm(c_q, q_norm_w) @ w_uq).reshape(b, t, MLA_HEADS, MLA_NOPE + MLA_ROPE)
    q_nope = q[..., :MLA_NOPE]
    q_rope = apply_rope(q[..., MLA_NOPE:], cos[:, :, None, :], sin[:, :, None, :])
    kv = (rms_norm(c_kv, kv_norm_w) @ w_ukv).reshape(b, t, MLA_HEADS, MLA_NOPE + MLA_V)
    k_nope, v = kv[..., :MLA_NOPE], kv[..., MLA_NOPE:]
    k_rope = apply_rope(k_r, cos, sin)
    o = causal_block_attention(q_nope, q_rope, k_nope, k_rope, v)
    return o.reshape(b, t, MLA_HEADS * MLA_V) @ w_o

def hybrid_mixer(x, cos, sin, w_in, b_gate,
                 dn_conv_w, dn_a_log, dn_dt_bias, dn_norm_w, dn_w_o,
                 cv_glu_b, cv_dw_w, cv_dw_b, cv_ln_g, cv_ln_b, cv_w_pw2, cv_b_pw2,
                 mla_q_norm_w, mla_w_uq, mla_kv_norm_w, mla_w_ukv, mla_w_o, w_out):
    b, t, d = x.shape
    proj = x @ w_in
    (dq, dk, dv, dz, da, dbeta, glu, c_q, c_kv, k_r, gate_logits) = jnp.split(proj, _split_points(), axis=-1)
    y_dn = deltanet_branch(dq, dk, dv, dz, da, dbeta, dn_conv_w, dn_a_log, dn_dt_bias, dn_norm_w, dn_w_o)
    y_cv = conv_branch(glu, cv_glu_b, cv_dw_w, cv_dw_b, cv_ln_g, cv_ln_b, cv_w_pw2, cv_b_pw2)
    y_mla = mla_branch(c_q, c_kv, k_r, cos, sin, mla_q_norm_w, mla_w_uq, mla_kv_norm_w, mla_w_ukv, mla_w_o)
    gates = jax.nn.sigmoid((gate_logits + b_gate).astype(jnp.float32)).astype(x.dtype).reshape(b, t, N_BRANCHES, d)
    merged = gates[:, :, 0] * y_dn + gates[:, :, 1] * y_cv + gates[:, :, 2] * y_mla
    return merged @ w_out

def second_inputs(seed: int = 0) -> dict:
    key = jax.random.key(seed)
    ks = iter(jax.random.split(key, 48))
    L = DEPTH
    f32 = jnp.float32

    def w(shape, fan_in, scale=1.0):
        return jax.random.normal(next(ks), shape, f32) * (scale * fan_in ** -0.5)

    def gain(shape):
        return 1.0 + 0.02 * jax.random.normal(next(ks), shape, f32)

    def bias(shape):
        return 0.02 * jax.random.normal(next(ks), shape, f32)

    x = jax.random.normal(next(ks), (BATCH, SEQ, D_MODEL), f32)
    positions = (jax.random.randint(next(ks), (BATCH, 1), 0, 4096, dtype=jnp.int32)
                 + jnp.arange(SEQ, dtype=jnp.int32)[None, :])
    dt = jnp.exp(jax.random.uniform(next(ks), (L, DN_HEADS), f32, np.log(1e-3), np.log(1e-1)))
    return {
        'x': x,
        'positions': positions,
        'ln1_g': gain((L, D_MODEL)),
        'ln1_b': bias((L, D_MODEL)),
        'ffn1_w_gate': w((L, D_MODEL, D_FF), D_MODEL),
        'ffn1_w_up': w((L, D_MODEL, D_FF), D_MODEL),
        'ffn1_w_down': w((L, D_FF, D_MODEL), D_FF, DEEPNORM_BETA),
        'w_in': w((L, D_MODEL, D_IN), D_MODEL),
        'b_gate': bias((L, N_BRANCHES * D_MODEL)),
        'dn_conv_w': w((L, DN_CONV, 2 * DN_KEY_DIM + DN_VAL_DIM), DN_CONV),
        'dn_a_log': jnp.log(jax.random.uniform(next(ks), (L, DN_HEADS), f32, 1.0, 16.0)),
        'dn_dt_bias': dt + jnp.log(-jnp.expm1(-dt)),
        'dn_norm_w': gain((L, DN_HEAD_DIM)),
        'dn_w_o': w((L, DN_VAL_DIM, D_MODEL), DN_VAL_DIM, DEEPNORM_BETA),
        'cv_glu_b': bias((L, 2 * CV_CHANNELS)),
        'cv_dw_w': w((L, CV_KERNEL, CV_CHANNELS), CV_KERNEL),
        'cv_dw_b': bias((L, CV_CHANNELS)),
        'cv_ln_g': gain((L, CV_CHANNELS)),
        'cv_ln_b': bias((L, CV_CHANNELS)),
        'cv_w_pw2': w((L, CV_CHANNELS, D_MODEL), CV_CHANNELS, DEEPNORM_BETA),
        'cv_b_pw2': bias((L, D_MODEL)),
        'mla_q_norm_w': gain((L, MLA_Q_LORA)),
        'mla_w_uq': w((L, MLA_Q_LORA, MLA_HEADS * (MLA_NOPE + MLA_ROPE)), MLA_Q_LORA),
        'mla_kv_norm_w': gain((L, MLA_KV_LORA)),
        'mla_w_ukv': w((L, MLA_KV_LORA, MLA_HEADS * (MLA_NOPE + MLA_V)), MLA_KV_LORA),
        'mla_w_o': w((L, MLA_HEADS * MLA_V, D_MODEL), MLA_HEADS * MLA_V, DEEPNORM_BETA),
        'w_out': w((L, D_MODEL, D_MODEL), D_MODEL, DEEPNORM_BETA),
        'ln2_g': gain((L, D_MODEL)),
        'ln2_b': bias((L, D_MODEL)),
        'ffn2_w_gate': w((L, D_MODEL, D_FF), D_MODEL),
        'ffn2_w_up': w((L, D_MODEL, D_FF), D_MODEL),
        'ffn2_w_down': w((L, D_FF, D_MODEL), D_FF, DEEPNORM_BETA),
        'ln3_g': gain((L, D_MODEL)),
        'ln3_b': bias((L, D_MODEL)),
    }

def second_block(x, positions, ln1_g, ln1_b, ffn1_w_gate, ffn1_w_up, ffn1_w_down, w_in, b_gate,
              dn_conv_w, dn_a_log, dn_dt_bias, dn_norm_w, dn_w_o,
              cv_glu_b, cv_dw_w, cv_dw_b, cv_ln_g, cv_ln_b, cv_w_pw2, cv_b_pw2,
              mla_q_norm_w, mla_w_uq, mla_kv_norm_w, mla_w_ukv, mla_w_o,
              w_out, ln2_g, ln2_b, ffn2_w_gate, ffn2_w_up, ffn2_w_down, ln3_g, ln3_b):
    cos, sin = rope_tables(positions)
    h = x
    for l in range(DEPTH):
        h = layer_norm(DEEPNORM_ALPHA * h + 0.5 * swiglu_2(h, ffn1_w_gate[l], ffn1_w_up[l], ffn1_w_down[l]),
                       ln1_g[l], ln1_b[l])
        mix = hybrid_mixer(h, cos, sin, w_in[l], b_gate[l],
                           dn_conv_w[l], dn_a_log[l], dn_dt_bias[l], dn_norm_w[l], dn_w_o[l],
                           cv_glu_b[l], cv_dw_w[l], cv_dw_b[l], cv_ln_g[l], cv_ln_b[l], cv_w_pw2[l], cv_b_pw2[l],
                           mla_q_norm_w[l], mla_w_uq[l], mla_kv_norm_w[l], mla_w_ukv[l], mla_w_o[l], w_out[l])
        h = layer_norm(DEEPNORM_ALPHA * h + mix, ln2_g[l], ln2_b[l])
        h = layer_norm(DEEPNORM_ALPHA * h + 0.5 * swiglu_2(h, ffn2_w_gate[l], ffn2_w_up[l], ffn2_w_down[l]),
                       ln3_g[l], ln3_b[l])
    return h


def setup_inputs(seed=0):
    out = dict(first_inputs(seed))
    for name, value in second_inputs(seed + 1).items():
        if name != "x":
            out[name + "_2"] = value
    return out


def reference(
    x, c, norm_g, w_ada, b_ada, ffn_wg, ffn_wu, ffn_wd, w_in_ab, qk_norm_g, lambda_q1,
    lambda_k1, lambda_q2, lambda_k2, subln_g, pool_w, pool_scale, w_out_ab, w_in_c, conv_w,
    w_out_c, positions_2, ln1_g_2, ln1_b_2, ffn1_w_gate_2, ffn1_w_up_2, ffn1_w_down_2, w_in_2,
    b_gate_2, dn_conv_w_2, dn_a_log_2, dn_dt_bias_2, dn_norm_w_2, dn_w_o_2, cv_glu_b_2,
    cv_dw_w_2, cv_dw_b_2, cv_ln_g_2, cv_ln_b_2, cv_w_pw2_2, cv_b_pw2_2, mla_q_norm_w_2,
    mla_w_uq_2, mla_kv_norm_w_2, mla_w_ukv_2, mla_w_o_2, w_out_2, ln2_g_2, ln2_b_2,
    ffn2_w_gate_2, ffn2_w_up_2, ffn2_w_down_2, ln3_g_2, ln3_b_2,
):
    x = first_block(
        x, c, norm_g, w_ada, b_ada, ffn_wg, ffn_wu, ffn_wd, w_in_ab, qk_norm_g, lambda_q1,
        lambda_k1, lambda_q2, lambda_k2, subln_g, pool_w, pool_scale, w_out_ab, w_in_c, conv_w,
        w_out_c,
    )
    return second_block(
        x, positions_2, ln1_g_2, ln1_b_2, ffn1_w_gate_2, ffn1_w_up_2, ffn1_w_down_2, w_in_2,
        b_gate_2, dn_conv_w_2, dn_a_log_2, dn_dt_bias_2, dn_norm_w_2, dn_w_o_2, cv_glu_b_2,
        cv_dw_w_2, cv_dw_b_2, cv_ln_g_2, cv_ln_b_2, cv_w_pw2_2, cv_b_pw2_2, mla_q_norm_w_2,
        mla_w_uq_2, mla_kv_norm_w_2, mla_w_ukv_2, mla_w_o_2, w_out_2, ln2_g_2, ln2_b_2,
        ffn2_w_gate_2, ffn2_w_up_2, ffn2_w_down_2, ln3_g_2, ln3_b_2,
    )


_drawn_inputs = setup_inputs


def setup_inputs(seed=0):
    import zlib

    import numpy as np

    out = dict(_drawn_inputs(seed))
    spreads = {}
    factors = {'qk_norm_g': 3.956,
     'lambda_q1': 8.0,
     'lambda_q2': 2.885,
     'subln_g': 2.708,
     'b_gate_2': 8.0,
     'dn_a_log_2': 4.011,
     'dn_dt_bias_2': 3.927,
     'dn_norm_w_2': 8.0,
     'cv_glu_b_2': 8.0,
     'cv_dw_b_2': 8.0,
     'cv_ln_g_2': 8.0,
     'cv_ln_b_2': 8.0,
     'cv_b_pw2_2': 8.0,
     'mla_q_norm_w_2': 8.0,
     'mla_w_uq_2': 2.761,
     'mla_kv_norm_w_2': 8.0}
    for name, (base, spread) in spreads.items():
        noise = np.random.default_rng([zlib.crc32(name.encode()), seed]).standard_normal(out[name].shape)
        drawn = base * np.exp(spread * noise) if base else spread * noise
        out[name] = jnp.asarray(drawn.astype(out[name].dtype))
    for name, factor in factors.items():
        out[name] = (out[name] * factor).astype(out[name].dtype)
    return out
```

```python
import math
from contextlib import ExitStack

import concourse.bass as bass
from concourse import mybir

F32 = mybir.dt.float32
F32R = mybir.dt.float32r
BF16 = mybir.dt.bfloat16
I32 = mybir.dt.int32
ALU = mybir.AluOpType
ACT = mybir.ActivationFunctionType
AX = mybir.AxisListType.X
ds = bass.ds

P = 128
T = 256
TT = T // P
D = 1024
KT = D // P
DFF = 2816
PAIRS = DFF // 256
RING = 3
CH = 2048
HEADS = 4
QK_DIM = 64
A_EPS = 1e-6
B_EPS = 1e-5
LAM_INIT = 0.8 - 0.6 * math.exp(0.0)
WINDOWS = (2, 4, 8, 16)
ALPHA = (2 * 2) ** 0.25
NEG = -1e30

FFN_CH = 3 * PAIRS
A0_CH = 8 + 4
A1_CH = 12 + 4
C_AB, C_GLU, C_CQ, C_KR, C_GATE = 2048, 2056, 3080, 3720, 3784
B_LOW = 5
B_CH = 8 + 4 + B_LOW + 12 + 2 + 2 + 2 + 4
A_CHUNKS = 4 * FFN_CH + A0_CH + A1_CH
B_LAYER_CH = 2 * FFN_CH + B_CH
assert B_LAYER_CH % RING == 0
LAYER_TURNS = B_LAYER_CH // RING
ADA_SLOTS = 6
LEVELS = 7
TAPS = 31
MIX_MEM = 12288


def block_kernel(nc, a, out):
    keep = ExitStack()
    with keep:
        def sb(name, shape, dt=F32):
            return keep.enter_context(nc.sbuf_tensor(name, shape, dt))

        def sem(name):
            return keep.enter_context(nc.semaphore(name))

        raw = [sb(f"raw{i}", [P, CH]) for i in range(RING)]
        w_hi = [sb(f"w_hi{i}", [P, CH], F32R) for i in range(RING)]
        w_lo = [sb(f"w_lo{i}", [P, CH], F32R) for i in range(RING)]
        x = sb("x", [P, KT, T])
        x_hi = sb("x_hi", [P, KT, T], F32R)
        x_lo = sb("x_lo", [P, KT, T], F32R)
        y_hi = sb("y_hi", [P, KT, T], F32R)
        y_lo = sb("y_lo", [P, KT, T], F32R)
        work = sb("work", [P, KT, T])
        silu_g = sb("silu_g", [P, 2 * T])
        hid = sb("hid", [P, 2 * T])
        hid_hi = sb("hid_hi", [P, 2, T], F32R)
        hid_lo = sb("hid_lo", [P, 2, T], F32R)
        ident = sb("ident", [P, P])
        ones = sb("ones", [P, P])
        zeros = sb("zeros", [P, 512], BF16)
        diag = sb("diag", [P, 16, P])
        moment = sb("moment", [P, 32])
        rstd = sb("rstd", [P, 32])
        half_neg = sb("half_neg", [P, 32])
        cmask = sb("cmask", [P, T])
        small = sb("small", [P, 16])
        masked = sb("masked", [P, 2, 2, T])
        probs = sb("probs", [P, 2, 2, T])
        weights = sb("weights", [P, T])
        turned = sb("turned", [P, 2, P])
        sums = sb("sums", [P, 8, 2])
        negmax = sb("negmax", [P, 8, 2])
        recips = sb("recips", [P, 8, 2])
        out_sb = sb("out_sb", [P, HEADS, T])
        mix_mem = sb("mix_mem", [P, MIX_MEM])
        levels = sb("levels", [P, P])
        tri = sb("tri", [P, P])
        rot = sb("rot", [64, P])
        inv_freq = sb("inv_freq", [64, 3])
        cos_t = sb("cos_t", [64, T])
        sin_t = sb("sin_t", [64, T])
        cols1 = sb("cols1", [P, 106])
        cols2 = sb("cols2", [P, 48])
        cols3 = sb("cols3", [P, 124])
        head_par = sb("head_par", [P, 2, 4])
        ab = sb("ab", [P, TT, 8])
        gl = sb("gl", [P, 12, 8])
        gcol = sb("gcol", [P, 8])

        def shaped(ap, shape):
            names = " ".join(f"d{i}" for i in range(len(shape)))
            sizes = {f"d{i}": n for i, n in enumerate(shape[:-1])}
            return ap if len(shape) == 1 else ap.rearrange(f"p ({names}) -> p {names}", **sizes)

        def flat(t):
            names = " ".join(f"d{i}" for i in range(len(t.shape) - 1))
            return t[:].rearrange(f"p {names} -> p ({names})") if len(t.shape) > 2 else t[:]

        class Carve:

            def __init__(self, start=0):
                self.at = start

            def __call__(self, *shape, parts=P):
                n = math.prod(shape)
                assert self.at + n <= MIX_MEM
                self.at += n
                return shaped(mix_mem[0:parts, self.at - n:self.at], shape)

        carve = Carve()
        ada_raw = [flat(masked), flat(probs), flat(out_sb)] + [carve(D) for _ in range(3)]
        ada_acc = carve(6, D)
        inv_count = carve(4, T)
        pool_w = carve(4, P)
        vpad = carve(2, T + 2)
        a_rows = carve(P, parts=85)
        b_rows = carve(2, P, parts=72)
        a_cols = carve(85)
        b_cols = carve(2, 72)
        c_act = carve(KT)
        mod = carve(18, KT)
        norm_col = carve(6, KT)
        gate_col = carve(6, KT)
        half_sel = carve(2)
        qk_gain = carve(2)
        lam_in = carve(4, parts=QK_DIM)
        lam_prod = carve(2, parts=QK_DIM)
        lam = carve(4)
        sub_gain = carve(1)
        carve = Carve()
        qk = carve(8, T)
        v_tok = carve(TT, 512)
        u_in = carve(4, T)
        win = [carve(4, T) for _ in range(2)]
        count_i = carve(T).bitcast(I32)
        c_sb = carve(2, T)
        x_rows = shaped(flat(diag), (TT, D))
        bc_half = diag

        carve = Carve()
        bmat = carve(8, P)
        qkv = carve(12, T)
        emat = carve(8, P)
        tmat = carve(8, P)
        amat = carve(8, P)
        qk_dec = carve(8, P)
        q_dec = carve(HEADS, P)
        low = carve(5, T)
        k_rope = carve(T, parts=64)
        gate = carve(KT, T)
        stage, sig, ptmp = silu_g, shaped(hid[:], (2, T)), shaped(silu_g[:], (2, T))
        z_act, glu = shaped(flat(masked), (4, T)), shaped(flat(probs), (4, T))
        conv = shaped(flat(diag)[:, 8 * P:16 * P], (4, T))
        carve = Carve(8 * P)
        dmat = carve(8, P)
        k_tok = carve(2, 512)
        v_beta = carve(2, 512)
        merged = shaped(mix_mem[:, 0:KT * T], (KT, T))
        u_sb = amat
        wt, s_state = tmat[:, 0:HEADS, :], tmat[:, HEADS:8, :]
        carve = Carve(16 * P)
        uq = carve(3, 768)
        ukv = carve(2, 1024)
        k_nope = carve(HEADS, T)
        v_mla = carve(TT, 512)
        q_nope = work[:, 4:8, :]
        q_rope = shaped(flat(out_sb)[0:64, :], (HEADS, T))
        rot_q = shaped(flat(masked)[0:64, :], (HEADS, T))
        rot_k = weights[0:64, :]
        par = flat(out_sb)
        w_kr = shaped(par[:, 0:512], (KT, 64))
        w_ab = shaped(par[:, 512:576], (KT, 8))
        rows1, rows2, rows3 = par[0:106, 576:704], par[0:48, 704:832], par[0:124, 832:960]
        y_rows = shaped(flat(mix_mem)[:, 12288 - 2048:12288], (TT, D))
        level_tmp = mix_mem[:, 0:P]
        rope_k = mix_mem[0:64, P:P + T].bitcast(I32)
        count_b = mix_mem[0:64, 3 * P:3 * P + 1].bitcast(I32)
        pos_i = hid[0:64, 0:T].bitcast(I32)

        ps = keep.enter_context(nc.psum_tensor("ps", [P, 8, 512], F32))

        landed = [sem(f"landed{i}") for i in range(RING)]
        hi_ready = sem("hi_ready")
        lo_ready = sem("lo_ready")
        chunk_used = sem("chunk_used")
        ada_landed = [sem(f"ada_landed{i}") for i in range(ADA_SLOTS)]
        ada_used = sem("ada_used")
        mod_summed = sem("mod_summed")
        mod_ready = sem("mod_ready")
        params_in = sem("params_in")
        params2_in = sem("params2_in")
        lam_exp = sem("lam_exp")
        cv_scaled = sem("cv_scaled")
        x_in = sem("x_in")
        const_ready = sem("const_ready")
        const_dve = sem("const_dve")
        rows_turned = sem("rows_turned")
        cols_ready = sem("cols_ready")
        c_ready = sem("c_ready")
        x_turned = sem("x_turned")
        x_new = sem("x_new")
        squares = sem("squares")
        stats = sem("stats")
        moments = sem("moments")
        rstd_ready = sem("rstd_ready")
        diag_ready = sem("diag_ready")
        rows_ready = sem("rows_ready")
        scaled = sem("scaled")
        x_hi_ready = sem("x_hi_ready")
        x_lo_ready = sem("x_lo_ready")
        gate_read = sem("gate_read")
        hid_made = sem("hid_made")
        hid_hi_ready = sem("hid_hi_ready")
        hid_lo_ready = sem("hid_lo_ready")
        evac = sem("evac")
        y_made = sem("y_made")
        y_hi_ready = sem("y_hi_ready")
        y_lo_ready = sem("y_lo_ready")
        at_scores = sem("at_scores")
        at_masked = sem("at_masked")
        at_max = sem("at_max")
        at_probs = sem("at_probs")
        at_weights = sem("at_weights")
        at_turned = sem("at_turned")
        at_copied = sem("at_copied")
        at_out = sem("at_out")
        hd_sq = sem("hd_sq")
        hd_stats = sem("hd_stats")
        hd_moment = sem("hd_moment")
        hd_rstd = sem("hd_rstd")
        hd_diag = sem("hd_diag")
        hd_rows = sem("hd_rows")
        hd_scaled = sem("hd_scaled")
        pooled = sem("pooled")
        pool_mm = sem("pool_mm")
        lam_done = sem("lam_done")
        lam_mm = sem("lam_mm")
        c_copied = sem("c_copied")
        cx_read = sem("cx_read")
        lay_rows = sem("lay_rows")
        lay_small = sem("lay_small")
        lay_turned = sem("lay_turned")
        lay_cols = sem("lay_cols")
        ab_mm = sem("ab_mm")
        ab_copied = sem("ab_copied")
        ab_in = sem("ab_in")
        ab_exp = sem("ab_exp")
        g_ready = sem("g_ready")
        conv_raw = sem("conv_raw")
        conv_done = sem("conv_done")
        qkv_act = sem("qkv_act")
        glu_parts = sem("glu_parts")
        glu_ready = sem("glu_ready")
        qk_hat = sem("qk_hat")
        g_mm = sem("g_mm")
        g_cols = sem("g_cols")
        dec_in = sem("dec_in")
        dec_exp = sem("dec_exp")
        kk_mm = sem("kk_mm")
        tok_mm = sem("tok_mm")
        tok_done = sem("tok_done")
        a_ready = sem("a_ready")
        b_ready = sem("b_ready")
        t_mm = sem("t_mm")
        t_copied = sem("t_copied")
        inv_mm = sem("inv_mm")
        inv_ready = sem("inv_ready")
        u_mm = sem("u_mm")
        u_copied = sem("u_copied")
        s_mm = sem("s_mm")
        s_ready = sem("s_ready")
        ws_mm = sem("ws_mm")
        v_new = sem("v_new")
        o_mm = sem("o_mm")
        branch_free = sem("branch_free")
        cv_pool = sem("cv_pool")
        cv_dve = sem("cv_dve")
        kr_mm = sem("kr_mm")
        mla_w = sem("mla_w")
        mla_mm = sem("mla_mm")
        mla_sb = sem("mla_sb")
        rot_mm = sem("rot_mm")
        rope_done = sem("rope_done")
        rope_in = sem("rope_in")
        rope_sin = sem("rope_sin")
        rope_pow = sem("rope_pow")
        rope_conv = sem("rope_conv")
        merged_ready = sem("merged_ready")
        out_turned = sem("out_turned")
        out_copied = sem("out_copied")
        stored = sem("stored")

        A_FFN = (0, FFN_CH + A0_CH, 2 * FFN_CH + A0_CH, 3 * FFN_CH + A0_CH + A1_CH)
        A_MIX = (FFN_CH, 3 * FFN_CH + A0_CH)
        B0 = A_CHUNKS
        B_FFN = (B0, B0 + FFN_CH + B_CH)
        B_MIX = B0 + FFN_CH

        def chunk_cols(n):
            return 1024 if B_MIX + 12 <= n < B_MIX + 12 + B_LOW else CH

        class Place:

            def __init__(self):
                self.n = 0
                self.turns = 0

            def count(self, back=0):
                return 3 * self.turns + (self.n - back)

            def slot(self):
                return self.n % RING

            def turn(self):
                return self.turns + self.n // RING

        def x_out(t):
            return y_rows[:, t, :]

        def bc(ap, shape):
            return ap.broadcast_to(list(shape))

        def acc(m, n=1):
            return ps[:, 4 + m // 2, T * (m % 2):T * (m % 2 + n)]

        def group_of(f):
            return f + 1 if f < 3 else None

        GROUPS = ((0, 0, 3, 0, 0), (0, 3, 6, 24, 4), (1, 0, 6, 72, 12), (1, 6, 3, 120, 20))

        def call_x(l, j):
            return 7 + 3 * l + j

        def call_n(l, j):
            return 6 + 3 * l + j

        def call_h(l, j):
            return 2 + 4 * l + j

        def sq_at(l, j):
            return 3 * l + (2 + j)

        def pos(g):
            return g if g < 17 else g + 2 * ((g - 17) // 4)

        def call_y(l, j):
            return 8 + 10 * l + j

        def call_e(l, j):
            return 8 + 29 * l + j

        LN_G, LN_B = (0, 16, 32), (8, 24, 40)
        CB_GATE, CB_GLU, CB_DW, CB_LNG, CB_LNB, CB_PW2, CB_QN, CB_KVN, CB_DN = 48, 72, 80, 84, 88, 92, 100, 103, 105

        block = keep.enter_context(nc.Block())

        @block.sync
        def _(sp):
            at = Place()

            def load(src, kt, wait=True):
                if wait and at.n >= RING:
                    sp.wait_ge(lo_ready, at.count(RING - 1))
                s = at.slot()
                n = src.shape[-1]
                dst = raw[s][:, 0:kt * n].rearrange("p (k n) -> p k n", k=kt)
                sp.dma_start(dst, src).then_inc(landed[s], 16)
                at.n += 1

            def cols_of(w, start, n=256):
                return w.rearrange("(k p) n -> p k n", p=P)[:, :, start:start + n] if isinstance(start, int) \
                    else w.rearrange("(k p) n -> p k n", p=P)[:, :, ds(start, n)]

            def rows_of(w, i):
                return w.rearrange("(f k p) n -> p f k n", p=P, k=2)[:, i, :, :] if isinstance(i, int) \
                    else w.rearrange("(f k p) n -> p (f k) n", p=P, k=2)[:, ds(i * 2, 2), :]

            def ffn(wg, wu, wd):
                load(cols_of(wg, 0), KT)
                load(cols_of(wu, 0), KT)

                def pair(i):
                    load(cols_of(wg, i * 256 + 256), KT)
                    load(cols_of(wu, i * 256 + 256), KT)
                    load(rows_of(wd, i), 2)

                base = at.turns
                pair(0)
                with sp.Fori(1, PAIRS - 1) as i:
                    at.turns = base + i - 1
                    pair(i)
                    at.n -= 3
                at.turns = base
                at.n += 3 * (PAIRS - 2)
                load(rows_of(wd, PAIRS - 1), 2)

            def mix_a0():
                for j in range(8):
                    load(cols_of(a["w_in_ab"][0], 256 * j), KT)
                for j in range(4):
                    load(cols_of(a["w_out_ab"][0], 256 * j), KT)

            def mix_a1():
                w = a["w_in_c"][0]
                for part in (1, 2, 0):
                    load(cols_of(w, part * D), KT)
                base = at.turns
                with sp.Fori(0, 3) as j:
                    at.turns = base + j
                    for part in (1, 2, 0):
                        load(cols_of(w, j * 256 + (part * D + 256)), KT)
                    at.n -= 3
                at.turns = base
                at.n += 9
                for j in range(4):
                    load(cols_of(a["w_out_c"][0], 256 * j), KT)

            def lay(name, l):
                w = a[name]
                return w[ds(l, 1)].rearrange("o k n -> (o k) n")

            ffn_a = lambda l, i: ffn(a["ffn_wg"][l, i], a["ffn_wu"][l, i], a["ffn_wd"][l, i])
            ffn_a(0, 0)
            mix_a0()
            ffn_a(0, 1)
            ffn_a(1, 0)
            mix_a1()
            ffn_a(1, 1)
            assert at.n == A_CHUNKS
            with sp.Fori(0, 2) as l:
                at.turns = l * LAYER_TURNS
                at.n = B0
                ffn(lay("ffn1_w_gate_2", l), lay("ffn1_w_up_2", l), lay("ffn1_w_down_2", l))
                w_in = lay("w_in_2", l)
                for j in range(8):
                    load(cols_of(w_in, 256 * j), KT)
                for j in range(2):
                    load(cols_of(w_in, C_GLU + 256 * j), KT)
                    load(cols_of(w_in, C_GLU + 512 + 256 * j), KT)
                for j in range(B_LOW):
                    load(cols_of(w_in, C_CQ + 128 * j, 128), KT)
                for b, name in enumerate(("dn_w_o_2", "cv_w_pw2_2", "mla_w_o_2")):
                    for j in range(4):
                        load(cols_of(w_in, C_GATE + D * b + 256 * j), KT)
                    for j in range(2):
                        load(cols_of(lay(name, l), 512 * j, 512), 4)
                for j in range(4):
                    load(cols_of(lay("w_out_2", l), 256 * j), KT)
                ffn(lay("ffn2_w_gate_2", l), lay("ffn2_w_up_2", l), lay("ffn2_w_down_2", l))
                assert at.n == B0 + B_LAYER_CH
            sp.wait_ge(out_copied, 4)
            for t in range(TT):
                sp.dma_start(out[0, t * P:(t + 1) * P, :], x_out(t)).then_inc(stored, 16)
            sp.wait_ge(stored, 16 * TT)

        @block.gpsimd
        def _(pool):
            g = nc.gpsimd

            def select(view, op, fill, base, pattern, mult):
                g.affine_select(out=view, in_=view, compare_op=op, fill=fill, base=base,
                                pattern=pattern, channel_multiplier=mult)

            def ada_unit(grp, k, j, slot):
                l, m0 = GROUPS[grp][0], GROUPS[grp][1]
                w = a["w_ada"][l].rearrange("(k p) n -> p k n", p=P)
                src = w[:, k:k + 1, D * (m0 + j):D * (m0 + j + 1)] if isinstance(k, int) \
                    else w[:, ds(k, 1), D * (m0 + j):D * (m0 + j + 1)]
                pool.dma_start(ada_raw[slot][:].rearrange("p (o n) -> p o n", o=1), src)\
                    .then_inc(ada_landed[slot], 16)

            for t in range(TT):
                pool.dma_start(x_rows[:, t, :], a["x"][0, t * P:(t + 1) * P, :]).then_inc(x_in, 16)
            rows = [(0, 48, a["norm_g"].rearrange("l j (t p) -> (l j t) p", p=P)),
                    (48, 49, a["subln_g"]),
                    (49, 53, a["pool_scale"].rearrange("o (t p) -> (o t) p", p=P)),
                    (53, 77, a["conv_w"].rearrange("o j (t p) -> (o j t) p", p=P)),
                    (77, 85, a["c"].rearrange("o (t p) -> (o t) p", p=P))]
            for lo_, hi_, src in rows:
                pool.dma_start(a_rows[lo_:hi_, :], src).then_inc(params_in, 16)
            pool.dma_start(b_rows[:, :, :], a["b_ada"].rearrange("l (r p) -> r l p", p=P)).then_inc(params_in, 16)
            g.memset(ident[:], 0.0)
            g.memset(cmask[:], 0.0)
            g.memset(half_neg[:], -0.5)
            g.memset(half_sel[:], 1.0)
            g.iota(count_i[:], pattern=[[1, T]], base=1, channel_multiplier=0)
            pool.drain()
            select(ident[:], ALU.not_equal, 1.0, 0, [[-1, P]], 1)
            select(cmask[:], ALU.is_ge, NEG, P, [[-1, T]], 1)
            select(half_sel[:, 0:1], ALU.is_ge, 0.0, QK_DIM - 1, [[0, 1]], -1)
            select(half_sel[:, 1:2], ALU.is_ge, 0.0, -QK_DIM, [[0, 1]], 1)
            pool.drain().then_inc(const_ready, 1)
            for k in range(KT):
                for j in range(3):
                    u = 3 * k + j
                    if u >= ADA_SLOTS:
                        pool.wait_ge(ada_used, u - ADA_SLOTS + 1)
                    ada_unit(0, k, j, u % ADA_SLOTS)
            for half in range(2):
                for j in range(2):
                    pool.dma_start(qk_gain[64 * half:64 * half + 64, j:j + 1],
                                   a["qk_norm_g"][0, j, :].rearrange("(p o) -> p o", o=1)).then_inc(params2_in, 16)
            for j, name in enumerate(("lambda_q1", "lambda_k1", "lambda_q2", "lambda_k2")):
                pool.dma_start(lam_in[:, j:j + 1], a[name].rearrange("o p -> p o")).then_inc(params2_in, 16)
            pool.dma_start(pool_w[:, :, :], a["pool_w"].rearrange("o g c d -> c (o g) d")).then_inc(params2_in, 16)

            def power(call, n, ready=moments, done=rstd_ready):
                pool.wait_ge(ready, call + 1)
                g.tensor_tensor(rstd[:, 0:n], moment[:, 0:n], half_neg[:, 0:n], ALU.pow).then_inc(done, 1)

            def head_power(call, n):
                power(call, n, hd_moment, hd_rstd)

            def ada_group(f):
                grp = group_of(f)
                if grp is None:
                    return
                width = GROUPS[grp][2]
                unit0 = GROUPS[grp][3]
                if width == 6:
                    with pool.Fori(0, KT) as k:
                        for j in range(6):
                            pool.wait_ge(ada_used, k * 6 + (unit0 + j - ADA_SLOTS + 1))
                            ada_unit(grp, k, j, j)
                else:
                    pool.wait_ge(ada_used, unit0)
                    for j in range(3):
                        ada_unit(grp, 0, j, j)
                    with pool.Fori(1, KT) as k:
                        for j in range(3):
                            pool.wait_ge(ada_used, k * 3 + (unit0 + j - 2))
                            ada_unit(grp, k, j, j)

            def windows():
                pool.wait_ge(evac, 8)
                for n, width in enumerate(WINDOWS):
                    half = width // 2
                    src = u_in if n == 0 else win[(n + 1) % 2]
                    dst = win[n % 2]
                    g.tensor_tensor(dst[:, n:4, half:T], src[:, n:4, half:T], src[:, n:4, 0:T - half], ALU.add)
                    g.tensor_copy(dst[:, n:4, 0:half], src[:, n:4, 0:half])
                    pool.drain()
                    g.tensor_tensor(inv_count[:, n, :], dst[:, n, :], inv_count[:, n, :], ALU.mult)
                pool.drain()
                last = g.tensor_tensor(inv_count[:], inv_count[:], u_in[:], ALU.subtract)
                last.then_inc(pooled, 1)

            power(0, 2)
            ada_group(0)
            power(1, 2)
            head_power(0, 32)
            windows()
            head_power(1, 8)
            power(2, 2)
            ada_group(1)
            power(3, 2)
            ada_group(2)
            power(4, 2)
            power(5, 2)

            pool.wait_ge(x_lo_ready, 56)
            g.memset(levels[:], 0.0)
            g.memset(tri[:], 1.0)
            g.memset(rot[:], 0.0)
            pool.drain()
            select(tri[:], ALU.is_ge, 0.0, 0, [[1, P]], -1)
            select(rot[:, 0:64], ALU.not_equal, -1.0, -32, [[-1, 64]], 1)
            pool.drain()
            select(rot[:, 0:64], ALU.not_equal, 1.0, 32, [[-1, 64]], 1)
            for s in range(LEVELS):
                w = 2 ** s
                v = level_tmp.rearrange("p (b h w) -> p b h w", h=2, w=w)
                g.memset(v[:, :, 0, :], 0.0)
                g.memset(v[:, :, 1, :], s + 1.0)
                pool.drain()
                n = P // (2 * w)
                upper = v[:, :, 1, :]
                select(upper, ALU.is_ge, 0.0, 0, [[-2 * w, n], [0, w]], 1)
                pool.drain()
                select(upper, ALU.is_ge, 0.0, w - 1, [[2 * w, n], [0, w]], -1)
                pool.drain()
                g.tensor_tensor(levels[:], levels[:], level_tmp, ALU.add)
                pool.drain()
            for half in range(2):
                pool.drain()
                g.iota(count_b[32 * half:32 * half + 32, :], pattern=[[0, 1]], base=0, channel_multiplier=1)
            pool.drain()
            g.memset(inv_freq[:, 0:1], 10000.0)
            pool.drain()
            g.tensor_copy(inv_freq[:, 1:2], count_b[:])
            pool.drain()
            g.tensor_scalar(inv_freq[:, 1:2], inv_freq[:, 1:2], -1.0 / 32, None, ALU.mult)
            pool.drain()
            g.tensor_tensor(inv_freq[:, 2:3], inv_freq[:, 0:1], inv_freq[:, 1:2], ALU.pow)
            pool.dma_start(pos_i, bc(a["positions_2"], (64, T))).then_inc(rope_in, 16)
            pool.drain().then_inc(rope_pow, 1)

            def vec(name, l):
                w = a[name]
                return w[ds(l, 1), :].rearrange("o (r p) -> (o r) p", p=P)

            with pool.Fori(0, 2) as l:
                pool.wait_ge(x_lo_ready, l * 24 + 56)
                for name, r0, n in (("ln1_g_2", 0, 8), ("ln1_b_2", 8, 8), ("ln2_g_2", 16, 8), ("ln2_b_2", 24, 8),
                                    ("ln3_g_2", 32, 8), ("ln3_b_2", 40, 8), ("b_gate_2", CB_GATE, 24),
                                    ("cv_glu_b_2", CB_GLU, 8), ("cv_dw_b_2", CB_DW, 4), ("cv_ln_g_2", CB_LNG, 4),
                                    ("cv_ln_b_2", CB_LNB, 4), ("cv_b_pw2_2", CB_PW2, 8), ("mla_q_norm_w_2", CB_QN, 3),
                                    ("mla_kv_norm_w_2", CB_KVN, 2), ("dn_norm_w_2", CB_DN, 1)):
                    pool.dma_start(rows1[r0:r0 + n, :], vec(name, l)).then_inc(lay_rows, 16)
                pool.dma_start(rows2[:, :], a["dn_conv_w_2"][ds(l, 1)].rearrange("o j (t p) -> (o j t) p", p=P))\
                    .then_inc(lay_rows, 16)
                pool.dma_start(rows3[:, :], a["cv_dw_w_2"][ds(l, 1)].rearrange("o j (t p) -> (o j t) p", p=P))\
                    .then_inc(lay_rows, 16)
                w_in = a["w_in_2"][ds(l, 1)].rearrange("o (k p) n -> p (o k) n", p=P)
                pool.dma_start(w_ab[:, :, :], w_in[:, :, C_AB:C_AB + 8]).then_inc(lay_small, 16)
                pool.dma_start(w_kr[:, :, :], w_in[:, :, C_KR:C_KR + 64]).then_inc(lay_small, 16)
                pool.dma_start(head_par[:, 0, :], bc(a["dn_a_log_2"][ds(l, 1), :], (P, 4))).then_inc(lay_small, 16)
                pool.dma_start(head_par[:, 1, :], bc(a["dn_dt_bias_2"][ds(l, 1), :], (P, 4))).then_inc(lay_small, 16)
                power(call_n(l, 0), 2)
                head_power(call_h(l, 0), 16)
                head_power(call_h(l, 1), 8)
                for j in range(TAPS - 1, -1, -1):
                    sh = TAPS - 1 - j
                    for t in (2, 3):
                        wcol = cols3[:, 4 * j + t:4 * j + t + 1]
                        if sh == 0:
                            g.tensor_scalar(conv[:, t, :], glu[:, t, :], wcol,
                                            cols1[:, CB_DW + t:CB_DW + t + 1], ALU.mult, ALU.add)
                        else:
                            g.tensor_scalar(ptmp[:, t - 2, 0:T - sh], glu[:, t, 0:T - sh], wcol, None, ALU.mult)
                    pool.drain()
                    if sh:
                        for t in (2, 3):
                            g.tensor_tensor(conv[:, t, sh:T], conv[:, t, sh:T], ptmp[:, t - 2, 0:T - sh], ALU.add)
                        pool.drain()
                pool.drain().then_inc(cv_pool, 1)
                pool.wait_ge(branch_free, l * 2 + 1)
                pool.dma_start(uq[:, :, :], a["mla_w_uq_2"][ds(l, 1)].rearrange("o (k p) n -> p (o k) n", p=P))\
                    .then_inc(mla_w, 16)
                pool.dma_start(ukv[:, :, :], a["mla_w_ukv_2"][ds(l, 1)].rearrange("o (k p) n -> p (o k) n", p=P))\
                    .then_inc(mla_w, 16)
                head_power(call_h(l, 2), 2)
                head_power(call_h(l, 3), 4)
                power(call_n(l, 1), 2)
                power(call_n(l, 2), 2)

        @block.tensor
        def _(pe):
            at = Place()

            def take():
                pe.wait_ge(lo_ready, at.count() + 1)
                return at.slot()

            def used(last):
                last.then_inc(chunk_used, 1)
                at.n += 1

            def split_mm(dst, wh, wl, vh, vl, start, stop_):
                pe.matmul(dst, wh, vh, start=start, stop=False, skip_group_check=True)
                pe.matmul(dst, wh, vl, start=False, stop=False, skip_group_check=True)
                return pe.matmul(dst, wl, vh, start=False, stop=stop_, skip_group_check=True)

            def cols_chunk(bank, vh, vl, kt=KT, n=256, waits=None, order=None, first=0):
                s = take()
                h = w_hi[s][:, 0:kt * n].rearrange("p (k n) -> p k n", k=kt)
                lw = w_lo[s][:, 0:kt * n].rearrange("p (k n) -> p k n", k=kt)
                order = order or list(range(kt))
                for m in range(n // P):
                    dst = ps[:, bank + m // 2, T * (m % 2):T * (m % 2) + T]
                    for i, k in enumerate(order):
                        if m == 0 and waits is not None:
                            waits(i)
                        last = split_mm(dst, h[:, k, m * P:m * P + P], lw[:, k, m * P:m * P + P],
                                        vh[:, first + k, :], vl[:, first + k, :], i == 0, i == kt - 1)
                used(last)

            def x_waits(call):
                return lambda k: pe.wait_ge(x_lo_ready, call * 8 + (k + 1))

            def down_chunk(call, i):
                s = take()
                pe.wait_ge(hid_lo_ready, call * PAIRS + i + 1)
                h = w_hi[s][:].rearrange("p (k n) -> p k n", k=2)
                lw = w_lo[s][:].rearrange("p (k n) -> p k n", k=2)
                for m in range(KT):
                    for k in range(2):
                        last = split_mm(acc(m), h[:, k, m * P:m * P + P], lw[:, k, m * P:m * P + P],
                                        hid_hi[:, k, :], hid_lo[:, k, :], False, False)
                used(last)

            def ffn(f, call, before_last=None):
                x_waits(call)(0)
                for b in range(4, 8):
                    pe.matmul(ps[:, b, :], zeros[:, 0:P], zeros[:], start=True, stop=True, skip_group_check=True)
                cols_chunk(0, x_hi, x_lo, waits=x_waits(call))
                cols_chunk(1, x_hi, x_lo)
                base = at.turns
                with pe.Fori(0, PAIRS - 1) as i:
                    at.turns = base + i
                    pe.wait_ge(gate_read, f * PAIRS + i + 1)
                    cols_chunk(0, x_hi, x_lo)
                    pe.wait_ge(hid_made, f * PAIRS + i + 1)
                    cols_chunk(1, x_hi, x_lo)
                    down_chunk(f, i)
                    at.n -= 3
                at.turns = base
                at.n += 3 * (PAIRS - 1)
                pe.wait_ge(hid_made, f * PAIRS + PAIRS)
                if before_last:
                    before_last()
                down_chunk(f, PAIRS - 1)

            def mod_sums(grp):
                width, unit0 = GROUPS[grp][2], GROUPS[grp][3]
                pe.wait_ge(ada_used, unit0 + 8 * width)
                for j in range(width):
                    for t in range(KT):
                        last = pe.matmul(ps[:, 1, j * KT + t:j * KT + t + 1], ada_acc[:, j, t * P:t * P + P],
                                         ones[:, 0:1], start=True, stop=True)
                last.then_inc(mod_summed, 1)

            def norm(n, call, with_mean):
                for m in range(KT):
                    pe.wait_ge(squares, n * 8 + (m + 1))
                    for t in range(TT):
                        last = pe.matmul(ps[:, 2, t:t + 1], work[:, m, t * P:t * P + P], ones[:, 0:1],
                                         start=(m == 0 and t == 0), stop=(m == KT - 1), skip_group_check=True)
                        if with_mean:
                            last = pe.matmul(ps[:, 2, 2 + t:3 + t], x[:, m, t * P:t * P + P], ones[:, 0:1],
                                             start=False, stop=(m == KT - 1), skip_group_check=True)
                last.then_inc(stats, 1)
                pe.wait_ge(diag_ready, n + 1)
                w = (2 if with_mean else 1) * TT
                pe.matmul(ps[:, 3, 0:w * P], ones[:], diag[:, 0:w, :], start=True, stop=True).then_inc(rows_ready, 1)

            def head_sums(tiles, src, bank, ready, value):
                pe.wait_ge(ready, value)
                for i in range(tiles):
                    for t in range(TT):
                        c = i * TT + t
                        last = pe.matmul(ps[:, bank, c:c + 1], src[:, i, t * P:t * P + P], ones[:, 0:1],
                                         start=True, stop=True)
                last.then_inc(hd_stats, 1)

            def head_rows(call, n, bank):
                pe.wait_ge(hd_diag, call + 1)
                for i in range(0, n, 4):
                    w = min(4, n - i)
                    last = pe.matmul(ps[:, bank + i // 4, 0:w * P], ones[:], diag[:, i:i + w, :], start=True, stop=True)
                last.then_inc(hd_rows, 1)

            def attention(item0, score, v_tiles):
                def scores(it):
                    if it >= 2:
                        pe.wait_ge(at_masked, item0 + (it - 1))
                    score(it % HEADS, it // HEADS, 4 + 2 * (it % 2)).then_inc(at_scores, 1)

                def turn(it):
                    pe.wait_ge(at_weights, item0 + (it + 1))
                    for kt in range(it // HEADS + 1):
                        last = pe.transpose(ps[:, 2 + it % 2, kt * P:kt * P + P], weights[:, kt * P:kt * P + P], ident[:])
                    last.then_inc(at_turned, 1)

                def values(it):
                    h, b = it % HEADS, it // HEADS
                    pe.wait_ge(at_copied, item0 + (it + 1))
                    dst = ps[:, h // 2, T * (h % 2) + P * b:T * (h % 2) + P * b + P]
                    for kt in range(b + 1):
                        last = pe.matmul(dst, v_tiles[:, kt, h * P:h * P + P], turned[:, kt, :],
                                         start=(kt == 0), stop=(kt == b))
                    last.then_inc(at_out, 1)

                scores(0)
                scores(1)
                for it in range(8):
                    turn(it)
                    if it + 2 < 8:
                        scores(it + 2)
                    values(it)

            pe.wait_ge(const_ready, 1)
            pe.wait_ge(const_dve, 1)
            pe.wait_ge(params_in, 6 * 16)
            pe.transpose(ps[:, 0, 0:85], a_rows[:], ident[0:85, 0:85])
            pe.transpose(ps[:, 0, 128:200], b_rows[:, 0, :], ident[0:72, 0:72])
            pe.transpose(ps[:, 0, 256:328], b_rows[:, 1, :], ident[0:72, 0:72]).then_inc(rows_turned, 1)
            pe.wait_ge(x_in, 16 * TT)
            for m in range(KT):
                for t in range(TT):
                    last = pe.transpose(acc(m)[:, t * P:t * P + P], x_rows[:, t, m * P:m * P + P], ident[:])
                last.then_inc(x_turned, 1)
            mod_sums(0)
            norm(0, 0, False)
            ffn(0, 0, lambda: mod_sums(1))
            norm(1, 1, False)

            def mix_a0():
                for j in range(8):
                    bank = j % 3
                    if j >= 3:
                        pe.wait_ge(evac, j - 2)
                    if j in (4, 5):
                        s = take()
                        h = w_hi[s][:].rearrange("p (k n) -> p k n", k=KT)
                        lw = w_lo[s][:].rearrange("p (k n) -> p k n", k=KT)
                        for t in range(TT):
                            dst = ps[:, bank, T * t:T * t + T]
                            for k in range(KT):
                                xs = slice(t * P, t * P + P)
                                last = split_mm(dst, x_hi[:, k, xs], x_lo[:, k, xs], h[:, k, :], lw[:, k, :],
                                                k == 0, k == KT - 1)
                        used(last)
                    else:
                        cols_chunk(bank, x_hi, x_lo, waits=x_waits(1) if j == 0 else None)
                    if j == 5:
                        pe.wait_ge(evac, 4)
                        for i in range(8):
                            for t in range(TT):
                                c = (i * TT + t) * 2
                                last = pe.matmul(ps[:, 4, c:c + 2], work[:, i, t * P:t * P + P], half_sel[:],
                                                 start=True, stop=True)
                        last.then_inc(hd_stats, 1)
                pe.wait_ge(hd_diag, 1)
                for i in range(16):
                    last = pe.matmul(ps[:, 4 + i // 4, (i % 4) * P:(i % 4) * P + P], bc_half[:, i, :], ident[:],
                                     start=True, stop=True)
                last.then_inc(hd_rows, 1)
                pe.wait_ge(hd_scaled, 1)
                pe.wait_ge(evac, 8)

                def score(h, b, bank):
                    for j in range(2):
                        part = slice(64 * j, 64 * j + 64)
                        last = pe.matmul(ps[:, bank + j, 0:P * (b + 1)], qk[part, h, P * b:P * b + P],
                                         qk[part, 4 + h, 0:P * (b + 1)], start=True, stop=True)
                    return last

                attention(0, score, v_tok)
                pe.wait_ge(pooled, 1)
                for i in range(4):
                    last = pe.matmul(ps[:, 2 + i // 2, T * (i % 2):T * (i % 2) + T], pool_w[:, i, :], inv_count[:, i, :],
                                     start=True, stop=True)
                last.then_inc(pool_mm, 1)
                head_sums(4, work, 4, hd_sq, 1)
                head_rows(1, 8, 6)
                order = [4, 5, 6, 7, 0, 1, 2, 3]
                for j in range(4):
                    cols_chunk(4 + j, y_hi, y_lo, order=order,
                               waits=(lambda i: pe.wait_ge(y_lo_ready, i // 2 + 1)) if j == 0 else None)

            def mix_a1():
                def turn(j, first):
                    if not first:
                        pe.wait_ge(c_copied, j)
                    cols_chunk(0, x_hi, x_lo, waits=x_waits(4) if first else None)
                    if not first:
                        pe.wait_ge(cx_read, j)
                    cols_chunk(1, x_hi, x_lo)
                    if not first:
                        pe.wait_ge(y_made, j + 2)
                    cols_chunk(2, x_hi, x_lo)

                turn(0, True)
                base = at.turns
                with pe.Fori(1, 4) as j:
                    at.turns = base + j - 1
                    turn(j, False)
                    at.n -= 3
                at.turns = base
                at.n += 9
                for j in range(4):
                    cols_chunk(4 + j, y_hi, y_lo,
                               waits=(lambda i: pe.wait_ge(y_lo_ready, 4 + i // 2 + 1)) if j == 0 else None)

            pe.wait_ge(lam_done, 1)
            pe.matmul(ps[:, 2, 400:402], ones[0:64, :], lam_prod[:], start=True, stop=True).then_inc(lam_mm, 1)
            mix_a0()
            norm(2, 2, False)
            ffn(1, 2, lambda: mod_sums(2))
            norm(3, 3, False)
            ffn(2, 3, lambda: mod_sums(3))
            norm(4, 4, False)
            mix_a1()
            norm(5, 5, False)
            ffn(3, 5)
            assert at.n == A_CHUNKS

            def mix_b(l):
                x_c = call_x(l, 0)
                evac0 = call_e(l, 0)

                def proj(g, n=256, waits=None):
                    if g >= 3:
                        pe.wait_ge(evac, evac0 + (g - 2))
                    cols_chunk(g % 3, x_hi, x_lo, n=n, waits=waits)

                pe.wait_ge(lay_small, l * 64 + 64)
                for g in range(3):
                    proj(g, waits=x_waits(x_c) if g == 0 else None)
                for t in range(TT):
                    for k in range(KT):
                        last = pe.matmul(ps[:, 3, t * 8:t * 8 + 8], x[:, k, t * P:t * P + P], w_ab[:, k, :],
                                         start=(k == 0), stop=(k == KT - 1))
                last.then_inc(ab_mm, 1)
                for k in range(KT):
                    last = pe.matmul(ps[0:64, 4, 0:T], w_kr[:, k, :], x[:, k, :], start=(k == 0), stop=(k == KT - 1))
                last.then_inc(kr_mm, 1)
                for g in range(3, 7):
                    proj(g)
                pe.wait_ge(ab_copied, l * 2 + 2)
                head_sums(8, work, 3, qkv_act, l * 6 + 4)
                for g in range(7, 9):
                    proj(g)
                head_rows(call_h(l, 0), 16, 4)
                for g in range(9, 11):
                    proj(g)
                pe.wait_ge(g_ready, l + 1)
                pe.wait_ge(qk_hat, l + 1)
                pe.matmul(ps[:, 3, 64:72], tri[:], gl[:, 9, :], start=True, stop=True)
                for i in range(8):
                    pe.matmul(ps[:, 4 + i // 4, (i % 4) * P:(i % 4) * P + P], diag[:, i, :], tri[:], start=True, stop=True)
                for i in range(8):
                    last = pe.matmul(ps[:, 6 + i // 4, (i % 4) * P:(i % 4) * P + P], diag[:, 8 + i, :], ident[:],
                                     start=True, stop=True)
                last.then_inc(g_mm, 1)
                for g in range(11, 13):
                    proj(g, n=128 if g >= 12 else 256)
                pe.wait_ge(dec_exp, l + 1)
                for c in range(2):
                    for h in range(HEADS):
                        kc = qkv[:, 4 + h, c * P:c * P + P]
                        pe.matmul(ps[:, 4 + c, h * P:h * P + P], kc, kc, start=True, stop=True)
                for c in range(2):
                    for h in range(HEADS):
                        last = pe.matmul(ps[:, 6 + c, h * P:h * P + P], qkv[:, 4 + h, c * P:c * P + P],
                                         qkv[:, h, c * P:c * P + P], start=True, stop=True)
                last.then_inc(kk_mm, 1)
                for g in range(13, 15):
                    proj(g, n=128)
                pe.wait_ge(a_ready, l + 1)
                pe.wait_ge(qkv_act, l * 6 + 6)
                for c in range(2):
                    for h in range(HEADS):
                        pe.transpose(ps[:, 4 + c, h * P:h * P + P], qkv[:, 4 + h, c * P:c * P + P], ident[:])
                for c in range(2):
                    for h in range(HEADS):
                        last = pe.transpose(ps[:, 6 + c, h * P:h * P + P], qkv[:, 8 + h, c * P:c * P + P], ident[:])
                last.then_inc(tok_mm, 1)
                for g in range(15, 17):
                    proj(g, n=128)
                pe.wait_ge(tok_done, l + 1)
                for s in range(LEVELS):
                    pe.wait_ge(b_ready, l * LEVELS + (s + 1))
                    pe.wait_ge(inv_ready, l * (LEVELS + 1) + (s + 1))
                    for i in range(8):
                        last = pe.matmul(ps[:, 4 + i // 4, (i % 4) * P:(i % 4) * P + P], bmat[:, i, :], dmat[:, i, :],
                                         start=True, stop=True)
                    last.then_inc(t_mm, 1)
                    if s < 4:
                        proj(17 + s)
                    pe.wait_ge(t_copied, l * LEVELS + (s + 1))
                    for i in range(8):
                        last = pe.matmul(ps[:, 6 + i // 4, (i % 4) * P:(i % 4) * P + P], emat[:, i, :], tmat[:, i, :],
                                         start=True, stop=True)
                    last.then_inc(inv_mm, 1)
                    for i in range(8):
                        last = pe.matmul(ps[:, 4 + i // 4, (i % 4) * P:(i % 4) * P + P], tmat[:, i, :], emat[:, i, :],
                                         start=True, stop=True)
                    last.then_inc(inv_mm, 1)
                pe.wait_ge(inv_ready, l * (LEVELS + 1) + LEVELS + 1)
                for i in range(8):
                    c, h = i // 4, i % 4
                    pe.matmul(ps[:, 4 + c, h * P:h * P + P], emat[:, i, :], v_beta[:, c, h * P:h * P + P],
                              start=True, stop=True)
                for h in range(HEADS):
                    last = pe.matmul(ps[:, 6, h * P:h * P + P], k_tok[:, 1, h * P:h * P + P], emat[:, 4 + h, :],
                                     start=True, stop=True)
                last.then_inc(u_mm, 1)
                pe.wait_ge(u_copied, l + 1)
                for h in range(HEADS):
                    last = pe.matmul(ps[:, 7, h * P:h * P + P], k_tok[:, 0, h * P:h * P + P], u_sb[:, h, :],
                                     start=True, stop=True)
                last.then_inc(s_mm, 1)
                pe.wait_ge(s_ready, l + 1)
                for h in range(HEADS):
                    last = pe.matmul(ps[:, 4, h * P:h * P + P], wt[:, h, :], s_state[:, h, :], start=True, stop=True)
                last.then_inc(ws_mm, 1)
                pe.wait_ge(v_new, l + 1)
                for h in range(HEADS):
                    dst = ps[:, 6 + h // 2, T * (h % 2):T * (h % 2) + T]
                    pe.matmul(dst[:, 0:P], u_sb[:, h, :], qk_dec[:, h, :], start=True, stop=True)
                    pe.matmul(dst[:, P:T], s_state[:, h, :], q_dec[:, h, :], start=True, stop=False)
                    last = pe.matmul(dst[:, P:T], u_sb[:, 4 + h, :], qk_dec[:, 4 + h, :], start=False, stop=True)
                last.then_inc(o_mm, 1)
                head_sums(4, work, 3, hd_sq, sq_at(l, 0))
                head_rows(call_h(l, 1), 8, 4)

                def branch(j, first):
                    for c in range(2):
                        cols_chunk(4 + 2 * c, y_hi, y_lo, kt=4, n=512, first=first,
                                   waits=(lambda i: pe.wait_ge(y_lo_ready, call_y(l, 2 * j) + i // 2 + 1))
                                   if c == 0 else None)

                branch(0, 0)
                for g in range(21, 25):
                    proj(g)
                pe.wait_ge(hd_sq, sq_at(l, 1))
                for i in range(4):
                    for t in range(TT):
                        pe.matmul(ps[:, 3, t:t + 1], work[:, 4 + i, t * P:t * P + P], ones[:, 0:1],
                                  start=(i == 0 and t == 0), stop=(i == 3), skip_group_check=True)
                        last = pe.matmul(ps[:, 3, 2 + t:3 + t], conv[:, i, t * P:t * P + P], ones[:, 0:1],
                                         start=False, stop=(i == 3), skip_group_check=True)
                last.then_inc(hd_stats, 1)
                head_rows(call_h(l, 2), 4, 3)
                pe.wait_ge(branch_free, l * 2 + 1)
                branch(1, 4)
                pe.wait_ge(hd_sq, sq_at(l, 2))
                for i in range(5):
                    for t in range(TT):
                        c = t if i < 3 else 2 + t
                        last = pe.matmul(ps[:, 3, c:c + 1], work[:, i, t * P:t * P + P], ones[:, 0:1],
                                         start=(i == 0 and t == 0), stop=(i in (2, 4)), skip_group_check=True)
                last.then_inc(hd_stats, 1)
                for g in range(25, 27):
                    proj(g)
                head_rows(call_h(l, 3), 4, 3)
                for g in range(27, 29):
                    proj(g)
                pe.wait_ge(branch_free, l * 2 + 2)
                pe.wait_ge(mla_w, l * 32 + 32)
                pe.wait_ge(hd_scaled, l + 2)
                for h in range(HEADS):
                    for k in range(3):
                        pe.matmul(ps[:, 4 + h // 2, T * (h % 2):T * (h % 2) + T], uq[:, k, 192 * h:192 * h + P],
                                  low[:, k, :], start=(k == 0), stop=(k == 2))
                for h in range(HEADS):
                    for k in range(3):
                        last = pe.matmul(ps[0:64, 6 + h // 2, T * (h % 2):T * (h % 2) + T],
                                         uq[:, k, 192 * h + P:192 * h + 192], low[:, k, :], start=(k == 0), stop=(k == 2))
                last.then_inc(mla_mm, 1)
                pe.wait_ge(mla_sb, l * 2 + 1)
                for h in range(HEADS):
                    for k in range(2):
                        pe.matmul(ps[:, 4 + h // 2, T * (h % 2):T * (h % 2) + T], ukv[:, k, 256 * h:256 * h + P],
                                  low[:, 3 + k, :], start=(k == 0), stop=(k == 1))
                ukv_v = ukv[:].rearrange("p k (h n) -> p k h n", h=HEADS)
                for t in range(TT):
                    for k in range(2):
                        last = pe.matmul(ps[:, 6 + t, :], low[:, 3 + k, t * P:t * P + P], ukv_v[:, k, :, P:2 * P],
                                         start=(k == 0), stop=(k == 1))
                last.then_inc(mla_mm, 1)
                pe.wait_ge(mla_sb, l * 2 + 2)
                for i in range(2):
                    pe.matmul(ps[:, 4 + i, :], rot[:], q_rope[:, 2 * i:2 * i + 2, :], start=True, stop=True)
                pe.matmul(ps[:, 3, 0:T], rot[:], k_rope[:], start=True, stop=True).then_inc(rot_mm, 1)
                pe.wait_ge(rope_done, l + 1)
                pe.wait_ge(evac, evac0 + 29)

                def score(h, b, bank):
                    dst = ps[:, bank, 0:P * (b + 1)]
                    pe.matmul(dst, q_nope[:, h, P * b:P * b + P], k_nope[:, h, 0:P * (b + 1)], start=True, stop=False)
                    return pe.matmul(dst, q_rope[:, h, P * b:P * b + P], k_rope[:, 0:P * (b + 1)], start=False, stop=True)

                attention(l * 8 + 8, score, v_mla)
                branch(2, 0)
                for j in range(4):
                    cols_chunk(4 + j, y_hi, y_lo,
                               waits=(lambda i: pe.wait_ge(y_lo_ready, call_y(l, 6) + i // 2 + 1)) if j == 0 else None)

            with pe.Fori(0, 2) as l:
                at.turns = l * LAYER_TURNS
                at.n = B0

                def turn_params():
                    pe.wait_ge(lay_rows, l * (17 * 16) + 17 * 16)
                    pe.transpose(ps[:, 2, 0:106], rows1[:], ident[0:106, 0:106])
                    pe.transpose(ps[:, 2, 128:176], rows2[:], ident[0:48, 0:48])
                    pe.transpose(ps[:, 2, 256:380], rows3[:], ident[0:124, 0:124]).then_inc(lay_turned, 1)

                ffn(l * 2 + 4, l * 3 + 6, turn_params)
                pe.wait_ge(lay_cols, l + 1)
                norm(call_n(l, 0), call_x(l, 0), True)
                mix_b(l)
                norm(call_n(l, 1), call_x(l, 1), True)
                ffn(l * 2 + 5, call_x(l, 1))
                norm(call_n(l, 2), call_x(l, 2), True)
            pe.wait_ge(x_lo_ready, 13 * 8)
            for t in range(TT):
                for m in range(KT):
                    last = pe.transpose(ps[:, 4 + 2 * t + m // 4, (m % 4) * P:(m % 4) * P + P],
                                        x[:, m, t * P:t * P + P], ident[:])
                    if m % 4 == 3:
                        last.then_inc(out_turned, 1)

        @block.scalar
        def _(act):
            f = nc.scalar.activation
            at = Place()
            limit = [A_CHUNKS]

            def convert():
                s, n = at.slot(), chunk_cols(at.n)
                act.wait_ge(landed[s], 16 * (at.turn() + 1))
                if at.n >= RING:
                    act.wait_ge(chunk_used, at.count(RING - 1))
                f(w_hi[s][:, 0:n], raw[s][:, 0:n], ACT.Copy).then_inc(hi_ready, 1)
                at.n += 1

            def ahead(n):
                while at.n < min(n, limit[0]):
                    convert()

            def chunk_done(n):
                act.wait_ge(chunk_used, 3 * at.turns + (n + 1))

            def sq(n, call, b=None):
                for m in range(KT):
                    if b is not None and m % 2 == 0:
                        ahead(b + m // 2 + 3)
                    act.wait_ge(x_new, call * 8 + (m + 1))
                    f(work[:, m, :], x[:, m, :], ACT.Square).then_inc(squares, 1)

            def norm_out(n, shift, dst):
                for k in range(KT):
                    act.wait_ge(scaled, n * 8 + (k + 1))
                    f(x_hi[:, k, :], work[:, k, :], ACT.Identity, bias=shift(k))
                    f(dst[:, k, :], work[:, k, :], ACT.Identity, bias=shift(k)).then_inc(x_hi_ready, 1)

            def ffn(b, call):
                def first_half(i, g):
                    chunk_done(g)
                    if not (isinstance(i, int) and i == 0):
                        act.wait_ge(hid_made, call * PAIRS + i)
                    f(silu_g[:], ps[:, 0, :], ACT.Silu).then_inc(gate_read, 1)

                def rounded(i):
                    act.wait_ge(hid_made, call * PAIRS + (i + 1))
                    f(hid_hi[:], hid[:].rearrange("p (k n) -> p k n", k=2), ACT.Copy).then_inc(hid_hi_ready, 1)

                ahead(b + 3)
                first_half(0, b)
                ahead(b + 5)
                rounded(0)
                base = at.turns
                with act.Fori(1, PAIRS - 1) as i:
                    at.turns = base + i - 1
                    first_half(i, b + 2)
                    convert()
                    convert()
                    chunk_done(b + 4)
                    rounded(i)
                    convert()
                    at.n -= 3
                at.turns = base
                at.n += 3 * (PAIRS - 2)
                last = b + 2 + 3 * (PAIRS - 2)
                first_half(PAIRS - 1, last)
                ahead(last + 5)
                chunk_done(last + 2)
                rounded(PAIRS - 1)
                ahead(last + 6)

            act.wait_ge(cols_ready, 1)
            f(c_act[:], a_cols[:, 77:85], ACT.Silu).then_inc(c_ready, 1)

            def shift_of(n):
                return lambda k: mod[:, 3 * n, k:k + 1]

            def exps(it, item0, heads, scale):
                act.wait_ge(at_max, item0 + (it + 1))
                if it >= 2:
                    act.wait_ge(at_weights, item0 + (it - 1))
                n = P * (it // HEADS + 1)
                for j in range(heads):
                    last = f(probs[:, it % 2, j, 0:n], masked[:, it % 2, j, 0:n], ACT.Exp,
                             bias=negmax[:, it, j:j + 1], scale=scale, accum_out=sums[:, it, j:j + 1])
                last.then_inc(at_probs, 1)

            def attention(item0, heads, scale):
                exps(0, item0, heads, scale)
                for it in range(8):
                    if it < 7:
                        exps(it + 1, item0, heads, scale)
                    act.wait_ge(at_turned, item0 + (it + 1))
                    if it >= 1:
                        act.wait_ge(at_out, item0 + it)
                    n = it // HEADS + 1
                    f(turned[:, 0:n, :], ps[:, 2 + it % 2, 0:n * P].rearrange("p (k n) -> p k n", k=n),
                      ACT.Copy).then_inc(at_copied, 1)
                act.wait_ge(at_out, item0 + 8)

            def two_banks(b):
                return ps[:, b:b + 2, :].rearrange("p b (k n) -> p (b k) n", k=2)

            def y_round(count0, made, src, pair):
                act.wait_ge(y_made, made)
                f(y_hi[:, 2 * pair:2 * pair + 2, :], src[:, 2 * pair:2 * pair + 2, :], ACT.Copy)\
                    .then_inc(y_hi_ready, 1)

            def mix_a0(b):
                for j in range(8):
                    ahead(b + j + 3)
                    chunk_done(b + j)
                    src = ps[:, j % 3, :].rearrange("p (k n) -> p k n", k=2)
                    if j < 4:
                        f(qk[:, 2 * j:2 * j + 2, :], src, ACT.Copy)
                        f(work[:, 2 * j:2 * j + 2, :], src, ACT.Square).then_inc(evac, 1)
                    elif j < 6:
                        f(v_tok[:, :, T * (j - 4):T * (j - 4) + T], src, ACT.Copy).then_inc(evac, 1)
                    else:
                        f(u_in[:, 2 * (j - 6):2 * (j - 6) + 2, :], src, ACT.Copy).then_inc(evac, 1)
                ahead(b + 11)
                attention(0, 2, QK_DIM ** -0.5)
                f(out_sb[:], two_banks(0), ACT.Copy)
                f(work[:, 0:4, :], two_banks(0), ACT.Square).then_inc(hd_sq, 1)
                act.wait_ge(pool_mm, 1)
                for i in range(4):
                    src = ps[:, 2 + i // 2, T * (i % 2):T * (i % 2) + T]
                    col = a_cols[:, 49 + i:50 + i]
                    f(work[:, 4 + i, :], src, ACT.Copy, scale=col)
                    last = f(y_hi[:, 4 + i, :], src, ACT.Copy, scale=col)
                    if i % 2:
                        last.then_inc(y_hi_ready, 1)
                for i in range(2):
                    y_round(0, i + 1, work, i)

            def mix_a1(b):
                for j in range(4):
                    n = b + 3 * j
                    chunk_done(n)
                    if j:
                        act.wait_ge(cx_read, j)
                    f(c_sb[:], ps[:, 0, :].rearrange("p (k n) -> p k n", k=2), ACT.Copy).then_inc(c_copied, 1)
                    ahead(n + 6)
                    y_round(4, 2 + j + 1, work, j)

            sq(0, 0)
            act.wait_ge(mod_ready, 1)
            ahead(3)
            norm_out(0, shift_of(0), work)
            ffn(0, 0)
            sq(1, 1)
            act.wait_ge(mod_ready, 2)
            norm_out(1, shift_of(1), work)
            act.wait_ge(lam_mm, 1)
            f(lam[:, 1:3], ps[:, 2, 400:402], ACT.Exp).then_inc(lam_exp, 1)
            ahead(A_MIX[0] + 3)
            mix_a0(A_MIX[0])
            sq(2, 2, A_MIX[0] + 8)
            ahead(A_FFN[1] + 3)
            norm_out(2, shift_of(2), work)
            ffn(A_FFN[1], 1)
            sq(3, 3)
            act.wait_ge(mod_ready, 3)
            norm_out(3, shift_of(3), work)
            ffn(A_FFN[2], 2)
            sq(4, 4)
            act.wait_ge(mod_ready, 4)
            norm_out(4, shift_of(4), work)
            ahead(A_MIX[1] + 3)
            mix_a1(A_MIX[1])
            sq(5, 5, A_MIX[1] + 12)
            ahead(A_FFN[3] + 3)
            norm_out(5, shift_of(5), work)
            ffn(A_FFN[3], 3)
            for k in range(KT):
                act.wait_ge(x_new, 6 * 8 + k + 1)
                f(x_hi[:, k, :], x[:, k, :], ACT.Copy).then_inc(x_hi_ready, 1)

            act.wait_ge(rope_conv, 1)
            f(sin_t[:], silu_g[0:64, 0:T], ACT.Sin)
            f(cos_t[:], silu_g[0:64, 0:T], ACT.Sin, scale=0.5).then_inc(rope_sin, 1)

            def mix_b(l):
                n0 = B_MIX

                def bank(g):
                    return ps[:, g % 3, :]

                def arrived(g):
                    ahead(n0 + pos(g) + 3)
                    chunk_done(n0 + pos(g))

                def act_qkv(g):
                    act.wait_ge(conv_done, l * 6 + (g + 1))
                    pair = qkv[:, 2 * g:2 * g + 2, :]
                    last = f(pair, pair, ACT.Silu)
                    if g < 4:
                        act.drain()
                        last = f(work[:, 2 * g:2 * g + 2, :], pair, ACT.Square)
                    last.then_inc(qkv_act, 1)

                def gate_out(g):
                    arrived(g)
                    br, j = (g - 17) // 4, (g - 17) % 4
                    if br and j == 0:
                        act.wait_ge(branch_free, l * 2 + br)
                    for i in range(2):
                        m = 2 * j + i
                        last = f(gate[:, m, :], bank(g)[:, T * i:T * i + T], ACT.Sigmoid,
                                 bias=cols1[:, CB_GATE + 8 * br + m:CB_GATE + 8 * br + m + 1])
                    last.then_inc(evac, 1)

                for g in range(6):
                    arrived(g)
                    if g:
                        act.wait_ge(conv_done, l * 6 + g)
                    f(stage[:], bank(g), ACT.Copy)
                    for i in range(2):
                        t = 2 * g + i
                        last = f(qkv[:, t, :], bank(g)[:, T * i:T * i + T], ACT.Copy, scale=cols2[:, 36 + t:37 + t])
                    last.then_inc(evac, 1)
                    act_qkv(g)
                    if g == 3:
                        act.wait_ge(ab_mm, l + 1)
                        f(ab[:], ps[:, 3, 0:16].rearrange("p (t n) -> p t n", t=TT), ACT.Copy).then_inc(ab_copied, 1)
                        act.wait_ge(kr_mm, l + 1)
                        f(k_rope[:], ps[0:64, 4, 0:T], ACT.Copy).then_inc(ab_copied, 1)
                    if g == 4:
                        act.wait_ge(ab_in, l + 1)
                        f(gl[:, 2, :], gl[:, 1, :], ACT.Exp)
                        f(gl[:, 3, :].rearrange("p (t h) -> p t h", t=TT), ab[:, :, 4:8], ACT.Exp, scale=-1.0)
                        f(gl[:, 4, 0:4], head_par[:, 0, :], ACT.Exp).then_inc(ab_exp, 1)
                for g in (6, 7):
                    arrived(g)
                    f(z_act[:, 2 * (g - 6):2 * (g - 6) + 2, :], bank(g).rearrange("p (k n) -> p k n", k=2), ACT.Silu)\
                        .then_inc(evac, 1)
                for g in range(8, 12):
                    arrived(g)
                    p = (g - 8) // 2
                    gated = g % 2
                    if g == 11:
                        act.wait_ge(glu_ready, l * 2 + 1)
                    for i in range(2):
                        t = 2 * p + i
                        c = CB_GLU + 4 * gated + t
                        last = f(sig[:, i, :] if gated else glu[:, t, :], bank(g)[:, T * i:T * i + T],
                                 ACT.Sigmoid if gated else ACT.Identity, bias=cols1[:, c:c + 1])
                    last.then_inc(evac, 1)
                act.wait_ge(dec_in, l + 1)
                f(emat[:], emat[:], ACT.Exp)
                f(gl[:, 8, 0:4], gcol[:, 4:8], ACT.Exp)
                f(gl[:, 8, 4:8], gl[:, 11, 0:4], ACT.Exp)
                f(q_dec[:], ps[:, 5, :].rearrange("p (h n) -> p h n", h=HEADS), ACT.Exp)
                f(tmat[:], ps[:, 6:8, :].rearrange("p b (h n) -> p (b h) n", n=P), ACT.Copy).then_inc(dec_exp, 1)
                for g in range(12, 17):
                    arrived(g)
                    f(low[:, g - 12, :], bank(g)[:, 0:T], ACT.Copy).then_inc(evac, 1)
                for s in range(LEVELS):
                    act.wait_ge(t_mm, l * LEVELS + (s + 1))
                    f(tmat[:], ps[:, 4:6, :].rearrange("p b (h n) -> p (b h) n", n=P), ACT.Copy).then_inc(t_copied, 1)
                    if s < 4:
                        gate_out(17 + s)
                act.wait_ge(u_mm, l + 1)
                f(u_sb[:], ps[:, 4:6, :].rearrange("p b (h n) -> p (b h) n", n=P), ACT.Copy)
                f(wt[:], ps[:, 6, :].rearrange("p (h n) -> p h n", n=P), ACT.Copy).then_inc(u_copied, 1)
                act.wait_ge(o_mm, l + 1)
                f(out_sb[:], two_banks(6), ACT.Copy)
                f(work[:, 0:4, :], two_banks(6), ACT.Square).then_inc(hd_sq, 1)
                for i in range(2):
                    y_round(0, 6 * l + (7 + i), work, i)
                for g in range(21, 25):
                    gate_out(g)
                act.wait_ge(cv_dve, l + 1)
                act.wait_ge(cv_pool, l + 1)
                f(work[:, 4:8, :], conv[:], ACT.Square).then_inc(hd_sq, 1)
                act.wait_ge(cv_scaled, l + 1)
                for t in range(4):
                    f(work[:, 4 + t, :], conv[:, t, :], ACT.Silu, scale=cols1[:, CB_LNG + t:CB_LNG + t + 1],
                      bias=cols1[:, CB_LNB + t:CB_LNB + t + 1])
                act.drain()
                for i in range(2):
                    f(y_hi[:, 4 + 2 * i:6 + 2 * i, :], work[:, 4 + 2 * i:6 + 2 * i, :], ACT.Copy).then_inc(y_hi_ready, 1)
                act.wait_ge(y_lo_ready, call_y(l, 4))
                f(work[:, 0:5, :], low[:], ACT.Square).then_inc(hd_sq, 1)
                for g in range(25, 29):
                    gate_out(g)
                act.wait_ge(mla_mm, l * 2 + 1)
                f(q_nope[:], two_banks(4), ACT.Copy)
                f(q_rope[:], ps[0:64, 6:8, :].rearrange("p b (k n) -> p (b k) n", k=2), ACT.Copy).then_inc(mla_sb, 1)
                act.wait_ge(mla_mm, l * 2 + 2)
                f(k_nope[:], two_banks(4), ACT.Copy)
                f(v_mla[:], ps[:, 6:8, :], ACT.Copy).then_inc(mla_sb, 1)
                attention(l * 8 + 8, 1, 192 ** -0.5)
                for i in range(2):
                    src = ps[:, i, :].rearrange("p (k n) -> p k n", k=2)
                    f(work[:, 2 * i:2 * i + 2, :], src, ACT.Copy)
                    f(y_hi[:, 2 * i:2 * i + 2, :], src, ACT.Copy).then_inc(y_hi_ready, 1)
                ahead(n0 + 33 + 3)
                for i in range(4):
                    y_round(0, 6 * l + (9 + i), merged, i)

            with act.Fori(0, 2) as l:
                at.turns = l * LAYER_TURNS
                at.n = B0
                limit[0] = B0 + B_LAYER_CH
                col = lambda c0: (lambda k: cols1[:, c0 + k:c0 + k + 1])
                ffn(B0, l * 2 + 4)
                sq(call_n(l, 0), call_x(l, 0))
                act.wait_ge(lay_cols, l + 1)
                norm_out(call_n(l, 0), col(LN_B[0]), x)
                ahead(B_MIX + 3)
                mix_b(l)
                sq(call_n(l, 1), call_x(l, 1), B_MIX + 35)
                ahead(B_FFN[1] + 3)
                norm_out(call_n(l, 1), col(LN_B[1]), x)
                ffn(B_FFN[1], l * 2 + 5)
                sq(call_n(l, 2), call_x(l, 2))
                norm_out(call_n(l, 2), col(LN_B[2]), x)
            for i in range(4):
                act.wait_ge(out_turned, i + 1)
                f(y_rows[:, i // 2, 512 * (i % 2):512 * (i % 2) + 512], ps[:, 4 + i, :], ACT.Copy).then_inc(out_copied, 1)

        @block.vector
        def _(dve):
            v = nc.vector
            at = Place()
            limit = [A_CHUNKS]

            def convert():
                s, n = at.slot(), chunk_cols(at.n)
                dve.wait_ge(hi_ready, at.count() + 1)
                v.tensor_tensor(w_lo[s][:, 0:n], raw[s][:, 0:n], w_hi[s][:, 0:n].bitcast(F32), ALU.subtract)\
                    .then_inc(lo_ready, 1)
                at.n += 1

            def ahead(n):
                while at.n < min(n, limit[0]):
                    convert()

            def chunk_done(n):
                dve.wait_ge(chunk_used, 3 * at.turns + (n + 1))

            def lo_of(dst, whole, hi):
                return v.tensor_tensor(dst, whole, hi.bitcast(F32), ALU.subtract)

            def make_diag(n, done):
                v.tensor_tensor(diag[:, 0:n, :], bc(ident[:].unsqueeze(1), (P, n, P)),
                                bc(rstd[:, 0:n].unsqueeze(2), (P, n, P)), ALU.mult).then_inc(done, 1)

            def mean_moments(bank, n, eps, done):
                v.tensor_scalar(small[:, 0:4], ps[:, bank, 0:4], 1.0 / n, None, ALU.mult)
                dve.drain()
                v.tensor_tensor(small[:, 4:6], small[:, 2:4], small[:, 2:4], ALU.mult)
                dve.drain()
                v.tensor_tensor(small[:, 6:8], small[:, 0:2], small[:, 4:6], ALU.subtract)
                dve.drain()
                v.tensor_scalar(moment[:, 0:2], small[:, 6:8], 0.0, eps, ALU.max, ALU.add).then_inc(done, 1)

            def mean_scales():
                v.scalar_tensor_tensor(out=rstd[:, 2:4], in0=small[:, 2:4], scalar=-1.0, in1=rstd[:, 0:2],
                                       op0=ALU.mult, op1=ALU.mult)
                dve.drain()

            def norm_a(n):
                dve.wait_ge(stats, n + 1)
                v.tensor_scalar(moment[:, 0:2], ps[:, 2, 0:2], 1.0 / D, A_EPS, ALU.mult, ALU.add).then_inc(moments, 1)
                dve.wait_ge(rstd_ready, n + 1)
                make_diag(2, diag_ready)
                dve.wait_ge(rows_ready, n + 1)
                for k in range(KT):
                    v.scalar_tensor_tensor(out=work[:, k, :], in0=x[:, k, :], scalar=norm_col[:, n, k:k + 1],
                                           in1=ps[:, 3, 0:T], op0=ALU.mult, op1=ALU.mult).then_inc(scaled, 1)

            def norm_b(n, gain, eps):
                dve.wait_ge(stats, n + 1)
                mean_moments(2, D, eps, moments)
                dve.wait_ge(rstd_ready, n + 1)
                mean_scales()
                make_diag(4, diag_ready)
                dve.wait_ge(rows_ready, n + 1)
                for k in range(KT):
                    v.scalar_tensor_tensor(out=work[:, k, :], in0=x[:, k, :], scalar=gain(k), in1=ps[:, 3, 0:T],
                                           op0=ALU.mult, op1=ALU.mult)
                    dve.drain()
                    v.scalar_tensor_tensor(out=work[:, k, :], in0=ps[:, 3, T:2 * T], scalar=gain(k), in1=work[:, k, :],
                                           op0=ALU.mult, op1=ALU.add).then_inc(scaled, 1)

            def x_lo_parts(call, whole):
                for k in range(KT):
                    dve.wait_ge(x_hi_ready, call * 8 + (k + 1))
                    lo_of(x_lo[:, k, :], whole[:, k, :], x_hi[:, k, :]).then_inc(x_lo_ready, 1)

            def residual_a(n):
                for m in range(KT):
                    v.scalar_tensor_tensor(out=x[:, m, :], in0=acc(m), scalar=gate_col[:, n, m:m + 1], in1=x[:, m, :],
                                           op0=ALU.mult, op1=ALU.add).then_inc(x_new, 1)

            def residual_b(scale):
                for m in range(KT):
                    v.scalar_tensor_tensor(out=x[:, m, :], in0=x[:, m, :], scalar=scale, in1=acc(m),
                                           op0=ALU.mult, op1=ALU.add).then_inc(x_new, 1)

            def residual_chunks(b, how):
                for c in range(4):
                    ahead(b + c + 3)
                    chunk_done(b + c)
                    for m in (2 * c, 2 * c + 1):
                        how(m)
                ahead(b + 7)

            def ada_steps(grp, k, js):
                l, m0, width, unit0, round0 = GROUPS[grp]
                first = isinstance(k, int) and k == 0
                dve.drain()
                for j in js:
                    if grp == 0:
                        u = 3 * k + j
                        slot, turn = u % ADA_SLOTS, u // ADA_SLOTS + 1
                    else:
                        slot, turn = j, k + (round0 + 1)
                    dve.wait_ge(ada_landed[slot], turn * 16)
                    ck = c_act[:, k:k + 1] if isinstance(k, int) else c_act[:, ds(k, 1)]
                    if first:
                        v.tensor_scalar(ada_acc[:, j, :], ada_raw[slot][:], ck, None, ALU.mult).then_inc(ada_used, 1)
                    else:
                        v.scalar_tensor_tensor(out=ada_acc[:, j, :], in0=ada_raw[slot][:], scalar=ck,
                                               in1=ada_acc[:, j, :], op0=ALU.mult, op1=ALU.add).then_inc(ada_used, 1)

            def mod_finish(grp):
                l, m0, width, _, _ = GROUPS[grp]
                dve.wait_ge(mod_summed, grp + 1)
                m = 9 * l + m0
                v.tensor_tensor(mod[:, m:m + width, :], ps[:, 1, 0:width * KT].rearrange("p (j t) -> p j t", t=KT),
                                b_cols[:, l, m0 * KT:(m0 + width) * KT].rearrange("p (j t) -> p j t", t=KT), ALU.add)
                dve.drain()
                for n in range(m // 3, (m + width) // 3):
                    v.scalar_tensor_tensor(out=norm_col[:, n, :], in0=mod[:, 3 * n + 1, :], scalar=1.0,
                                           in1=a_cols[:, 8 * n:8 * n + 8], op0=ALU.add, op1=ALU.mult)
                    v.tensor_scalar(gate_col[:, n, :], mod[:, 3 * n + 2, :], 1.0 if n % 3 == 1 else 0.5, None, ALU.mult)
                dve.drain().then_inc(mod_ready, 1)

            def ffn(b, call, grp=None):
                width = GROUPS[grp][2] if grp is not None else 0
                third = width // 3

                def made(i, g):
                    dve.drain()
                    dve.wait_ge(gate_read, call * PAIRS + (i + 1))
                    chunk_done(g + 1)
                    if not (isinstance(i, int) and i == 0):
                        dve.wait_ge(hid_hi_ready, call * PAIRS + i)
                    v.tensor_tensor(hid[:], silu_g[:], ps[:, 1, :], ALU.mult).then_inc(hid_made, 1)

                def rest(i):
                    dve.wait_ge(hid_hi_ready, call * PAIRS + (i + 1))
                    lo_of(hid_lo[:], hid[:].rearrange("p (k n) -> p k n", k=2), hid_hi[:]).then_inc(hid_lo_ready, 1)

                def ada(k, part):
                    if grp is not None:
                        ada_steps(grp, k, range(part * third, part * third + third))

                ahead(b + 3)
                ada(0, 0)
                made(0, b)
                ahead(b + 5)
                ada(0, 1)
                rest(0)
                ada(0, 2)
                base = at.turns

                def body(i, with_ada):
                    convert()
                    if with_ada:
                        ada(i, 0)
                    made(i, b + 2)
                    convert()
                    if with_ada:
                        ada(i, 1)
                    rest(i)
                    convert()
                    if with_ada:
                        ada(i, 2)
                    at.n -= 3

                split = KT if grp is not None else 1
                if grp is not None:
                    with dve.Fori(1, KT) as i:
                        at.turns = base + i - 1
                        body(i, True)
                with dve.Fori(split, PAIRS - 1) as i:
                    at.turns = base + i - 1
                    body(i, False)
                at.turns = base
                at.n += 3 * (PAIRS - 2)
                last = b + 2 + 3 * (PAIRS - 2)
                ahead(last + 4)
                made(PAIRS - 1, last)
                ahead(last + 5)
                rest(PAIRS - 1)
                if grp is not None:
                    mod_finish(grp)
                ahead(last + 6)
                chunk_done(last + 3)

            def attention(item0, heads, scale):
                def mask(it):
                    n = P * (it // HEADS + 1)
                    par = it % 2
                    dve.wait_ge(at_scores, item0 + (it + 1))
                    if it >= 2:
                        dve.wait_ge(at_probs, item0 + (it - 1))
                    src = ps[:, 4 + 2 * par:4 + 2 * par + heads, 0:n]
                    v.tensor_tensor(masked[:, par, 0:heads, 0:n], src,
                                    bc(cmask[:, T - n:T].unsqueeze(1), (P, heads, n)), ALU.add)\
                        .then_inc(at_masked, 1)
                    dve.drain()
                    v.tensor_reduce(recips[:, it, 0:heads], masked[:, par, 0:heads, 0:n], AX, ALU.max)
                    dve.drain()
                    v.tensor_scalar(negmax[:, it, 0:heads], recips[:, it, 0:heads], -scale, None, ALU.mult)\
                        .then_inc(at_max, 1)

                def weight(it):
                    n = P * (it // HEADS + 1)
                    par = it % 2
                    dve.wait_ge(at_probs, item0 + (it + 1))
                    v.reciprocal(recips[:, it, 0:heads], sums[:, it, 0:heads])
                    dve.drain()
                    if it >= 1:
                        dve.wait_ge(at_turned, item0 + it)
                    if heads == 1:
                        v.tensor_scalar(weights[:, 0:n], probs[:, par, 0, 0:n], recips[:, it, 0:1], None, ALU.mult)\
                            .then_inc(at_weights, 1)
                        return
                    v.tensor_scalar(weights[:, 0:n], probs[:, par, 1, 0:n], recips[:, it, 1:2], lam[:, 0:1],
                                    ALU.mult, ALU.mult)
                    dve.drain()
                    v.scalar_tensor_tensor(out=weights[:, 0:n], in0=probs[:, par, 0, 0:n], scalar=recips[:, it, 0:1],
                                           in1=weights[:, 0:n], op0=ALU.mult, op1=ALU.add).then_inc(at_weights, 1)

                mask(0)
                for it in range(8):
                    if it < 7:
                        mask(it + 1)
                    weight(it)

            def y_rest(count, whole, pair):
                dve.wait_ge(y_hi_ready, count)
                sl = slice(2 * pair, 2 * pair + 2)
                lo_of(y_lo[:, sl, :], whole[:, sl, :], y_hi[:, sl, :]).then_inc(y_lo_ready, 1)

            def head_scales(call, bank, n, inv, eps):
                dve.wait_ge(hd_stats, call + 1)
                v.tensor_scalar(moment[:, 0:n], ps[:, bank, 0:n], inv, eps, ALU.mult, ALU.add).then_inc(hd_moment, 1)
                dve.wait_ge(hd_rstd, call + 1)

            v.memset(ones[:], 1.0)
            v.memset(zeros[:], 0.0)
            v.memset(vpad[:], 0.0)
            dve.drain().then_inc(const_dve, 1)
            dve.wait_ge(rows_turned, 1)
            v.tensor_copy(a_cols[:], ps[:, 0, 0:85])
            v.tensor_copy(b_cols[:, 0, :], ps[:, 0, 128:200])
            v.tensor_copy(b_cols[:, 1, :], ps[:, 0, 256:328])
            dve.drain().then_inc(cols_ready, 1)
            dve.wait_ge(const_ready, 1)
            v.tensor_copy(win[0][:, 0, :], count_i[:])
            dve.drain()
            for n, width in enumerate(WINDOWS):
                v.tensor_scalar(win[1][:, n, :], win[0][:, 0, :], float(width), None, ALU.min)
            dve.drain()
            v.reciprocal(inv_count[:], win[1][:])
            for m in range(KT):
                if m % 2 == 0:
                    dve.wait_ge(x_turned, m + 2)
                v.tensor_copy(x[:, m, :], acc(m)).then_inc(x_new, 1)
            dve.wait_ge(c_ready, 1)
            for k in range(KT):
                ada_steps(0, k, range(3))
            mod_finish(0)
            dve.wait_ge(params2_in, 9 * 16)
            v.tensor_tensor(lam_prod[:, 0:1], lam_in[:, 0:1], lam_in[:, 1:2], ALU.mult)
            v.tensor_tensor(lam_prod[:, 1:2], lam_in[:, 2:3], lam_in[:, 3:4], ALU.mult)
            v.tensor_scalar(sub_gain[:], a_cols[:, 48:49], 1.0 - LAM_INIT, None, ALU.mult)
            dve.drain().then_inc(lam_done, 1)

            norm_a(0)
            x_lo_parts(0, work)
            ffn(0, 0, 1)
            residual_a(0)
            norm_a(1)
            x_lo_parts(1, work)

            def mix_a0(b):
                for j in range(8):
                    ahead(b + j + 3)
                    if j == 5:
                        head_scales(0, 4, 32, 1.0 / QK_DIM, A_EPS)
                        v.tensor_copy(bc_half[:].rearrange("p i (s n) -> p (i s) n", s=2),
                                      bc(rstd[:].unsqueeze(2), (P, 32, 64))).then_inc(hd_diag, 1)
                dve.wait_ge(lam_exp, 1)
                v.tensor_tensor(lam[:, 3:4], lam[:, 2:3], lam[:, 1:2], ALU.subtract)
                dve.drain()
                v.tensor_scalar(lam[:, 0:1], lam[:, 3:4], -LAM_INIT, None, ALU.add)
                dve.wait_ge(hd_rows, 1)
                for i in range(4):
                    last = v.scalar_tensor_tensor(
                        out=qk[:, 2 * i:2 * i + 2, :], in0=qk[:, 2 * i:2 * i + 2, :], scalar=qk_gain[:, i // 2:i // 2 + 1],
                        in1=ps[:, 4 + i, :].rearrange("p (k n) -> p k n", k=2), op0=ALU.mult, op1=ALU.mult)
                last.then_inc(hd_scaled, 1)
                ahead(b + 11)
                attention(0, 2, QK_DIM ** -0.5)
                head_scales(1, 4, 8, 1.0 / P, A_EPS)
                make_diag(8, hd_diag)
                for i in range(2):
                    y_rest(i + 1, work, 2 + i)
                dve.wait_ge(hd_rows, 2)
                for i in range(2):
                    v.scalar_tensor_tensor(
                        out=work[:, 2 * i:2 * i + 2, :], in0=out_sb[:, 2 * i:2 * i + 2, :], scalar=sub_gain[:, 0:1],
                        in1=ps[:, 6 + i, :].rearrange("p (k n) -> p k n", k=2), op0=ALU.mult, op1=ALU.mult)\
                        .then_inc(y_made, 1)
                for i in range(2):
                    y_rest(i + 3, work, i)

            def gated(n):
                return lambda m: v.scalar_tensor_tensor(
                    out=x[:, m, :], in0=acc(m), scalar=gate_col[:, n, m:m + 1], in1=x[:, m, :],
                    op0=ALU.mult, op1=ALU.add).then_inc(x_new, 1)

            def mix_a1(b):
                for j in range(4):
                    n = b + 3 * j
                    ahead(n + 4)
                    chunk_done(n + 1)
                    dve.wait_ge(c_copied, j + 1)
                    v.tensor_tensor(vpad[:, :, 2:T + 2], c_sb[:], ps[:, 1, :].rearrange("p (k n) -> p k n", k=2), ALU.mult)\
                        .then_inc(cx_read, 1)
                    dve.drain()
                    for tap in range(3):
                        for i in range(2):
                            t = 2 * j + i
                            col = a_cols[:, 53 + 8 * tap + t:54 + 8 * tap + t]
                            if tap == 0:
                                v.tensor_scalar(work[:, t, :], vpad[:, i, 0:T], col, None, ALU.mult)
                            else:
                                v.scalar_tensor_tensor(out=work[:, t, :], in0=vpad[:, i, tap:T + tap], scalar=col,
                                                       in1=work[:, t, :], op0=ALU.mult, op1=ALU.add)
                        dve.drain()
                    ahead(n + 5)
                    chunk_done(n + 2)
                    v.tensor_tensor(work[:, 2 * j:2 * j + 2, :], work[:, 2 * j:2 * j + 2, :],
                                    ps[:, 2, :].rearrange("p (k n) -> p k n", k=2), ALU.mult).then_inc(y_made, 1)
                    ahead(n + 6)
                    y_rest(4 + j + 1, work, j)

            ahead(A_MIX[0] + 3)
            mix_a0(A_MIX[0])
            residual_chunks(A_MIX[0] + 8, gated(1))
            norm_a(2)
            x_lo_parts(2, work)
            ffn(A_FFN[1], 1, 2)
            residual_a(2)
            norm_a(3)
            x_lo_parts(3, work)
            ffn(A_FFN[2], 2, 3)
            residual_a(3)
            norm_a(4)
            x_lo_parts(4, work)
            ahead(A_MIX[1] + 3)
            mix_a1(A_MIX[1])
            residual_chunks(A_MIX[1] + 12, gated(4))
            norm_a(5)
            x_lo_parts(5, work)
            ffn(A_FFN[3], 3)
            residual_a(5)
            x_lo_parts(6, x)

            angle, turns_f = silu_g[0:64, 0:T], hid[0:64, T:2 * T]
            dve.wait_ge(rope_pow, 1)
            dve.wait_ge(rope_in, 16)
            v.tensor_copy(angle, pos_i)
            dve.drain()
            v.tensor_scalar(angle, angle, inv_freq[:, 2:3], None, ALU.mult)
            dve.drain()
            v.tensor_scalar(rope_k[:], angle, 1.0 / (2 * math.pi), None, ALU.mult)
            dve.drain()
            v.tensor_copy(turns_f, rope_k[:])
            two_pi = 2 * math.pi
            part1 = 6.28125
            part2 = round((two_pi - part1) * 2 ** 21) / 2 ** 21
            for part in (part1, part2, two_pi - part1 - part2):
                dve.drain()
                v.scalar_tensor_tensor(out=angle, in0=turns_f, scalar=-part, in1=angle, op0=ALU.mult, op1=ALU.add)
            dve.drain()
            v.tensor_scalar(angle, angle, 3.1415925, -3.1415925, ALU.min, ALU.max).then_inc(rope_conv, 1)
            dve.wait_ge(rope_sin, 1)
            v.tensor_tensor(cos_t[:], cos_t[:], cos_t[:], ALU.mult)
            dve.drain()
            v.tensor_scalar(cos_t[:], cos_t[:], -2.0, 1.0, ALU.mult, ALU.add)

            def mix_b(l):
                n0 = B_MIX

                def evacuated(g):
                    dve.wait_ge(evac, call_e(l, g + 1))

                def log_decay():
                    dve.wait_ge(ab_exp, l + 1)
                    v.tensor_scalar(gl[:, 5, :], gl[:, 2, :], 2.0, None, ALU.add)
                    v.tensor_scalar(gl[:, 10, :], gl[:, 3, :], 1.0, None, ALU.add)
                    dve.drain()
                    v.reciprocal(gl[:, 6, :], gl[:, 5, :])
                    v.reciprocal(gl[:, 10, :], gl[:, 10, :])
                    dve.drain()
                    v.tensor_tensor(gl[:, 6, :], gl[:, 2, :], gl[:, 6, :], ALU.mult)
                    dve.drain()
                    v.tensor_tensor(gl[:, 7, :], gl[:, 6, :], gl[:, 6, :], ALU.mult)
                    dve.drain()
                    v.tensor_scalar(gl[:, 5, :], gl[:, 7, :], 1.0 / 15, None, ALU.mult)
                    for odd in (13, 11, 9, 7, 5, 3):
                        dve.drain()
                        v.scalar_tensor_tensor(out=gl[:, 5, :], in0=gl[:, 5, :], scalar=1.0 / odd, in1=gl[:, 7, :],
                                               op0=ALU.add, op1=ALU.mult)
                    dve.drain()
                    v.scalar_tensor_tensor(out=gl[:, 5, :], in0=gl[:, 5, :], scalar=1.0, in1=gl[:, 6, :],
                                           op0=ALU.add, op1=ALU.mult)
                    v.tensor_scalar(gl[:, 0, :], gl[:, 0, :], 0.0, None, ALU.max)
                    dve.drain()
                    v.scalar_tensor_tensor(out=gl[:, 5, :], in0=gl[:, 5, :], scalar=2.0, in1=gl[:, 0, :],
                                           op0=ALU.mult, op1=ALU.add)
                    dve.drain()
                    v.scalar_tensor_tensor(out=gl[:, 9, :].rearrange("p (t h) -> p t h", t=TT),
                                           in0=gl[:, 5, :].rearrange("p (t h) -> p t h", t=TT), scalar=-1.0,
                                           in1=bc(gl[:, 4, 0:4].unsqueeze(1), (P, TT, 4)), op0=ALU.mult, op1=ALU.mult)

                def level(s):
                    v.scalar_tensor_tensor(out=bmat, in0=bc(levels[:].unsqueeze(1), (P, 8, P)), scalar=s + 1.0,
                                           in1=amat, op0=ALU.is_equal, op1=ALU.mult).then_inc(b_ready, 1)

                for g in range(6):
                    ahead(n0 + g + 3)
                    evacuated(g)
                    for tap in (2, 1, 0):
                        sh = 3 - tap
                        for i in range(2):
                            t = 2 * g + i
                            last = v.scalar_tensor_tensor(
                                out=qkv[:, t, sh:T], in0=stage[:, T * i:T * i + T - sh],
                                scalar=cols2[:, 12 * tap + t:12 * tap + t + 1], in1=qkv[:, t, sh:T],
                                op0=ALU.mult, op1=ALU.add)
                        if tap:
                            dve.drain()
                    last.then_inc(conv_done, 1)
                    if g == 3:
                        dve.wait_ge(ab_copied, l * 2 + 2)
                        v.tensor_tensor(gl[:, 0, :].rearrange("p (t h) -> p t h", t=TT), ab[:, :, 0:4],
                                        bc(head_par[:, 1, :].unsqueeze(1), (P, TT, 4)), ALU.add)
                        dve.drain()
                        v.tensor_scalar(gl[:, 1, :], gl[:, 0, :], -1.0, None, ALU.mult)
                        dve.drain()
                        v.tensor_tensor(gl[:, 1, :], gl[:, 0, :], gl[:, 1, :], ALU.min).then_inc(ab_in, 1)
                    if g == 5:
                        log_decay()
                ahead(n0 + 9)
                head_scales(call_h(l, 0), 3, 16, 1.0, 1e-6)
                v.tensor_scalar(rstd[:, 0:8], rstd[:, 0:8], P ** -0.5, None, ALU.mult)
                dve.drain()
                make_diag(16, hd_diag)
                ahead(n0 + 11)
                dve.wait_ge(hd_rows, call_h(l, 0) + 1)
                for i in range(4):
                    last = v.tensor_tensor(qkv[:, 2 * i:2 * i + 2, :], qkv[:, 2 * i:2 * i + 2, :],
                                           ps[:, 4 + i, :].rearrange("p (k n) -> p k n", k=2), ALU.mult)
                last.then_inc(qk_hat, 1)
                v.tensor_copy(diag[:, 0:8, :], bc(gl[:, 9, :].unsqueeze(2), (P, 8, P)))
                v.tensor_copy(diag[:, 8:16, :], bc(gl[:, 10, :].unsqueeze(2), (P, 8, P))).then_inc(g_ready, 1)
                ahead(n0 + 12)
                evacuated(9)
                v.tensor_tensor(glu[:, 0:2, :], glu[:, 0:2, :], sig[:], ALU.mult).then_inc(glu_ready, 1)
                ahead(n0 + 13)
                dve.wait_ge(g_mm, l + 1)
                v.tensor_copy(gcol[:], ps[:, 3, 64:72])
                dve.drain()
                for c in range(2):
                    v.tensor_tensor(emat[:, 4 * c:4 * c + 4, :], ps[:, 4 + c, :].rearrange("p (h n) -> p h n", n=P),
                                    bc(gcol[:, 4 * c:4 * c + 4].unsqueeze(2), (P, 4, P)), ALU.subtract)
                v.tensor_tensor(gl[:, 11, 0:4], ps[:, 4, :].rearrange("p (h n) -> p h n", n=P)[:, :, P - 1],
                                gcol[:, 0:4], ALU.subtract)
                dve.drain()
                v.tensor_scalar(emat[:], emat[:], 0.0, None, ALU.min).then_inc(dec_in, 1)
                ahead(n0 + 14)
                evacuated(11)
                v.tensor_tensor(glu[:, 2:4, :], glu[:, 2:4, :], sig[:], ALU.mult).then_inc(glu_ready, 1)
                dve.wait_ge(dec_exp, l + 1)
                v.tensor_tensor(emat[:], emat[:], bc(tri[:].unsqueeze(1), (P, 8, P)), ALU.mult)
                v.tensor_tensor(q_dec[:], q_dec[:], qkv[:, 0:4, P:T], ALU.mult)
                v.tensor_tensor(gl[:, 7, 0:4], gl[:, 10, 4:8], gl[:, 8, 0:4], ALU.mult)
                ahead(n0 + 15)
                dve.drain()
                dve.wait_ge(kk_mm, l + 1)
                for c in range(2):
                    cs = slice(4 * c, 4 * c + 4)
                    v.tensor_tensor(amat[:, cs, :], emat[:, cs, :], ps[:, 4 + c, :].rearrange("p (h n) -> p h n", n=P), ALU.mult)
                    v.tensor_tensor(qk_dec[:, cs, :], emat[:, cs, :], ps[:, 6 + c, :].rearrange("p (h n) -> p h n", n=P), ALU.mult)
                dve.drain()
                v.tensor_tensor(amat[:], amat[:], tmat[:], ALU.mult).then_inc(a_ready, 1)
                v.tensor_copy(dmat[:], bc(ident[:].unsqueeze(1), (P, 8, P)))
                v.tensor_copy(emat[:], bc(ident[:].unsqueeze(1), (P, 8, P))).then_inc(inv_ready, 1)
                dve.drain()
                level(0)
                ahead(n0 + 17)
                dve.wait_ge(tok_mm, l + 1)
                for c in range(2):
                    col = gl[:, 8, 4:8] if c == 0 else gl[:, 7, 0:4]
                    v.tensor_tensor(k_tok[:, c, :].rearrange("p (h n) -> p h n", n=P),
                                    ps[:, 4 + c, :].rearrange("p (h n) -> p h n", n=P),
                                    bc(col.unsqueeze(2), (P, 4, P)), ALU.mult)
                    last = v.tensor_tensor(v_beta[:, c, :].rearrange("p (h n) -> p h n", n=P),
                                           ps[:, 6 + c, :].rearrange("p (h n) -> p h n", n=P),
                                           bc(gl[:, 10, 4 * c:4 * c + 4].unsqueeze(2), (P, 4, P)), ALU.mult)
                last.then_inc(tok_done, 1)
                ahead(n0 + 19)
                for s in range(LEVELS):
                    if s + 1 < LEVELS:
                        dve.wait_ge(t_mm, l * LEVELS + (s + 1))
                        level(s + 1)
                    dve.wait_ge(inv_mm, l * (2 * LEVELS) + (2 * s + 1))
                    v.tensor_tensor(dmat[:], dmat[:], ps[:, 6:8, :].rearrange("p b (h n) -> p (b h) n", n=P), ALU.subtract)
                    dve.wait_ge(inv_mm, l * (2 * LEVELS) + (2 * s + 2))
                    v.tensor_tensor(emat[:], emat[:], ps[:, 4:6, :].rearrange("p b (h n) -> p (b h) n", n=P), ALU.subtract)\
                        .then_inc(inv_ready, 1)
                    if s < 4:
                        ahead(n0 + 17 + s + 3)
                dve.wait_ge(s_mm, l + 1)
                v.tensor_copy(s_state[:], ps[:, 7, :].rearrange("p (h n) -> p h n", n=P)).then_inc(s_ready, 1)
                dve.wait_ge(ws_mm, l + 1)
                v.tensor_tensor(u_sb[:, 4:8, :], u_sb[:, 4:8, :], ps[:, 4, :].rearrange("p (h n) -> p h n", n=P), ALU.subtract)\
                    .then_inc(v_new, 1)
                head_scales(call_h(l, 1), 3, 8, 1.0 / P, B_EPS)
                make_diag(8, hd_diag)
                dve.wait_ge(hd_rows, call_h(l, 1) + 1)
                for i in range(2):
                    sl = slice(2 * i, 2 * i + 2)
                    v.scalar_tensor_tensor(out=work[:, sl, :], in0=out_sb[:, sl, :], scalar=cols1[:, CB_DN:CB_DN + 1],
                                           in1=ps[:, 4 + i, :].rearrange("p (k n) -> p k n", k=2),
                                           op0=ALU.mult, op1=ALU.mult)
                    dve.drain()
                    v.tensor_tensor(work[:, sl, :], work[:, sl, :], z_act[:, sl, :], ALU.mult).then_inc(y_made, 1)
                for i in range(2):
                    y_rest(call_y(l, i + 1), work, i)
                chunk_done(n0 + 22)
                for i in range(4):
                    last = v.tensor_tensor(merged[:, 2 * i:2 * i + 2, :], gate[:, 2 * i:2 * i + 2, :],
                                           ps[:, 4 + i, :].rearrange("p (k n) -> p k n", k=2), ALU.mult)
                last.then_inc(branch_free, 1)
                ahead(n0 + 26)
                for j in range(TAPS - 1, -1, -1):
                    sh = TAPS - 1 - j
                    for t in (0, 1):
                        wcol = cols3[:, 4 * j + t:4 * j + t + 1]
                        if sh == 0:
                            v.tensor_scalar(conv[:, t, :], glu[:, t, :], wcol, cols1[:, CB_DW + t:CB_DW + t + 1],
                                            ALU.mult, ALU.add)
                        else:
                            v.scalar_tensor_tensor(out=conv[:, t, sh:T], in0=glu[:, t, 0:T - sh], scalar=wcol,
                                                   in1=conv[:, t, sh:T], op0=ALU.mult, op1=ALU.add)
                    dve.drain()
                    if sh % 8 == 7:
                        ahead(n0 + 27 + sh // 8)
                dve.drain().then_inc(cv_dve, 1)
                ahead(n0 + 29)
                dve.wait_ge(hd_stats, call_h(l, 2) + 1)
                mean_moments(3, 512, B_EPS, hd_moment)
                dve.wait_ge(hd_rstd, call_h(l, 2) + 1)
                mean_scales()
                make_diag(4, hd_diag)
                dve.wait_ge(hd_rows, call_h(l, 2) + 1)
                v.tensor_tensor(conv[:], conv[:], bc(ps[:, 3, 0:T].unsqueeze(1), (P, 4, T)), ALU.mult)
                dve.drain()
                v.tensor_tensor(conv[:], conv[:], bc(ps[:, 3, T:2 * T].unsqueeze(1), (P, 4, T)), ALU.add)\
                    .then_inc(cv_scaled, 1)
                for i in range(2):
                    y_rest(call_y(l, 3 + i), work, 2 + i)
                ahead(n0 + 30)
                chunk_done(n0 + 28)
                for m in range(KT):
                    v.scalar_tensor_tensor(out=gate[:, m, :], in0=acc(m), scalar=cols1[:, CB_PW2 + m:CB_PW2 + m + 1],
                                           in1=gate[:, m, :], op0=ALU.add, op1=ALU.mult)
                dve.drain()
                v.tensor_tensor(merged[:], merged[:], gate[:], ALU.add).then_inc(branch_free, 1)
                ahead(n0 + 32)
                dve.wait_ge(hd_stats, call_h(l, 3) + 1)
                v.tensor_scalar(moment[:, 0:2], ps[:, 3, 0:2], 1.0 / 384, B_EPS, ALU.mult, ALU.add)
                v.tensor_scalar(moment[:, 2:4], ps[:, 3, 2:4], 1.0 / 256, B_EPS, ALU.mult, ALU.add).then_inc(hd_moment, 1)
                dve.wait_ge(hd_rstd, call_h(l, 3) + 1)
                make_diag(4, hd_diag)
                ahead(n0 + 34)
                dve.wait_ge(hd_rows, call_h(l, 3) + 1)
                for i in range(5):
                    r = 0 if i < 3 else T
                    last = v.scalar_tensor_tensor(out=low[:, i, :], in0=low[:, i, :], scalar=cols1[:, CB_QN + i:CB_QN + i + 1],
                                                  in1=ps[:, 3, r:r + T], op0=ALU.mult, op1=ALU.mult)
                last.then_inc(hd_scaled, 1)
                ahead(n0 + 35)
                dve.wait_ge(rot_mm, l + 1)
                v.tensor_tensor(rot_q[:], ps[0:64, 4:6, :].rearrange("p b (k n) -> p (b k) n", k=2),
                                bc(sin_t[:].unsqueeze(1), (64, HEADS, T)), ALU.mult)
                v.tensor_tensor(rot_k, ps[0:64, 3, 0:T], sin_t[:], ALU.mult)
                v.tensor_tensor(q_rope[:], q_rope[:], bc(cos_t[:].unsqueeze(1), (64, HEADS, T)), ALU.mult)
                v.tensor_tensor(k_rope[:], k_rope[:], cos_t[:], ALU.mult)
                dve.drain()
                v.tensor_tensor(q_rope[:], q_rope[:], rot_q[:], ALU.add)
                v.tensor_tensor(k_rope[:], k_rope[:], rot_k, ALU.add).then_inc(rope_done, 1)
                attention(l * 8 + 8, 1, 192 ** -0.5)
                for i in range(2):
                    y_rest(call_y(l, 5 + i), work, i)
                chunk_done(n0 + 34)
                for i in range(4):
                    sl = slice(2 * i, 2 * i + 2)
                    v.tensor_tensor(gate[:, sl, :], gate[:, sl, :], ps[:, 4 + i, :].rearrange("p (k n) -> p k n", k=2), ALU.mult)
                dve.drain()
                for i in range(4):
                    sl = slice(2 * i, 2 * i + 2)
                    v.tensor_tensor(merged[:, sl, :], merged[:, sl, :], gate[:, sl, :], ALU.add).then_inc(y_made, 1)
                for i in range(4):
                    y_rest(call_y(l, 7 + i), merged, i)
                residual_chunks(n0 + 35, lambda m: v.scalar_tensor_tensor(
                    out=x[:, m, :], in0=x[:, m, :], scalar=ALPHA, in1=acc(m), op0=ALU.mult, op1=ALU.add)
                    .then_inc(x_new, 1))

            with dve.Fori(0, 2) as l:
                at.turns = l * LAYER_TURNS
                at.n = B0
                limit[0] = B0 + B_LAYER_CH
                col = lambda c0: (lambda k: cols1[:, c0 + k:c0 + k + 1])
                ffn(B0, l * 2 + 4)
                dve.wait_ge(lay_turned, l + 1)
                v.tensor_copy(cols1[:], ps[:, 2, 0:106])
                v.tensor_copy(cols2[:], ps[:, 2, 128:176])
                v.tensor_copy(cols3[:], ps[:, 2, 256:380])
                dve.drain().then_inc(lay_cols, 1)
                residual_b(2 * ALPHA)
                norm_b(call_n(l, 0), col(LN_G[0]), 4 * B_EPS)
                x_lo_parts(call_x(l, 0), x)
                ahead(B_MIX + 3)
                mix_b(l)
                norm_b(call_n(l, 1), col(LN_G[1]), B_EPS)
                x_lo_parts(call_x(l, 1), x)
                ffn(B_FFN[1], l * 2 + 5)
                residual_b(2 * ALPHA)
                norm_b(call_n(l, 2), col(LN_G[2]), 4 * B_EPS)
                x_lo_parts(call_x(l, 2), x)


_OUT = ("out_0_dram", (1, 256, 1024))


def kernel(**inputs):
    import numpy as _np
    import concourse.bacc as _bacc
    from concourse import mybir as _mybir
    from concourse.bass_utils import run_bass_kernel_spmd as _run

    nc = _bacc.Bacc("TRN2", target_bir_lowering=False, num_devices=1)
    arrays, args = {}, {}
    for name in inputs:
        v = _np.ascontiguousarray(inputs[name])
        arrays[f"in_{name}_dram"] = v
        args[name] = nc.dram_tensor(f"in_{name}_dram", v.shape, _mybir.dt.from_np(v.dtype), kind="ExternalInput").ap()
    out = nc.dram_tensor(_OUT[0], _OUT[1], _mybir.dt.float32, kind="ExternalOutput").ap()
    block_kernel(nc, args, out)
    r = _run(nc, [arrays], core_ids=[0])
    return r.results[0][_OUT[0]]
```

```python
import math
from contextlib import ExitStack

import concourse.bass as bass
from concourse import mybir

F32 = mybir.dt.float32
F32R = mybir.dt.float32r
BF16 = mybir.dt.bfloat16
I32 = mybir.dt.int32
ALU = mybir.AluOpType
ACT = mybir.ActivationFunctionType
AX = mybir.AxisListType.X
ds = bass.ds

P = 128
T = 256
TT = T // P
D = 1024
KT = D // P
DFF = 2816
PAIRS = DFF // 256
RING = 3
CH = 2048
HEADS = 4
QK_DIM = 64
A_EPS = 1e-6
B_EPS = 1e-5
LAM_INIT = 0.8 - 0.6 * math.exp(0.0)
WINDOWS = (2, 4, 8, 16)
ALPHA = (2 * 2) ** 0.25
NEG = -1e30

FFN_CH = 3 * PAIRS
A0_CH = 8 + 4
A1_CH = 12 + 4
C_AB, C_GLU, C_CQ, C_KR, C_GATE = 2048, 2056, 3080, 3720, 3784
B_LOW = 5
B_CH = 8 + 4 + B_LOW + 12 + 2 + 2 + 2 + 4
A_CHUNKS = 4 * FFN_CH + A0_CH + A1_CH
B_LAYER_CH = 2 * FFN_CH + B_CH
assert B_LAYER_CH % RING == 0
LAYER_TURNS = B_LAYER_CH // RING
EARLY = 2
ADA_SLOTS = 6
LEVELS = 7
HALVES = 2 * (LEVELS - 1)
TAPS = 31
POOL_LO = 5
MIX_MEM = 12288


def block_kernel(nc, a, out):
    keep = ExitStack()
    with keep:
        def sb(name, shape, dt=F32):
            return keep.enter_context(nc.sbuf_tensor(name, shape, dt))

        def sem(name):
            return keep.enter_context(nc.semaphore(name))

        raw = [sb(f"raw{i}", [P, CH]) for i in range(RING)]
        w_hi = [sb(f"w_hi{i}", [P, CH], F32R) for i in range(RING)]
        w_lo = [sb(f"w_lo{i}", [P, CH], F32R) for i in range(RING)]
        x = sb("x", [P, KT, T])
        x_hi = sb("x_hi", [P, KT, T], F32R)
        x_lo = sb("x_lo", [P, KT, T], F32R)
        y_hi = sb("y_hi", [P, KT, T], F32R)
        y_lo = sb("y_lo", [P, KT, T], F32R)
        work = sb("work", [P, KT, T])
        silu_g = sb("silu_g", [P, 2 * T])
        hid = sb("hid", [P, 2 * T])
        hid_hi = sb("hid_hi", [P, 2, T], F32R)
        hid_lo = sb("hid_lo", [P, 2, T], F32R)
        ident = sb("ident", [P, P])
        ones = sb("ones", [P, P])
        zeros = sb("zeros", [P, 512], BF16)
        diag = sb("diag", [P, 16, P])
        moment = sb("moment", [P, 32])
        rstd = sb("rstd", [P, 32])
        half_neg = sb("half_neg", [P, 32])
        ident_b = sb("ident_b", [P, P], BF16)
        cmask_b = sb("cmask_b", [P, P], BF16)
        small = sb("small", [P, 16])
        spare = sb("spare", [P, 2, 2, T])
        probs = sb("probs", [P, 2, 2, T])
        weights = sb("weights", [P, T])
        turned = sb("turned", [P, 2, P])
        sums = sb("sums", [P, 8, 2])
        negmax = sb("negmax", [P, 8, 2])
        recips = sb("recips", [P, 8, 2])
        out_sb = sb("out_sb", [P, HEADS, T])
        mix_mem = sb("mix_mem", [P, MIX_MEM])
        levels = sb("levels", [P, P])
        tri = sb("tri", [P, P])
        rot = sb("rot", [64, P])
        inv_freq = sb("inv_freq", [64, 3])
        cos_t = sb("cos_t", [64, T])
        sin_t = sb("sin_t", [64, T])
        cols1 = sb("cols1", [P, 106])
        cols2 = sb("cols2", [P, 48])
        cols3 = sb("cols3", [P, 124])
        head_par = sb("head_par", [P, 2, 4])
        ab = sb("ab", [P, TT, 8])
        gl = sb("gl", [P, 12, 8])
        gcol = sb("gcol", [P, 8])

        def shaped(ap, shape):
            names = " ".join(f"d{i}" for i in range(len(shape)))
            sizes = {f"d{i}": n for i, n in enumerate(shape[:-1])}
            return ap if len(shape) == 1 else ap.rearrange(f"p ({names}) -> p {names}", **sizes)

        def flat(t):
            names = " ".join(f"d{i}" for i in range(len(t.shape) - 1))
            return t[:].rearrange(f"p {names} -> p ({names})") if len(t.shape) > 2 else t[:]

        class Carve:

            def __init__(self, start=0):
                self.at = start

            def __call__(self, *shape, parts=P):
                n = math.prod(shape)
                assert self.at + n <= MIX_MEM
                self.at += n
                return shaped(mix_mem[0:parts, self.at - n:self.at], shape)

        carve = Carve()
        ada_raw = [flat(spare), flat(probs), flat(out_sb)] + [carve(D) for _ in range(3)]
        ada_acc = carve(6, D)
        inv_count = carve(4, T)
        pool_w = carve(4, P)
        vpad = carve(2, T + 2)
        a_rows = carve(P, parts=85)
        b_rows = carve(2, P, parts=72)
        a_cols = carve(85)
        b_cols = carve(2, 72)
        c_act = carve(KT)
        mod = carve(18, KT)
        norm_col = carve(6, KT)
        gate_col = carve(6, KT)
        half_sel = carve(2)
        qk_gain = carve(2)
        lam_in = carve(4, parts=QK_DIM)
        lam_prod = carve(2, parts=QK_DIM)
        lam = carve(4)
        sub_gain = carve(1)
        carve = Carve()
        qk = carve(8, T)
        v_tok = carve(TT, 512)
        u_in = carve(4, T)
        win = [carve(4, T) for _ in range(2)]
        count_i = carve(T).bitcast(I32)
        c_sb = carve(2, T)
        cmask = weights[:, 0:P]
        x_rows = shaped(flat(diag), (TT, D))
        x_sum = shaped(flat(diag)[:, 8 * P:8 * P + 2 * T], (2, T))
        bc_half = diag

        carve = Carve()
        bmat = carve(8, P)
        qkv = carve(12, T)
        emat = carve(8, P)
        tmat = carve(8, P)
        amat = carve(8, P)
        qk_dec = carve(8, P)
        q_dec = carve(HEADS, P)
        low = carve(5, T)
        k_rope = carve(T, parts=64)
        gate = carve(KT, T)
        stage, sig, ptmp = silu_g, shaped(hid[:], (2, T)), shaped(silu_g[:], (2, T))
        z_act, glu = shaped(flat(spare), (4, T)), shaped(flat(probs), (4, T))
        conv = shaped(flat(diag)[:, 8 * P:16 * P], (4, T))
        carve = Carve(8 * P)
        dmat = carve(8, P)
        k_tok = carve(2, 512)
        v_beta = carve(2, 512)
        merged = shaped(mix_mem[:, 0:KT * T], (KT, T))
        u_sb = amat
        wt, s_state = tmat[:, 0:HEADS, :], tmat[:, HEADS:8, :]
        carve = Carve(16 * P)
        uq = carve(3, 768)
        ukv = carve(2, 1024)
        k_nope = carve(HEADS, T)
        v_mla = carve(TT, 512)
        q_nope = work[:, 4:8, :]
        q_rope = shaped(flat(out_sb)[0:64, :], (HEADS, T))
        rot_q = shaped(flat(spare)[0:64, :], (HEADS, T))
        rot_k = weights[0:64, :]
        par = flat(out_sb)
        w_kr = shaped(par[:, 0:512], (KT, 64))
        w_ab = shaped(par[:, 512:576], (KT, 8))
        rows1, rows2, rows3 = par[0:106, 576:704], par[0:48, 704:832], par[0:124, 832:960]
        y_rows = shaped(flat(mix_mem)[:, MIX_MEM - TT * D:MIX_MEM], (TT, D))
        level_tmp = weights[:, 0:P]
        count_b = weights[0:64, P:P + 1].bitcast(I32)
        pos_i, angle, turns_f = flat(spare)[0:64, 0:T].bitcast(I32), probs[0:64, 0, 0, :], probs[0:64, 0, 1, :]
        rope_k = probs[0:64, 1, 0, :].bitcast(I32)

        ps = keep.enter_context(nc.psum_tensor("ps", [P, 8, 512], F32))

        landed = [sem(f"landed{i}") for i in range(RING)]
        hi_ready = sem("hi_ready")
        lo_ready = sem("lo_ready")
        chunk_used = sem("chunk_used")
        ada_landed = [sem(f"ada_landed{i}") for i in range(ADA_SLOTS)]
        ada_used = sem("ada_used")
        mod_summed = sem("mod_summed")
        params_in = sem("params_in")
        params2_in = sem("params2_in")
        lam_exp = sem("lam_exp")
        cv_scaled = sem("cv_scaled")
        x_in = sem("x_in")
        const_ready = sem("const_ready")
        const_dve = sem("const_dve")
        rows_turned = sem("rows_turned")
        cols_ready = sem("cols_ready")
        c_ready = sem("c_ready")
        x_turned = sem("x_turned")
        x_new = sem("x_new")
        squares = sem("squares")
        squares_added = sem("squares_added")
        x_added = sem("x_added")
        stats = sem("stats")
        moments = sem("moments")
        rstd_ready = sem("rstd_ready")
        diag_ready = sem("diag_ready")
        rows_ready = sem("rows_ready")
        scaled = sem("scaled")
        x_hi_ready = sem("x_hi_ready")
        x_lo_ready = sem("x_lo_ready")
        x_lo_last = sem("x_lo_last")
        gate_read = sem("gate_read")
        acc_ready = sem("acc_ready")
        hid_made = sem("hid_made")
        hid_hi_ready = sem("hid_hi_ready")
        hid_lo_ready = sem("hid_lo_ready")
        evac = sem("evac")
        y_made = sem("y_made")
        y_hi_ready = sem("y_hi_ready")
        y_lo_ready = sem("y_lo_ready")
        at_scores = sem("at_scores")
        at_max = sem("at_max")
        at_probs = sem("at_probs")
        at_weights = sem("at_weights")
        at_turned = sem("at_turned")
        at_copied = sem("at_copied")
        at_out = sem("at_out")
        hd_sq = sem("hd_sq")
        hd_stats = sem("hd_stats")
        hd_moment = sem("hd_moment")
        hd_rstd = sem("hd_rstd")
        hd_diag = sem("hd_diag")
        hd_rows = sem("hd_rows")
        hd_scaled = sem("hd_scaled")
        pooled = sem("pooled")
        pool_mm = sem("pool_mm")
        lam_done = sem("lam_done")
        lam_mm = sem("lam_mm")
        c_copied = sem("c_copied")
        cx_read = sem("cx_read")
        lay_rows = sem("lay_rows")
        lay_small = sem("lay_small")
        lay_turned = sem("lay_turned")
        lay_cols = sem("lay_cols")
        ab_mm = sem("ab_mm")
        ab_copied = sem("ab_copied")
        ab_in = sem("ab_in")
        ab_exp = sem("ab_exp")
        g_ready = sem("g_ready")
        conv_done = sem("conv_done")
        qkv_act = sem("qkv_act")
        glu_ready = sem("glu_ready")
        qk_hat = sem("qk_hat")
        g_mm = sem("g_mm")
        dec_in = sem("dec_in")
        dec_exp = sem("dec_exp")
        kk_mm = sem("kk_mm")
        tok_mm = sem("tok_mm")
        tok_done = sem("tok_done")
        a_ready = sem("a_ready")
        b_ready = sem("b_ready")
        t_mm = sem("t_mm")
        t_copied = sem("t_copied")
        e_first = sem("e_first")
        d_mm = sem("d_mm")
        d_copied = sem("d_copied")
        e_mm = sem("e_mm")
        e_copied = sem("e_copied")
        u_mm = sem("u_mm")
        u_copied = sem("u_copied")
        s_mm = sem("s_mm")
        s_ready = sem("s_ready")
        ws_mm = sem("ws_mm")
        v_new = sem("v_new")
        o_mm = sem("o_mm")
        branch_free = sem("branch_free")
        cv_pool = sem("cv_pool")
        cv_dve = sem("cv_dve")
        kr_mm = sem("kr_mm")
        mla_w = sem("mla_w")
        mla_mm = sem("mla_mm")
        mla_sb = sem("mla_sb")
        rot_mm = sem("rot_mm")
        rope_done = sem("rope_done")
        rope_in = sem("rope_in")
        rope_sin = sem("rope_sin")
        rope_pow = sem("rope_pow")
        rope_conv = sem("rope_conv")
        out_turned = sem("out_turned")
        out_copied = sem("out_copied")
        stored = sem("stored")

        A_FFN = (0, FFN_CH + A0_CH, 2 * FFN_CH + A0_CH, 3 * FFN_CH + A0_CH + A1_CH)
        A_MIX = (FFN_CH, 3 * FFN_CH + A0_CH)
        B0 = A_CHUNKS
        B_FFN = (B0, B0 + FFN_CH + B_CH)
        B_MIX = B0 + FFN_CH

        def chunk_cols(n):
            return 1024 if B_MIX + 12 <= n < B_MIX + 12 + B_LOW else CH

        class Place:

            def __init__(self):
                self.n = 0
                self.turns = 0

            def count(self, back=0):
                return 3 * self.turns + (self.n - back)

            def slot(self):
                return self.n % RING

            def turn(self):
                return self.turns + self.n // RING

        def bc(ap, shape):
            return ap.broadcast_to(list(shape))

        def acc(m, n=1):
            return ps[:, 4 + m // 2, T * (m % 2):T * (m % 2 + n)]

        def group_of(f):
            return f + 1 if f < 3 else None

        GROUPS = ((0, 2, 0, None), (2, 6, 16, (3, 3, 3, 3, 2, 2)), (8, 6, 64, (11, 11, 11, 11, 10, 10)),
                  (14, 4, 112, (19, 19, 19, 19)))

        def part_of(width, part):
            return (range(2 * part, 2 * part + 2) if width == 6 else (range(0, 2), range(2, 3), range(3, 4))[part])

        def call_x(l, j):
            return 7 + 3 * l + j

        def call_n(l, j):
            return 6 + 3 * l + j

        def call_h(l, j):
            return 2 + 4 * l + j

        def sq_at(l, j):
            return 3 * l + (2 + j)

        def pos(g):
            return g if g < 17 else g + 2 * ((g - 17) // 4)

        def call_y(l, j):
            return 8 + 10 * l + j

        def call_e(l, j):
            return 8 + 29 * l + j

        LN_G, LN_B = (0, 16, 32), (8, 24, 40)
        CB_GATE, CB_GLU, CB_DW, CB_LNG, CB_LNB, CB_PW2, CB_QN, CB_KVN, CB_DN = 48, 72, 80, 84, 88, 92, 100, 103, 105

        block = keep.enter_context(nc.Block())

        @block.sync
        def _(sp):
            at = Place()

            def load(src, kt, wait=True):
                if wait and at.n >= RING:
                    sp.wait_ge(lo_ready, at.count(RING - 1))
                s = at.slot()
                n = src.shape[-1]
                dst = raw[s][:, 0:kt * n].rearrange("p (k n) -> p k n", k=kt)
                sp.dma_start(dst, src).then_inc(landed[s], 16)
                at.n += 1

            def cols_of(w, start, n=256):
                return w.rearrange("(k p) n -> p k n", p=P)[:, :, start:start + n] if isinstance(start, int) \
                    else w.rearrange("(k p) n -> p k n", p=P)[:, :, ds(start, n)]

            def rows_of(w, i):
                return w.rearrange("(f k p) n -> p f k n", p=P, k=2)[:, i, :, :] if isinstance(i, int) \
                    else w.rearrange("(f k p) n -> p (f k) n", p=P, k=2)[:, ds(i * 2, 2), :]

            def ffn_start(wg, wu, late=False):
                load(cols_of(wg, 0), KT)
                if late:
                    sp.wait_ge(ada_used, 14)
                load(cols_of(wu, 0), KT)

            def ffn_rest(wg, wu, wd):
                def pair(i):
                    load(cols_of(wg, i * 256 + 256), KT)
                    load(cols_of(wu, i * 256 + 256), KT)
                    load(rows_of(wd, i), 2)

                base = at.turns
                load(cols_of(wg, 256), KT)
                sp.wait_ge(lo_ready, at.count(RING - 2))
                load(cols_of(wu, 256), KT, wait=False)
                load(rows_of(wd, 0), 2, wait=False)
                with sp.Fori(1, PAIRS - 1) as i:
                    at.turns = base + i - 1
                    pair(i)
                    at.n -= 3
                at.turns = base
                at.n += 3 * (PAIRS - 2)
                load(rows_of(wd, PAIRS - 1), 2)

            def mix_a0():
                for j in range(8):
                    load(cols_of(a["w_in_ab"][0], 256 * j), KT)
                for j in range(4):
                    load(cols_of(a["w_out_ab"][0], 256 * j), KT)

            def mix_a1():
                w = a["w_in_c"][0]
                for part in (1, 2, 0):
                    load(cols_of(w, part * D), KT)
                base = at.turns
                with sp.Fori(0, 3) as j:
                    at.turns = base + j
                    for part in (1, 2, 0):
                        load(cols_of(w, j * 256 + (part * D + 256)), KT)
                    at.n -= 3
                at.turns = base
                at.n += 9
                for j in range(4):
                    load(cols_of(a["w_out_c"][0], 256 * j), KT)

            def lay(name, l):
                w = a[name]
                return w[ds(l, 1)].rearrange("o k n -> (o k) n")

            for t in range(TT):
                sp.dma_start(x_rows[:, t, :], a["x"][0, t * P:(t + 1) * P, :]).then_inc(x_in, 16)
            rows = [(77, 85, a["c"].rearrange("o (t p) -> (o t) p", p=P)),
                    (0, 48, a["norm_g"].rearrange("l j (t p) -> (l j t) p", p=P)),
                    (48, 49, a["subln_g"]),
                    (49, 53, a["pool_scale"].rearrange("o (t p) -> (o t) p", p=P)),
                    (53, 77, a["conv_w"].rearrange("o j (t p) -> (o j t) p", p=P))]
            for lo_, hi_, src in rows:
                sp.dma_start(a_rows[lo_:hi_, :], src).then_inc(params_in, 16)
            sp.dma_start(b_rows[:, :, :], a["b_ada"].rearrange("l (r p) -> r l p", p=P)).then_inc(params_in, 16)

            def ffn_a(l, i, late=False):
                ffn_start(a["ffn_wg"][l, i], a["ffn_wu"][l, i], late)
                ffn_rest(a["ffn_wg"][l, i], a["ffn_wu"][l, i], a["ffn_wd"][l, i])

            ffn_a(0, 0, True)
            mix_a0()
            ffn_a(0, 1)
            ffn_a(1, 0)
            mix_a1()
            ffn_a(1, 1)
            assert at.n == A_CHUNKS
            ffn_start(a["ffn1_w_gate_2"][0], a["ffn1_w_up_2"][0])
            with sp.Fori(0, 2) as l:
                at.turns = l * LAYER_TURNS
                at.n = B0 + EARLY
                ffn_rest(lay("ffn1_w_gate_2", l), lay("ffn1_w_up_2", l), lay("ffn1_w_down_2", l))
                w_in = lay("w_in_2", l)
                for j in range(8):
                    load(cols_of(w_in, 256 * j), KT)
                for j in range(2):
                    load(cols_of(w_in, C_GLU + 256 * j), KT)
                    load(cols_of(w_in, C_GLU + 512 + 256 * j), KT)
                for j in range(B_LOW):
                    load(cols_of(w_in, C_CQ + 128 * j, 128), KT)
                for b, name in enumerate(("dn_w_o_2", "cv_w_pw2_2", "mla_w_o_2")):
                    for j in range(4):
                        load(cols_of(w_in, C_GATE + D * b + 256 * j), KT)
                    for j in range(2):
                        load(cols_of(lay(name, l), 512 * j, 512), 4)
                for j in range(4):
                    load(cols_of(lay("w_out_2", l), 256 * j), KT)
                ffn_start(lay("ffn2_w_gate_2", l), lay("ffn2_w_up_2", l))
                ffn_rest(lay("ffn2_w_gate_2", l), lay("ffn2_w_up_2", l), lay("ffn2_w_down_2", l))
                ffn_start(a["ffn1_w_gate_2"][1], a["ffn1_w_up_2"][1])
                assert at.n == B0 + B_LAYER_CH + EARLY
            for i in range(4):
                t, cols = i % 2, slice(512 * (i // 2), 512 * (i // 2) + 512)
                sp.wait_ge(out_copied, i + 1)
                sp.dma_start(out[0, t * P:(t + 1) * P, cols], y_rows[:, t, cols]).then_inc(stored, 16)
            sp.wait_ge(stored, 16 * 4)

        @block.gpsimd
        def _(pool):
            g = nc.gpsimd

            def select(view, op, fill, base, pattern, mult):
                g.affine_select(out=view, in_=view, compare_op=op, fill=fill, base=base,
                                pattern=pattern, channel_multiplier=mult)

            def ada_unit(grp, k, j, slot):
                l, m = divmod(GROUPS[grp][0] + j, 9)
                w = a["w_ada"][l].rearrange("(k p) n -> p k n", p=P)
                src = w[:, k:k + 1, D * m:D * m + D] if isinstance(k, int) else w[:, ds(k, 1), D * m:D * m + D]
                pool.dma_start(ada_raw[slot].rearrange("p (o n) -> p o n", o=1), src)\
                    .then_inc(ada_landed[slot], 16)

            def power(call, n, ready=moments, done=rstd_ready):
                pool.wait_ge(ready, call + 1)
                g.tensor_tensor(rstd[:, 0:n], moment[:, 0:n], half_neg[:, 0:n], ALU.pow).then_inc(done, 1)

            def norm_power(n):
                power(n, 2)

            g.memset(ident[:], 0.0)
            g.memset(cmask, 0.0)
            g.memset(half_neg[:], -0.5)
            g.memset(half_sel[:], 1.0)
            g.iota(count_i[:], pattern=[[1, T]], base=1, channel_multiplier=0)
            pool.drain()
            select(ident[:], ALU.not_equal, 1.0, 0, [[-1, P]], 1)
            select(cmask, ALU.is_ge, NEG, 0, [[-1, P]], 1)
            select(half_sel[:, 0:1], ALU.is_ge, 0.0, QK_DIM - 1, [[0, 1]], -1)
            select(half_sel[:, 1:2], ALU.is_ge, 0.0, -QK_DIM, [[0, 1]], 1)
            pool.drain().then_inc(const_ready, 1)
            for k in range(KT):
                for j in range(2):
                    u = 2 * k + j
                    if u >= ADA_SLOTS:
                        pool.wait_ge(ada_used, u - ADA_SLOTS + 1)
                    ada_unit(0, k, j, u % ADA_SLOTS)
            norm_power(0)
            for half in range(2):
                for j in range(2):
                    pool.dma_start(qk_gain[64 * half:64 * half + 64, j:j + 1],
                                   a["qk_norm_g"][0, j, :].rearrange("(p o) -> p o", o=1)).then_inc(params2_in, 16)
            for j, name in enumerate(("lambda_q1", "lambda_k1", "lambda_q2", "lambda_k2")):
                pool.dma_start(lam_in[:, j:j + 1], a[name].rearrange("o p -> p o")).then_inc(params2_in, 16)
            pool.dma_start(pool_w[:, :, :], a["pool_w"].rearrange("o g c d -> c (o g) d")).then_inc(params2_in, 16)

            def head_power(call, n):
                power(call, n, hd_moment, hd_rstd)

            def add_x(call):
                pool.wait_ge(x_new, call * 8 + 4)
                g.tensor_tensor(x_sum, x[:, 0:2, :], x[:, 2:4, :], ALU.add)
                pool.drain()
                pool.wait_ge(x_new, call * 8 + 6)
                g.tensor_tensor(x_sum, x_sum, x[:, 4:6, :], ALU.add).then_inc(x_added, 1)

            def x_lo_parts(call, whole):
                for k in range(POOL_LO):
                    pool.wait_ge(x_hi_ready, call * 8 + (k + 1))
                    g.tensor_tensor(x_lo[:, k, :], whole[:, k, :], x_hi[:, k, :].bitcast(F32), ALU.subtract)\
                        .then_inc(x_lo_ready, 1)

            def ada_group(f):
                grp = group_of(f)
                if grp is None:
                    return
                width, unit0 = GROUPS[grp][1], GROUPS[grp][2]
                pool.wait_ge(ada_used, unit0)
                for j in range(width):
                    ada_unit(grp, 0, j, j)
                with pool.Fori(1, KT) as k:
                    for j in range(width):
                        pool.wait_ge(ada_used, k * width + (unit0 + j - width + 1))
                        ada_unit(grp, k, j, j)

            def windows():
                pool.wait_ge(evac, 8)
                for n, width in enumerate(WINDOWS):
                    half = width // 2
                    src = u_in if n == 0 else win[(n + 1) % 2]
                    dst = win[n % 2]
                    g.tensor_tensor(dst[:, n:4, half:T], src[:, n:4, half:T], src[:, n:4, 0:T - half], ALU.add)
                    g.tensor_copy(dst[:, n:4, 0:half], src[:, n:4, 0:half])
                    pool.drain()
                    g.tensor_tensor(inv_count[:, n, :], dst[:, n, :], inv_count[:, n, :], ALU.mult)
                pool.drain()
                last = g.tensor_tensor(inv_count[:], inv_count[:], u_in[:], ALU.subtract)
                last.then_inc(pooled, 1)

            x_lo_parts(0, work)
            ada_group(0)
            norm_power(1)
            x_lo_parts(1, work)
            head_power(0, 32)
            windows()
            head_power(1, 8)
            norm_power(2)
            x_lo_parts(2, work)
            ada_group(1)
            norm_power(3)
            x_lo_parts(3, work)
            ada_group(2)
            norm_power(4)
            x_lo_parts(4, work)
            pool.drain()
            g.memset(levels[:], 0.0)
            g.memset(tri[:], 1.0)
            g.memset(rot[:], 0.0)
            pool.drain()
            select(tri[:], ALU.is_ge, 0.0, 0, [[1, P]], -1)
            select(rot[:, 0:64], ALU.not_equal, -1.0, -32, [[-1, 64]], 1)
            pool.drain()
            select(rot[:, 0:64], ALU.not_equal, 1.0, 32, [[-1, 64]], 1)
            for s in range(LEVELS):
                w = 2 ** s
                v = level_tmp.rearrange("p (b h w) -> p b h w", h=2, w=w)
                g.memset(v[:, :, 0, :], 0.0)
                g.memset(v[:, :, 1, :], s + 1.0)
                pool.drain()
                n = P // (2 * w)
                upper = v[:, :, 1, :]
                select(upper, ALU.is_ge, 0.0, 0, [[-2 * w, n], [0, w]], 1)
                pool.drain()
                select(upper, ALU.is_ge, 0.0, w - 1, [[2 * w, n], [0, w]], -1)
                pool.drain()
                g.tensor_tensor(levels[:], levels[:], level_tmp, ALU.add)
                pool.drain()
            for half in range(2):
                pool.drain()
                g.iota(count_b[32 * half:32 * half + 32, :], pattern=[[0, 1]], base=0, channel_multiplier=1)
            pool.drain()
            g.memset(inv_freq[:, 0:1], 10000.0)
            pool.drain()
            g.tensor_copy(inv_freq[:, 1:2], count_b[:])
            pool.drain()
            g.tensor_scalar(inv_freq[:, 1:2], inv_freq[:, 1:2], -1.0 / 32, None, ALU.mult)
            pool.drain()
            g.tensor_tensor(inv_freq[:, 2:3], inv_freq[:, 0:1], inv_freq[:, 1:2], ALU.pow)
            pool.dma_start(pos_i, bc(a["positions_2"], (64, T))).then_inc(rope_in, 16)
            pool.drain().then_inc(rope_pow, 1)
            norm_power(5)
            x_lo_parts(5, work)
            x_lo_parts(6, x)

            def vec(name, l):
                w = a[name]
                return w[ds(l, 1), :].rearrange("o (r p) -> (o r) p", p=P)

            with pool.Fori(0, 2) as l:
                pool.wait_ge(x_lo_last, l * (3 * (KT - POOL_LO)) + 7 * (KT - POOL_LO))
                for name, r0, n in (("ln1_g_2", 0, 8), ("ln1_b_2", 8, 8), ("ln2_g_2", 16, 8), ("ln2_b_2", 24, 8),
                                    ("ln3_g_2", 32, 8), ("ln3_b_2", 40, 8), ("b_gate_2", CB_GATE, 24),
                                    ("cv_glu_b_2", CB_GLU, 8), ("cv_dw_b_2", CB_DW, 4), ("cv_ln_g_2", CB_LNG, 4),
                                    ("cv_ln_b_2", CB_LNB, 4), ("cv_b_pw2_2", CB_PW2, 8), ("mla_q_norm_w_2", CB_QN, 3),
                                    ("mla_kv_norm_w_2", CB_KVN, 2), ("dn_norm_w_2", CB_DN, 1)):
                    pool.dma_start(rows1[r0:r0 + n, :], vec(name, l)).then_inc(lay_rows, 16)
                pool.dma_start(rows2[:, :], a["dn_conv_w_2"][ds(l, 1)].rearrange("o j (t p) -> (o j t) p", p=P))\
                    .then_inc(lay_rows, 16)
                pool.dma_start(rows3[:, :], a["cv_dw_w_2"][ds(l, 1)].rearrange("o j (t p) -> (o j t) p", p=P))\
                    .then_inc(lay_rows, 16)
                w_in = a["w_in_2"][ds(l, 1)].rearrange("o (k p) n -> p (o k) n", p=P)
                pool.dma_start(w_ab[:, :, :], w_in[:, :, C_AB:C_AB + 8]).then_inc(lay_small, 16)
                pool.dma_start(w_kr[:, :, :], w_in[:, :, C_KR:C_KR + 64]).then_inc(lay_small, 16)
                pool.dma_start(head_par[:, 0, :], bc(a["dn_a_log_2"][ds(l, 1), :], (P, 4))).then_inc(lay_small, 16)
                pool.dma_start(head_par[:, 1, :], bc(a["dn_dt_bias_2"][ds(l, 1), :], (P, 4))).then_inc(lay_small, 16)
                add_x(call_x(l, 0))
                norm_power(call_n(l, 0))
                x_lo_parts(call_x(l, 0), x)
                head_power(call_h(l, 0), 16)
                pool.wait_ge(glu_ready, l * 2 + 2)
                for sh in range(TAPS):
                    j = TAPS - 1 - sh
                    if sh == 23:
                        head_power(call_h(l, 1), 8)
                    for t in (2, 3):
                        wcol = cols3[:, 4 * j + t:4 * j + t + 1]
                        if sh == 0:
                            g.tensor_tensor(conv[:, t, :], glu[:, t, :], bc(wcol, (P, T)), ALU.mult)
                            pool.drain()
                            g.tensor_scalar(conv[:, t, :], conv[:, t, :], cols1[:, CB_DW + t:CB_DW + t + 1], None, ALU.add)
                        else:
                            g.tensor_scalar(ptmp[:, t - 2, 0:T - sh], glu[:, t, 0:T - sh], wcol, None, ALU.mult)
                    pool.drain()
                    if sh:
                        for t in (2, 3):
                            g.tensor_tensor(conv[:, t, sh:T], conv[:, t, sh:T], ptmp[:, t - 2, 0:T - sh], ALU.add)
                        pool.drain()
                pool.drain().then_inc(cv_pool, 1)
                pool.wait_ge(branch_free, l * 2 + 1)
                pool.dma_start(uq[:, :, :], a["mla_w_uq_2"][ds(l, 1)].rearrange("o (k p) n -> p (o k) n", p=P))\
                    .then_inc(mla_w, 16)
                pool.dma_start(ukv[:, :, :], a["mla_w_ukv_2"][ds(l, 1)].rearrange("o (k p) n -> p (o k) n", p=P))\
                    .then_inc(mla_w, 16)
                head_power(call_h(l, 2), 2)
                head_power(call_h(l, 3), 4)
                add_x(call_x(l, 1))
                norm_power(call_n(l, 1))
                x_lo_parts(call_x(l, 1), x)
                add_x(call_x(l, 2))
                norm_power(call_n(l, 2))
                x_lo_parts(call_x(l, 2), x)

        @block.tensor
        def _(pe):
            at = Place()

            def take():
                pe.wait_ge(lo_ready, at.count() + 1)
                return at.slot()

            def used(last):
                last.then_inc(chunk_used, 1)
                at.n += 1

            def split_mm(dst, wh, wl, vh, vl, start, stop_):
                pe.matmul(dst, wh, vh, start=start, stop=False, skip_group_check=True)
                pe.matmul(dst, wh, vl, start=False, stop=False, skip_group_check=True)
                return pe.matmul(dst, wl, vh, start=False, stop=stop_, skip_group_check=True)

            def cols_chunk(bank, vh, vl, kt=KT, n=256, waits=None, order=None, first=0):
                s = take()
                h = w_hi[s][:, 0:kt * n].rearrange("p (k n) -> p k n", k=kt)
                lw = w_lo[s][:, 0:kt * n].rearrange("p (k n) -> p k n", k=kt)
                order = order or list(range(kt))
                for m in range(n // P):
                    dst = ps[:, bank + m // 2, T * (m % 2):T * (m % 2) + T]
                    for i, k in enumerate(order):
                        if m == 0 and waits is not None:
                            waits(i)
                        last = split_mm(dst, h[:, k, m * P:m * P + P], lw[:, k, m * P:m * P + P],
                                        vh[:, first + k, :], vl[:, first + k, :], i == 0, i == kt - 1)
                used(last)

            def x_waits(call):
                return lambda k: pe.wait_ge(x_lo_ready, call * POOL_LO + (k + 1)) if k < POOL_LO \
                    else pe.wait_ge(x_lo_last, call * (KT - POOL_LO) + (k - POOL_LO + 1))

            def norm_stats(n, call, with_mean):
                started = [False]

                def column(c, tile, t, stop_=False):
                    last = pe.matmul(ps[:, 2, c + t:c + t + 1], tile[:, t * P:t * P + P], ones[:, 0:1],
                                     start=not started[0], stop=stop_, skip_group_check=True)
                    started[0] = True
                    return last

                if with_mean:
                    pe.wait_ge(x_added, call - 6)
                    for i in range(2):
                        for t in range(TT):
                            column(2, x_sum[:, i, :], t)
                    pe.wait_ge(x_new, call * 8 + 8)
                    for m in (6, 7):
                        for t in range(TT):
                            column(2, x[:, m, :], t, m == 7)
                pe.wait_ge(squares_added, n + 1)
                for m in (0, 1):
                    for t in range(TT):
                        column(0, work[:, m, :], t)
                pe.wait_ge(squares, n * 8 + 8)
                for m in (6, 7):
                    for t in range(TT):
                        last = column(0, work[:, m, :], t, m == 7)
                last.then_inc(stats, 1)

            def norm_rows(n, with_mean):
                pe.wait_ge(diag_ready, n + 1)
                w = (2 if with_mean else 1) * TT
                pe.matmul(ps[:, 3, 0:w * P], ones[:], diag[:, 0:w, :], start=True, stop=True).then_inc(rows_ready, 1)

            def clear_sums():
                for b in range(4, 8):
                    pe.matmul(ps[:, b, :], zeros[:, 0:P], zeros[:], start=True, stop=True, skip_group_check=True)

            def down_chunk(call, i, last_pair=False):
                s = take()
                pe.wait_ge(hid_lo_ready, call * PAIRS + i + 1)
                h = w_hi[s][:].rearrange("p (k n) -> p k n", k=2)
                lw = w_lo[s][:].rearrange("p (k n) -> p k n", k=2)
                for m in range(KT):
                    for k in range(2):
                        last = split_mm(acc(m), h[:, k, m * P:m * P + P], lw[:, k, m * P:m * P + P],
                                        hid_hi[:, k, :], hid_lo[:, k, :], False, False)
                    if last_pair and m in (1, 3, 5):
                        last.then_inc(acc_ready, 1)
                used(last)

            def ffn(f, call, before_last=None):
                cols_chunk(0, x_hi, x_lo, waits=x_waits(call))
                cols_chunk(1, x_hi, x_lo)
                base = at.turns
                with pe.Fori(0, PAIRS - 1) as i:
                    at.turns = base + i
                    pe.wait_ge(gate_read, f * PAIRS + i + 1)
                    cols_chunk(0, x_hi, x_lo)
                    pe.wait_ge(hid_made, f * PAIRS + i + 1)
                    cols_chunk(1, x_hi, x_lo)
                    down_chunk(f, i)
                    at.n -= 3
                at.turns = base
                at.n += 3 * (PAIRS - 1)
                pe.wait_ge(hid_made, f * PAIRS + PAIRS)
                if before_last:
                    before_last()
                down_chunk(f, PAIRS - 1, True)

            def mod_sums(grp):
                width, unit0 = GROUPS[grp][1], GROUPS[grp][2]
                pe.wait_ge(ada_used, unit0 + 8 * width)
                for j in range(width):
                    for t in range(KT):
                        last = pe.matmul(ps[:, 1, j * KT + t:j * KT + t + 1], ada_acc[:, j, t * P:t * P + P],
                                         ones[:, 0:1], start=True, stop=True)
                last.then_inc(mod_summed, 1)

            def head_sums(tiles, src, bank, ready, value):
                pe.wait_ge(ready, value)
                for i in range(tiles):
                    for t in range(TT):
                        c = i * TT + t
                        last = pe.matmul(ps[:, bank, c:c + 1], src[:, i, t * P:t * P + P], ones[:, 0:1],
                                         start=True, stop=True)
                last.then_inc(hd_stats, 1)

            def head_rows(call, n, bank):
                pe.wait_ge(hd_diag, call + 1)
                for i in range(0, n, 4):
                    w = min(4, n - i)
                    last = pe.matmul(ps[:, bank + i // 4, 0:w * P], ones[:], diag[:, i:i + w, :], start=True, stop=True)
                last.then_inc(hd_rows, 1)

            def attention(item0, heads, score, v_tiles):
                def scores(it):
                    if it >= 2:
                        pe.wait_ge(at_probs, item0 + (it - 1))
                    b = it // HEADS
                    score(it % HEADS, b, 4 + 2 * (it % 2))
                    for j in range(heads):
                        last = pe.matmul(ps[:, 4 + 2 * (it % 2) + j, P * b:P * b + P], ident_b[:], cmask_b[:],
                                         start=False, stop=True, skip_group_check=True)
                    last.then_inc(at_scores, 1)

                def turn(it):
                    pe.wait_ge(at_weights, item0 + (it + 1))
                    for kt in range(it // HEADS + 1):
                        last = pe.transpose(ps[:, 2 + it % 2, kt * P:kt * P + P], weights[:, kt * P:kt * P + P], ident[:])
                    last.then_inc(at_turned, 1)

                def values(it):
                    h, b = it % HEADS, it // HEADS
                    pe.wait_ge(at_copied, item0 + (it + 1))
                    dst = ps[:, h // 2, T * (h % 2) + P * b:T * (h % 2) + P * b + P]
                    for kt in range(b + 1):
                        last = pe.matmul(dst, v_tiles[:, kt, h * P:h * P + P], turned[:, kt, :],
                                         start=(kt == 0), stop=(kt == b))
                    last.then_inc(at_out, 1)

                scores(0)
                scores(1)
                for it in range(8):
                    turn(it)
                    if it + 2 < 8:
                        scores(it + 2)
                    values(it)

            pe.wait_ge(const_ready, 1)
            pe.wait_ge(const_dve, 1)
            pe.wait_ge(params_in, 6 * 16)
            pe.transpose(ps[:, 0, 0:85], a_rows[:], ident[0:85, 0:85])
            pe.transpose(ps[:, 0, 128:200], b_rows[:, 0, :], ident[0:72, 0:72])
            pe.transpose(ps[:, 0, 256:328], b_rows[:, 1, :], ident[0:72, 0:72]).then_inc(rows_turned, 1)
            pe.wait_ge(x_in, 16 * TT)
            for m in range(KT):
                for t in range(TT):
                    last = pe.transpose(acc(m)[:, t * P:t * P + P], x_rows[:, t, m * P:m * P + P], ident[:])
                last.then_inc(x_turned, 1)
            norm_stats(0, 0, False)
            clear_sums()
            norm_rows(0, False)
            mod_sums(0)
            ffn(0, 0, lambda: mod_sums(1))
            norm_stats(1, 1, False)
            norm_rows(1, False)

            def mix_a0():
                for j in range(8):
                    bank = j % 3
                    if j >= 3:
                        pe.wait_ge(evac, j - 2)
                    if j in (4, 5):
                        s = take()
                        h = w_hi[s][:].rearrange("p (k n) -> p k n", k=KT)
                        lw = w_lo[s][:].rearrange("p (k n) -> p k n", k=KT)
                        for t in range(TT):
                            dst = ps[:, bank, T * t:T * t + T]
                            for k in range(KT):
                                xs = slice(t * P, t * P + P)
                                last = split_mm(dst, x_hi[:, k, xs], x_lo[:, k, xs], h[:, k, :], lw[:, k, :],
                                                k == 0, k == KT - 1)
                        used(last)
                    else:
                        cols_chunk(bank, x_hi, x_lo, waits=x_waits(1) if j == 0 else None)
                    if j == 5:
                        pe.wait_ge(evac, 4)
                        for i in range(8):
                            for t in range(TT):
                                c = (i * TT + t) * 2
                                last = pe.matmul(ps[:, 4, c:c + 2], work[:, i, t * P:t * P + P], half_sel[:],
                                                 start=True, stop=True)
                        last.then_inc(hd_stats, 1)
                pe.wait_ge(hd_diag, 1)
                for i in range(16):
                    last = pe.matmul(ps[:, 4 + i // 4, (i % 4) * P:(i % 4) * P + P], bc_half[:, i, :], ident[:],
                                     start=True, stop=True)
                last.then_inc(hd_rows, 1)
                pe.wait_ge(hd_scaled, 1)
                pe.wait_ge(evac, 8)

                def score(h, b, bank):
                    for j in range(2):
                        part = slice(64 * j, 64 * j + 64)
                        pe.matmul(ps[:, bank + j, 0:P * (b + 1)], qk[part, h, P * b:P * b + P],
                                         qk[part, 4 + h, 0:P * (b + 1)], start=True, stop=False,
                                         skip_group_check=True)

                attention(0, 2, score, v_tok)
                pe.wait_ge(pooled, 1)
                for i in range(4):
                    last = pe.matmul(ps[:, 2 + i // 2, T * (i % 2):T * (i % 2) + T], pool_w[:, i, :], inv_count[:, i, :],
                                     start=True, stop=True)
                last.then_inc(pool_mm, 1)
                head_sums(4, work, 4, hd_sq, 1)
                head_rows(1, 8, 6)
                order = [4, 5, 6, 7, 0, 1, 2, 3]
                for j in range(4):
                    cols_chunk(4 + j, y_hi, y_lo, order=order,
                               waits=(lambda i: pe.wait_ge(y_lo_ready, i // 2 + 1)) if j == 0 else None)

            def mix_a1():
                def turn(j, first):
                    if not first:
                        pe.wait_ge(c_copied, j)
                    cols_chunk(0, x_hi, x_lo, waits=x_waits(4) if first else None)
                    if not first:
                        pe.wait_ge(cx_read, j)
                    cols_chunk(1, x_hi, x_lo)
                    if not first:
                        pe.wait_ge(y_made, j + 2)
                    cols_chunk(2, x_hi, x_lo)

                turn(0, True)
                base = at.turns
                with pe.Fori(1, 4) as j:
                    at.turns = base + j - 1
                    turn(j, False)
                    at.n -= 3
                at.turns = base
                at.n += 9
                for j in range(4):
                    cols_chunk(4 + j, y_hi, y_lo,
                               waits=(lambda i: pe.wait_ge(y_lo_ready, 4 + i // 2 + 1)) if j == 0 else None)

            pe.wait_ge(lam_done, 1)
            pe.matmul(ps[:, 2, 400:402], ones[0:64, :], lam_prod[:], start=True, stop=True).then_inc(lam_mm, 1)
            mix_a0()
            norm_stats(2, 2, False)
            clear_sums()
            norm_rows(2, False)
            ffn(1, 2, lambda: mod_sums(2))
            norm_stats(3, 3, False)
            clear_sums()
            norm_rows(3, False)
            ffn(2, 3, lambda: mod_sums(3))
            norm_stats(4, 4, False)
            norm_rows(4, False)
            mix_a1()
            norm_stats(5, 5, False)
            clear_sums()
            norm_rows(5, False)
            ffn(3, 5)
            pe.wait_ge(x_new, 6 * 8 + 8)
            clear_sums()
            assert at.n == A_CHUNKS

            def mix_b(l):
                x_c = call_x(l, 0)
                evac0 = call_e(l, 0)

                def proj(g, n=256, waits=None):
                    if g >= 3:
                        pe.wait_ge(evac, evac0 + (g - 2))
                    cols_chunk(g % 3, x_hi, x_lo, n=n, waits=waits)

                pe.wait_ge(lay_small, l * 64 + 64)
                for g in range(3):
                    proj(g, waits=x_waits(x_c) if g == 0 else None)
                for t in range(TT):
                    for k in range(KT):
                        last = pe.matmul(ps[:, 3, t * 8:t * 8 + 8], x[:, k, t * P:t * P + P], w_ab[:, k, :],
                                         start=(k == 0), stop=(k == KT - 1))
                last.then_inc(ab_mm, 1)
                for k in range(KT):
                    last = pe.matmul(ps[0:64, 4, 0:T], w_kr[:, k, :], x[:, k, :], start=(k == 0), stop=(k == KT - 1))
                last.then_inc(kr_mm, 1)
                for g in range(3, 7):
                    proj(g)
                pe.wait_ge(ab_copied, l * 2 + 2)
                head_sums(8, work, 3, qkv_act, l * 6 + 4)
                for g in range(7, 9):
                    proj(g)
                head_rows(call_h(l, 0), 16, 4)
                for g in range(9, 11):
                    proj(g)
                pe.wait_ge(g_ready, l + 1)
                pe.wait_ge(qk_hat, l + 1)
                pe.matmul(ps[:, 3, 64:72], tri[:], gl[:, 9, :], start=True, stop=True)
                for i in range(8):
                    pe.matmul(ps[:, 4 + i // 4, (i % 4) * P:(i % 4) * P + P], diag[:, i, :], tri[:], start=True, stop=True)
                for i in range(8):
                    last = pe.matmul(ps[:, 6 + i // 4, (i % 4) * P:(i % 4) * P + P], diag[:, 8 + i, :], ident[:],
                                     start=True, stop=True)
                last.then_inc(g_mm, 1)
                for g in range(11, 13):
                    proj(g, n=128 if g >= 12 else 256)
                pe.wait_ge(dec_exp, l + 1)
                for c in range(2):
                    for h in range(HEADS):
                        kc = qkv[:, 4 + h, c * P:c * P + P]
                        pe.matmul(ps[:, 4 + c, h * P:h * P + P], kc, kc, start=True, stop=True)
                for c in range(2):
                    for h in range(HEADS):
                        last = pe.matmul(ps[:, 6 + c, h * P:h * P + P], qkv[:, 4 + h, c * P:c * P + P],
                                         qkv[:, h, c * P:c * P + P], start=True, stop=True)
                last.then_inc(kk_mm, 1)
                for g in range(13, 15):
                    proj(g, n=128)
                pe.wait_ge(a_ready, l + 1)
                pe.wait_ge(qkv_act, l * 6 + 6)
                for c in range(2):
                    for h in range(HEADS):
                        pe.transpose(ps[:, 4 + c, h * P:h * P + P], qkv[:, 4 + h, c * P:c * P + P], ident[:])
                for c in range(2):
                    for h in range(HEADS):
                        last = pe.transpose(ps[:, 6 + c, h * P:h * P + P], qkv[:, 8 + h, c * P:c * P + P], ident[:])
                last.then_inc(tok_mm, 1)
                proj(15, n=128)
                proj(16, n=128)
                def half(h):
                    return [(i, slice((i % 4) * P, (i % 4) * P + P)) for i in range(4 * h, 4 * h + 4)]

                pe.wait_ge(e_first, l + 1)
                pe.wait_ge(evac, evac0 + 15)
                for h in range(2):
                    pe.matmul(ps[:, 2 + h, :], ident[:], emat[:, 4 * h:4 * h + 4, :], start=True, stop=True,
                              skip_group_check=True)
                pe.wait_ge(tok_done, l + 1)
                for h in range(2):
                    for i, cs in half(h):
                        last = pe.matmul(ps[:, 6 + h, cs], emat[:, i, :], ident[:], start=(i % 4 == 0), stop=True,
                                         skip_group_check=True)
                    last.then_inc(d_mm, 1)
                for s in range(1, LEVELS):
                    pe.wait_ge(b_ready, l * (LEVELS - 1) + s)
                    for h in range(2):
                        pe.wait_ge(d_copied, l * HALVES + (2 * s - 1 + h))
                        for i, cs in half(h):
                            last = pe.matmul(ps[:, 4 + h, cs], bmat[:, i, :], dmat[:, i, :], start=True, stop=True)
                        last.then_inc(t_mm, 1)

                    def parts_ready(h):
                        pe.wait_ge(t_copied, l * HALVES + (2 * s - 1 + h))
                        if s > 1:
                            pe.wait_ge(e_copied, l * HALVES + (2 * s - 3 + h))

                    if s + 1 < LEVELS:
                        for h in range(2):
                            parts_ready(h)
                            for i, cs in half(h):
                                last = pe.matmul(ps[:, 6 + h, cs], emat[:, i, :], tmat[:, i, :], start=False, stop=True,
                                                 skip_group_check=True)
                            last.then_inc(d_mm, 1)
                    for h in range(2):
                        if s + 1 == LEVELS:
                            parts_ready(h)
                        for i, cs in half(h):
                            last = pe.matmul(ps[:, 2 + h, cs], tmat[:, i, :], emat[:, i, :], start=False, stop=True,
                                             skip_group_check=True)
                        last.then_inc(e_mm, 1)
                pe.wait_ge(e_copied, l * HALVES + HALVES)
                for i in range(8):
                    c, h = i // 4, i % 4
                    pe.matmul(ps[:, 4 + c, h * P:h * P + P], emat[:, i, :], v_beta[:, c, h * P:h * P + P],
                              start=True, stop=True)
                for h in range(HEADS):
                    last = pe.matmul(ps[:, 6, h * P:h * P + P], k_tok[:, 1, h * P:h * P + P], emat[:, 4 + h, :],
                                     start=True, stop=True)
                last.then_inc(u_mm, 1)
                proj(17)
                pe.wait_ge(u_copied, l + 1)
                for h in range(HEADS):
                    last = pe.matmul(ps[:, 7, h * P:h * P + P], k_tok[:, 0, h * P:h * P + P], u_sb[:, h, :],
                                     start=True, stop=True)
                last.then_inc(s_mm, 1)
                pe.wait_ge(s_ready, l + 1)
                for h in range(HEADS):
                    last = pe.matmul(ps[:, 4, h * P:h * P + P], wt[:, h, :], s_state[:, h, :], start=True, stop=True)
                last.then_inc(ws_mm, 1)
                pe.wait_ge(v_new, l + 1)
                for h in range(HEADS):
                    dst = ps[:, 6 + h // 2, T * (h % 2):T * (h % 2) + T]
                    pe.matmul(dst[:, 0:P], u_sb[:, h, :], qk_dec[:, h, :], start=True, stop=True)
                    pe.matmul(dst[:, P:T], s_state[:, h, :], q_dec[:, h, :], start=True, stop=False)
                    last = pe.matmul(dst[:, P:T], u_sb[:, 4 + h, :], qk_dec[:, 4 + h, :], start=False, stop=True)
                last.then_inc(o_mm, 1)
                proj(18)
                head_sums(4, work, 3, hd_sq, sq_at(l, 0))
                proj(19)
                head_rows(call_h(l, 1), 8, 4)
                proj(20)

                def branch(j, first):
                    for c in range(2):
                        cols_chunk(4 + 2 * c, y_hi, y_lo, kt=4, n=512, first=first,
                                   waits=(lambda i: pe.wait_ge(y_lo_ready, call_y(l, 2 * j) + i // 2 + 1))
                                   if c == 0 else None)

                branch(0, 0)
                proj(21)
                proj(22)
                pe.wait_ge(hd_sq, sq_at(l, 1))
                for i in range(4):
                    for t in range(TT):
                        pe.matmul(ps[:, 3, t:t + 1], work[:, 4 + i, t * P:t * P + P], ones[:, 0:1],
                                  start=(i == 0 and t == 0), stop=(i == 3), skip_group_check=True)
                        last = pe.matmul(ps[:, 3, 2 + t:3 + t], conv[:, i, t * P:t * P + P], ones[:, 0:1],
                                         start=False, stop=(i == 3), skip_group_check=True)
                last.then_inc(hd_stats, 1)
                proj(23)
                head_rows(call_h(l, 2), 4, 3)
                proj(24)
                pe.wait_ge(branch_free, l * 2 + 1)
                branch(1, 4)
                pe.wait_ge(hd_sq, sq_at(l, 2))
                for i in range(5):
                    for t in range(TT):
                        c = t if i < 3 else 2 + t
                        last = pe.matmul(ps[:, 3, c:c + 1], work[:, i, t * P:t * P + P], ones[:, 0:1],
                                         start=(i == 0 and t == 0), stop=(i in (2, 4)), skip_group_check=True)
                last.then_inc(hd_stats, 1)
                proj(25)
                head_rows(call_h(l, 3), 4, 3)
                proj(26)
                pe.wait_ge(branch_free, l * 2 + 2)
                pe.wait_ge(mla_w, l * 32 + 32)
                pe.wait_ge(hd_scaled, l + 2)
                for h in range(HEADS):
                    for k in range(3):
                        pe.matmul(ps[:, 4 + h // 2, T * (h % 2):T * (h % 2) + T], uq[:, k, 192 * h:192 * h + P],
                                  low[:, k, :], start=(k == 0), stop=(k == 2))
                for h in range(HEADS):
                    for k in range(3):
                        last = pe.matmul(ps[0:64, 6 + h // 2, T * (h % 2):T * (h % 2) + T],
                                         uq[:, k, 192 * h + P:192 * h + 192], low[:, k, :], start=(k == 0), stop=(k == 2))
                last.then_inc(mla_mm, 1)
                proj(27)
                pe.wait_ge(mla_sb, l * 2 + 1)
                for i in range(2):
                    pe.matmul(ps[:, 4 + i, :], rot[:], q_rope[:, 2 * i:2 * i + 2, :], start=True, stop=True)
                pe.matmul(ps[:, 3, 0:T], rot[:], k_rope[:], start=True, stop=True).then_inc(rot_mm, 1)
                for h in range(HEADS):
                    for k in range(2):
                        pe.matmul(ps[:, 6 + h // 2, T * (h % 2):T * (h % 2) + T], ukv[:, k, 256 * h:256 * h + P],
                                  low[:, 3 + k, :], start=(k == 0), stop=(k == 1))
                ukv_v = ukv[:].rearrange("p k (h n) -> p k h n", h=HEADS)
                pe.wait_ge(rope_done, l + 1)
                for t in range(TT):
                    for k in range(2):
                        last = pe.matmul(ps[:, 4 + t, :], low[:, 3 + k, t * P:t * P + P], ukv_v[:, k, :, P:2 * P],
                                         start=(k == 0), stop=(k == 1))
                last.then_inc(mla_mm, 1)
                proj(28)
                pe.wait_ge(mla_sb, l * 2 + 2)
                pe.wait_ge(evac, evac0 + 29)

                def score(h, b, bank):
                    dst = ps[:, bank, 0:P * (b + 1)]
                    pe.matmul(dst, q_nope[:, h, P * b:P * b + P], k_nope[:, h, 0:P * (b + 1)], start=True, stop=False,
                              skip_group_check=True)
                    pe.matmul(dst, q_rope[:, h, P * b:P * b + P], k_rope[:, 0:P * (b + 1)], start=False, stop=False,
                              skip_group_check=True)

                attention(l * 8 + 8, 1, score, v_mla)
                branch(2, 4)
                for j in range(4):
                    cols_chunk(4 + j, y_hi, y_lo,
                               waits=(lambda i: pe.wait_ge(y_lo_ready, call_y(l, 6) + i // 2 + 1)) if j == 0 else None)

            with pe.Fori(0, 2) as l:
                at.turns = l * LAYER_TURNS
                at.n = B0

                def turn_params():
                    pe.wait_ge(lay_rows, l * (17 * 16) + 17 * 16)
                    pe.transpose(ps[:, 2, 0:106], rows1[:], ident[0:106, 0:106])
                    pe.transpose(ps[:, 2, 128:176], rows2[:], ident[0:48, 0:48])
                    pe.transpose(ps[:, 2, 256:380], rows3[:], ident[0:124, 0:124]).then_inc(lay_turned, 1)

                ffn(l * 2 + 4, l * 3 + 6, turn_params)
                pe.wait_ge(lay_cols, l + 1)
                norm_stats(call_n(l, 0), call_x(l, 0), True)
                norm_rows(call_n(l, 0), True)
                mix_b(l)
                norm_stats(call_n(l, 1), call_x(l, 1), True)
                clear_sums()
                norm_rows(call_n(l, 1), True)
                ffn(l * 2 + 5, call_x(l, 1))
                norm_stats(call_n(l, 2), call_x(l, 2), True)
                clear_sums()
                norm_rows(call_n(l, 2), True)
            for half in range(2):
                for t in range(TT):
                    for i in range(4):
                        m = 4 * half + i
                        if t == 0:
                            pe.wait_ge(scaled, 11 * 8 + (m + 1))
                        last = pe.transpose(ps[:, 4 + 2 * half + t, i * P:i * P + P], x[:, m, t * P:t * P + P], ident[:])
                    last.then_inc(out_turned, 1)

        @block.scalar
        def _(act):
            f = nc.scalar.activation
            at = Place()
            limit = [A_CHUNKS + EARLY]

            def convert():
                s, n = at.slot(), chunk_cols(at.n)
                act.wait_ge(landed[s], 16 * (at.turn() + 1))
                if at.n >= RING:
                    act.wait_ge(chunk_used, at.count(RING - 1))
                f(w_hi[s][:, 0:n], raw[s][:, 0:n], ACT.Copy).then_inc(hi_ready, 1)
                at.n += 1

            def ahead(n):
                while at.n < min(n, limit[0]):
                    convert()

            def chunk_done(n):
                act.wait_ge(chunk_used, 3 * at.turns + (n + 1))

            def sq(n, call, b=None):
                for m in range(KT):
                    if b is not None and m % 2 == 0:
                        ahead(b + m // 2 + 3)
                    act.wait_ge(x_new, call * 8 + (m + 1))
                    f(work[:, m, :], x[:, m, :], ACT.Square).then_inc(squares, 1)

            def norm_out(n, whole):
                for k in range(KT):
                    act.wait_ge(scaled, n * 8 + (k + 1))
                    f(x_hi[:, k, :], whole[:, k, :], ACT.Copy).then_inc(x_hi_ready, 1)

            def ffn(b, call):
                def first_half(i, g):
                    chunk_done(g)
                    if not (isinstance(i, int) and i == 0):
                        act.wait_ge(hid_made, call * PAIRS + i)
                    f(silu_g[:], ps[:, 0, :], ACT.Silu).then_inc(gate_read, 1)

                def rounded(i):
                    act.wait_ge(hid_made, call * PAIRS + (i + 1))
                    f(hid_hi[:], hid[:].rearrange("p (k n) -> p k n", k=2), ACT.Copy).then_inc(hid_hi_ready, 1)

                ahead(b + 3)
                first_half(0, b)
                ahead(b + 5)
                rounded(0)
                base = at.turns
                with act.Fori(1, PAIRS - 1) as i:
                    at.turns = base + i - 1
                    first_half(i, b + 2)
                    convert()
                    convert()
                    chunk_done(b + 4)
                    rounded(i)
                    convert()
                    at.n -= 3
                at.turns = base
                at.n += 3 * (PAIRS - 2)
                last = b + 2 + 3 * (PAIRS - 2)
                first_half(PAIRS - 1, last)
                ahead(last + 5)
                chunk_done(last + 2)
                rounded(PAIRS - 1)
                ahead(last + 6)

            act.wait_ge(cols_ready, 1)
            f(c_act[:], a_cols[:, 77:85], ACT.Silu).then_inc(c_ready, 1)

            def exps(it, item0, heads, scale):
                act.wait_ge(at_max, item0 + (it + 1))
                if it >= 2:
                    act.wait_ge(at_weights, item0 + (it - 1))
                n = P * (it // HEADS + 1)
                for j in range(heads):
                    last = f(probs[:, it % 2, j, 0:n], ps[:, 4 + 2 * (it % 2) + j, 0:n], ACT.Exp,
                             bias=negmax[:, it, j:j + 1], scale=scale, accum_out=sums[:, it, j:j + 1])
                last.then_inc(at_probs, 1)

            def attention(item0, heads, scale):
                exps(0, item0, heads, scale)
                for it in range(8):
                    if it < 7:
                        exps(it + 1, item0, heads, scale)
                    act.wait_ge(at_turned, item0 + (it + 1))
                    if it >= 1:
                        act.wait_ge(at_out, item0 + it)
                    n = it // HEADS + 1
                    f(turned[:, 0:n, :], ps[:, 2 + it % 2, 0:n * P].rearrange("p (k n) -> p k n", k=n),
                      ACT.Copy).then_inc(at_copied, 1)
                act.wait_ge(at_out, item0 + 8)

            def two_banks(b):
                return ps[:, b:b + 2, :].rearrange("p b (k n) -> p (b k) n", k=2)

            def y_round(count0, made, src, pair):
                act.wait_ge(y_made, made)
                f(y_hi[:, 2 * pair:2 * pair + 2, :], src[:, 2 * pair:2 * pair + 2, :], ACT.Copy)\
                    .then_inc(y_hi_ready, 1)

            def mix_a0(b):
                for j in range(8):
                    ahead(b + j + 3)
                    chunk_done(b + j)
                    src = ps[:, j % 3, :].rearrange("p (k n) -> p k n", k=2)
                    if j < 4:
                        f(qk[:, 2 * j:2 * j + 2, :], src, ACT.Copy)
                        f(work[:, 2 * j:2 * j + 2, :], src, ACT.Square).then_inc(evac, 1)
                    elif j < 6:
                        f(v_tok[:, :, T * (j - 4):T * (j - 4) + T], src, ACT.Copy).then_inc(evac, 1)
                    else:
                        f(u_in[:, 2 * (j - 6):2 * (j - 6) + 2, :], src, ACT.Copy).then_inc(evac, 1)
                ahead(b + 11)
                attention(0, 2, QK_DIM ** -0.5)
                f(out_sb[:], two_banks(0), ACT.Copy)
                f(work[:, 0:4, :], two_banks(0), ACT.Square).then_inc(hd_sq, 1)
                act.wait_ge(pool_mm, 1)
                for i in range(4):
                    src = ps[:, 2 + i // 2, T * (i % 2):T * (i % 2) + T]
                    col = a_cols[:, 49 + i:50 + i]
                    f(work[:, 4 + i, :], src, ACT.Copy, scale=col)
                    last = f(y_hi[:, 4 + i, :], src, ACT.Copy, scale=col)
                    if i % 2:
                        last.then_inc(y_hi_ready, 1)
                for i in range(2):
                    y_round(0, i + 1, work, i)

            def mix_a1(b):
                for j in range(4):
                    n = b + 3 * j
                    chunk_done(n)
                    if j:
                        act.wait_ge(cx_read, j)
                    f(c_sb[:], ps[:, 0, :].rearrange("p (k n) -> p k n", k=2), ACT.Copy).then_inc(c_copied, 1)
                    ahead(n + 6)
                    y_round(4, 2 + j + 1, work, j)
                    if j == 2:
                        act.wait_ge(rope_conv, 1)
                        f(sin_t[:], angle, ACT.Sin)
                        f(cos_t[:], angle, ACT.Sin, scale=0.5).then_inc(rope_sin, 1)

            sq(0, 0)
            ahead(2)
            norm_out(0, work)
            ffn(0, 0)
            sq(1, 1)
            norm_out(1, work)
            act.wait_ge(lam_mm, 1)
            f(lam[:, 1:3], ps[:, 2, 400:402], ACT.Exp).then_inc(lam_exp, 1)
            ahead(A_MIX[0] + 3)
            mix_a0(A_MIX[0])
            sq(2, 2, A_MIX[0] + 8)
            ahead(A_FFN[1] + 3)
            norm_out(2, work)
            ffn(A_FFN[1], 1)
            sq(3, 3)
            norm_out(3, work)
            ffn(A_FFN[2], 2)
            sq(4, 4)
            norm_out(4, work)
            ahead(A_MIX[1] + 3)
            mix_a1(A_MIX[1])
            sq(5, 5, A_MIX[1] + 12)
            ahead(A_FFN[3] + 3)
            norm_out(5, work)
            ffn(A_FFN[3], 3)
            for k in range(KT):
                act.wait_ge(x_new, 6 * 8 + k + 1)
                f(x_hi[:, k, :], x[:, k, :], ACT.Copy).then_inc(x_hi_ready, 1)

            def mix_b(l):
                n0 = B_MIX

                def bank(g):
                    return ps[:, g % 3, :]

                def arrived(g):
                    ahead(n0 + pos(g) + 3)
                    chunk_done(n0 + pos(g))

                def act_qkv(g):
                    act.wait_ge(conv_done, l * 6 + (g + 1))
                    pair = qkv[:, 2 * g:2 * g + 2, :]
                    last = f(pair, pair, ACT.Silu)
                    if g < 4:
                        act.drain()
                        last = f(work[:, 2 * g:2 * g + 2, :], pair, ACT.Square)
                    last.then_inc(qkv_act, 1)

                def gate_out(g):
                    arrived(g)
                    br, j = (g - 17) // 4, (g - 17) % 4
                    if br and j == 0:
                        act.wait_ge(branch_free, l * 2 + br)
                    for i in range(2):
                        m = 2 * j + i
                        last = f(gate[:, m, :], bank(g)[:, T * i:T * i + T], ACT.Sigmoid,
                                 bias=cols1[:, CB_GATE + 8 * br + m:CB_GATE + 8 * br + m + 1])
                    last.then_inc(evac, 1)

                for g in range(6):
                    arrived(g)
                    if g:
                        act.wait_ge(conv_done, l * 6 + g)
                    f(stage[:], bank(g), ACT.Copy)
                    for i in range(2):
                        t = 2 * g + i
                        last = f(qkv[:, t, :], bank(g)[:, T * i:T * i + T], ACT.Copy, scale=cols2[:, 36 + t:37 + t])
                    last.then_inc(evac, 1)
                    act_qkv(g)
                    if g == 3:
                        act.wait_ge(ab_mm, l + 1)
                        f(ab[:], ps[:, 3, 0:16].rearrange("p (t n) -> p t n", t=TT), ACT.Copy).then_inc(ab_copied, 1)
                        act.wait_ge(kr_mm, l + 1)
                        f(k_rope[:], ps[0:64, 4, 0:T], ACT.Copy).then_inc(ab_copied, 1)
                    if g == 4:
                        act.wait_ge(ab_in, l + 1)
                        f(gl[:, 2, :], gl[:, 1, :], ACT.Exp)
                        f(gl[:, 3, :].rearrange("p (t h) -> p t h", t=TT), ab[:, :, 4:8], ACT.Exp, scale=-1.0)
                        f(gl[:, 4, 0:4], head_par[:, 0, :], ACT.Exp).then_inc(ab_exp, 1)
                for g in (6, 7):
                    arrived(g)
                    f(z_act[:, 2 * (g - 6):2 * (g - 6) + 2, :], bank(g).rearrange("p (k n) -> p k n", k=2), ACT.Silu)\
                        .then_inc(evac, 1)
                for g in range(8, 12):
                    arrived(g)
                    p = (g - 8) // 2
                    gated = g % 2
                    if g == 11:
                        act.wait_ge(glu_ready, l * 2 + 1)
                    for i in range(2):
                        t = 2 * p + i
                        c = CB_GLU + 4 * gated + t
                        last = f(sig[:, i, :] if gated else glu[:, t, :], bank(g)[:, T * i:T * i + T],
                                 ACT.Sigmoid if gated else ACT.Identity, bias=cols1[:, c:c + 1])
                    last.then_inc(evac, 1)
                act.wait_ge(dec_in, l + 1)
                f(emat[:], emat[:], ACT.Exp)
                f(gl[:, 8, 0:4], gcol[:, 4:8], ACT.Exp)
                f(gl[:, 8, 4:8], gl[:, 11, 0:4], ACT.Exp)
                f(q_dec[:], ps[:, 5, :].rearrange("p (h n) -> p h n", h=HEADS), ACT.Exp)
                f(tmat[:], ps[:, 6:8, :].rearrange("p b (h n) -> p (b h) n", n=P), ACT.Copy, scale=-1.0)\
                    .then_inc(dec_exp, 1)
                def low_out(g):
                    arrived(g)
                    f(low[:, g - 12, :], bank(g)[:, 0:T], ACT.Copy).then_inc(evac, 1)

                for g in range(12, 17):
                    low_out(g)

                def half_out(dst, bank, h, ready, done, value):
                    act.wait_ge(ready, value)
                    f(dst[:, 4 * h:4 * h + 4, :], ps[:, bank + h, :].rearrange("p (h n) -> p h n", n=P), ACT.Copy)\
                        .then_inc(done, 1)

                for s in range(1, LEVELS):
                    for h in range(2):
                        half_out(tmat, 4, h, t_mm, t_copied, l * HALVES + (2 * s - 1 + h))
                    for h in range(2):
                        half_out(emat, 2, h, e_mm, e_copied, l * HALVES + (2 * s - 1 + h))
                    if s == 1:
                        ahead(n0 + 20)
                act.wait_ge(u_mm, l + 1)
                f(u_sb[:], ps[:, 4:6, :].rearrange("p b (h n) -> p (b h) n", n=P), ACT.Copy)
                f(wt[:], ps[:, 6, :].rearrange("p (h n) -> p h n", n=P), ACT.Copy).then_inc(u_copied, 1)
                gate_out(17)
                act.wait_ge(o_mm, l + 1)
                f(out_sb[:], two_banks(6), ACT.Copy)
                f(work[:, 0:4, :], two_banks(6), ACT.Square).then_inc(hd_sq, 1)
                gate_out(18)
                gate_out(19)
                for i in range(2):
                    y_round(0, 6 * l + (7 + i), work, i)
                gate_out(20)
                gate_out(21)
                ahead(n0 + 26)
                act.wait_ge(cv_dve, l + 1)
                act.wait_ge(cv_pool, l + 1)
                f(work[:, 4:8, :], conv[:], ACT.Square).then_inc(hd_sq, 1)
                gate_out(22)
                ahead(n0 + 28)
                for i in range(2):
                    act.wait_ge(cv_scaled, l * 2 + (i + 1))
                    for t in (2 * i, 2 * i + 1):
                        f(work[:, 4 + t, :], conv[:, t, :], ACT.Silu, scale=cols1[:, CB_LNG + t:CB_LNG + t + 1],
                          bias=cols1[:, CB_LNB + t:CB_LNB + t + 1])
                    act.drain()
                    f(y_hi[:, 4 + 2 * i:6 + 2 * i, :], work[:, 4 + 2 * i:6 + 2 * i, :], ACT.Copy).then_inc(y_hi_ready, 1)
                gate_out(23)
                gate_out(24)
                act.wait_ge(y_lo_ready, call_y(l, 4))
                f(work[:, 0:5, :], low[:], ACT.Square).then_inc(hd_sq, 1)
                for g in range(25, 27):
                    gate_out(g)
                act.wait_ge(mla_mm, l * 2 + 1)
                f(q_nope[:], two_banks(4), ACT.Copy)
                f(q_rope[:], ps[0:64, 6:8, :].rearrange("p b (k n) -> p (b k) n", k=2), ACT.Copy).then_inc(mla_sb, 1)
                gate_out(27)
                act.wait_ge(mla_mm, l * 2 + 2)
                f(k_nope[:], two_banks(6), ACT.Copy)
                f(v_mla[:], ps[:, 4:6, :], ACT.Copy).then_inc(mla_sb, 1)
                gate_out(28)
                attention(l * 8 + 8, 1, 192 ** -0.5)
                for i in range(2):
                    src = ps[:, i, :].rearrange("p (k n) -> p k n", k=2)
                    f(work[:, 4 + 2 * i:6 + 2 * i, :], src, ACT.Copy)
                    f(y_hi[:, 4 + 2 * i:6 + 2 * i, :], src, ACT.Copy).then_inc(y_hi_ready, 1)
                ahead(n0 + 37)
                for i in range(4):
                    y_round(0, 6 * l + (9 + i), merged, i)

            assert at.n == limit[0]
            with act.Fori(0, 2) as l:
                at.turns = l * LAYER_TURNS
                at.n = B0 + EARLY
                limit[0] = B0 + EARLY + B_LAYER_CH
                ffn(B0, l * 2 + 4)
                sq(call_n(l, 0), call_x(l, 0))
                act.wait_ge(lay_cols, l + 1)
                norm_out(call_n(l, 0), x)
                ahead(B_MIX + 3)
                mix_b(l)
                sq(call_n(l, 1), call_x(l, 1), B_MIX + 35)
                ahead(B_FFN[1] + 3)
                norm_out(call_n(l, 1), x)
                ffn(B_FFN[1], l * 2 + 5)
                sq(call_n(l, 2), call_x(l, 2))
                norm_out(call_n(l, 2), x)
                assert at.n == limit[0]
            for i in range(4):
                act.wait_ge(out_turned, i + 1)
                f(y_rows[:, i % 2, 512 * (i // 2):512 * (i // 2) + 512], ps[:, 4 + i, :], ACT.Copy).then_inc(out_copied, 1)

        @block.vector
        def _(dve):
            v = nc.vector
            at = Place()
            limit = [A_CHUNKS + EARLY]

            def convert():
                s, n = at.slot(), chunk_cols(at.n)
                dve.wait_ge(hi_ready, at.count() + 1)
                v.tensor_tensor(w_lo[s][:, 0:n], raw[s][:, 0:n], w_hi[s][:, 0:n].bitcast(F32), ALU.subtract)\
                    .then_inc(lo_ready, 1)
                at.n += 1

            def ahead(n):
                while at.n < min(n, limit[0]):
                    convert()

            def chunk_done(n):
                dve.wait_ge(chunk_used, 3 * at.turns + (n + 1))

            def lo_of(dst, whole, hi):
                return v.tensor_tensor(dst, whole, hi.bitcast(F32), ALU.subtract)

            def make_diag(n, done):
                v.tensor_tensor(diag[:, 0:n, :], bc(ident[:].unsqueeze(1), (P, n, P)),
                                bc(rstd[:, 0:n].unsqueeze(2), (P, n, P)), ALU.mult).then_inc(done, 1)

            def mean_moments(bank, n, eps, done):
                v.tensor_scalar(small[:, 0:4], ps[:, bank, 0:4], 1.0 / n, None, ALU.mult)
                dve.drain()
                v.tensor_tensor(small[:, 4:6], small[:, 2:4], small[:, 2:4], ALU.mult)
                dve.drain()
                v.tensor_tensor(small[:, 6:8], small[:, 0:2], small[:, 4:6], ALU.subtract)
                dve.drain()
                v.tensor_scalar(moment[:, 0:2], small[:, 6:8], 0.0, eps, ALU.max, ALU.add).then_inc(done, 1)

            def mean_scales():
                v.scalar_tensor_tensor(out=rstd[:, 2:4], in0=small[:, 2:4], scalar=-1.0, in1=rstd[:, 0:2],
                                       op0=ALU.mult, op1=ALU.mult)
                dve.drain()

            def x_lo_rest(call, whole):
                for k in range(POOL_LO, KT):
                    dve.wait_ge(x_hi_ready, call * 8 + (k + 1))
                    lo_of(x_lo[:, k, :], whole[:, k, :], x_hi[:, k, :]).then_inc(x_lo_last, 1)

            def add_squares(n, m):
                if m in (5, 7):
                    dve.wait_ge(squares, n * 8 + (m - 1))
                    last = v.tensor_tensor(work[:, 0:2, :], work[:, 0:2, :], work[:, m - 3:m - 1, :], ALU.add)
                    if m == 7:
                        last.then_inc(squares_added, 1)
                    else:
                        dve.drain()

            def square_moments(n):
                dve.wait_ge(stats, n + 1)
                v.tensor_scalar(moment[:, 0:2], ps[:, 2, 0:2], 1.0 / D, A_EPS, ALU.mult, ALU.add).then_inc(moments, 1)

            def square_scales(n):
                dve.wait_ge(rstd_ready, n + 1)
                make_diag(2, diag_ready)

            def norm_a(n):
                if n > 0:
                    square_moments(n)
                    square_scales(n)
                dve.wait_ge(rows_ready, n + 1)
                for i in range(4):
                    for k in (2 * i, 2 * i + 1):
                        v.scalar_tensor_tensor(out=work[:, k, :], in0=x[:, k, :], scalar=norm_col[:, n, k:k + 1],
                                               in1=ps[:, 3, 0:T], op0=ALU.mult, op1=ALU.mult)
                    dve.drain()
                    for k in (2 * i, 2 * i + 1):
                        v.tensor_scalar(work[:, k, :], work[:, k, :], mod[:, 3 * n, k:k + 1], None, ALU.add)\
                            .then_inc(scaled, 1)
                x_lo_rest(n, work)

            def norm_b(n, call, gain, shift, eps):
                dve.wait_ge(stats, n + 1)
                mean_moments(2, D, eps, moments)
                dve.wait_ge(rstd_ready, n + 1)
                mean_scales()
                make_diag(4, diag_ready)
                dve.wait_ge(rows_ready, n + 1)
                for i in range(4):
                    sl = slice(2 * i, 2 * i + 2)
                    v.tensor_tensor(work[:, sl, :], x[:, sl, :], bc(ps[:, 3, 0:T].unsqueeze(1), (P, 2, T)), ALU.mult)
                    dve.drain()
                    v.tensor_tensor(work[:, sl, :], work[:, sl, :], bc(ps[:, 3, T:2 * T].unsqueeze(1), (P, 2, T)),
                                    ALU.add)
                    dve.drain()
                    for k in (2 * i, 2 * i + 1):
                        v.tensor_scalar(x[:, k, :], work[:, k, :], gain(k), shift(k), ALU.mult, ALU.add)\
                            .then_inc(scaled, 1)
                x_lo_rest(call, x)

            def residual_a(n, call, last):
                for m in range(KT):
                    acc_done(call, m, last)
                    v.scalar_tensor_tensor(out=x[:, m, :], in0=acc(m), scalar=gate_col[:, n, m:m + 1], in1=x[:, m, :],
                                           op0=ALU.mult, op1=ALU.add).then_inc(x_new, 1)
                    if n < 5:
                        add_squares(n + 1, m)
                ahead(last + 3)

            def residual_b(scale, call, last, n):
                for m in range(KT):
                    acc_done(call, m, last)
                    v.scalar_tensor_tensor(out=x[:, m, :], in0=x[:, m, :], scalar=scale, in1=acc(m),
                                           op0=ALU.mult, op1=ALU.add).then_inc(x_new, 1)
                    add_squares(n, m)
                ahead(last + 3)

            def residual_chunks(b, n, how):
                for c in range(4):
                    ahead(b + c + 3)
                    chunk_done(b + c)
                    for m in (2 * c, 2 * c + 1):
                        how(m)
                        add_squares(n, m)
                ahead(b + 7)

            def ada_steps(grp, k, js):
                rounds = GROUPS[grp][3]
                first = isinstance(k, int) and k == 0
                dve.drain()
                for j in js:
                    if grp == 0:
                        u = 2 * k + j
                        slot, turn = u % ADA_SLOTS, u // ADA_SLOTS + 1
                    else:
                        slot, turn = j, k + (rounds[j] + 1)
                    dve.wait_ge(ada_landed[slot], turn * 16)
                    ck = c_act[:, k:k + 1] if isinstance(k, int) else c_act[:, ds(k, 1)]
                    if first:
                        v.tensor_scalar(ada_acc[:, j, :], ada_raw[slot], ck, None, ALU.mult).then_inc(ada_used, 1)
                    else:
                        v.scalar_tensor_tensor(out=ada_acc[:, j, :], in0=ada_raw[slot], scalar=ck,
                                               in1=ada_acc[:, j, :], op0=ALU.mult, op1=ALU.add).then_inc(ada_used, 1)

            def mod_finish(grp):
                m0, width = GROUPS[grp][0], GROUPS[grp][1]
                dve.wait_ge(mod_summed, grp + 1)
                v.tensor_tensor(mod[:, m0:m0 + width, :], ps[:, 1, 0:width * KT].rearrange("p (j t) -> p j t", t=KT),
                                b_cols.rearrange("p l (j t) -> p (l j) t", t=KT)[:, m0:m0 + width, :], ALU.add)
                dve.drain()
                for m in range(m0, m0 + width):
                    n = m // 3
                    if m % 3 == 1:
                        v.scalar_tensor_tensor(out=norm_col[:, n, :], in0=mod[:, m, :], scalar=1.0,
                                               in1=a_cols[:, 8 * n:8 * n + 8], op0=ALU.add, op1=ALU.mult)
                    elif m % 3 == 2:
                        v.tensor_scalar(gate_col[:, n, :], mod[:, m, :], 1.0 if n % 3 == 1 else 0.5, None, ALU.mult)
                dve.drain()

            def ffn(b, call, grp=None, after_rest=None):

                def made(i, g):
                    dve.drain()
                    dve.wait_ge(gate_read, call * PAIRS + (i + 1))
                    chunk_done(g + 1)
                    if not (isinstance(i, int) and i == 0):
                        dve.wait_ge(hid_hi_ready, call * PAIRS + i)
                    v.tensor_tensor(hid[:], silu_g[:], ps[:, 1, :], ALU.mult).then_inc(hid_made, 1)

                def rest(i):
                    dve.wait_ge(hid_hi_ready, call * PAIRS + (i + 1))
                    lo_of(hid_lo[:], hid[:].rearrange("p (k n) -> p k n", k=2), hid_hi[:]).then_inc(hid_lo_ready, 1)

                def ada(k, part):
                    if grp is not None:
                        ada_steps(grp, k, part_of(GROUPS[grp][1], part))

                ahead(b + 3)
                ada(0, 0)
                made(0, b)
                ahead(b + 5)
                ada(0, 1)
                rest(0)
                ada(0, 2)
                base = at.turns

                def body(i, with_ada):
                    convert()
                    if with_ada:
                        ada(i, 0)
                    made(i, b + 2)
                    convert()
                    if with_ada:
                        ada(i, 1)
                    rest(i)
                    convert()
                    if with_ada:
                        ada(i, 2)
                    at.n -= 3

                split = KT if grp is not None else 1
                if grp is not None:
                    with dve.Fori(1, KT) as i:
                        at.turns = base + i - 1
                        body(i, True)
                with dve.Fori(split, PAIRS - 1) as i:
                    at.turns = base + i - 1
                    body(i, False)
                at.turns = base
                at.n += 3 * (PAIRS - 2)
                last = b + 2 + 3 * (PAIRS - 2)
                ahead(last + 4)
                made(PAIRS - 1, last)
                ahead(last + 5)
                rest(PAIRS - 1)
                if grp is not None:
                    mod_finish(grp)
                if after_rest:
                    after_rest()

            def acc_done(call, m, last):
                if m in (0, 2, 4):
                    dve.wait_ge(acc_ready, call * 3 + (m // 2 + 1))
                elif m == 6:
                    chunk_done(last)

            def attention(item0, heads, scale):
                def largest(it):
                    n = P * (it // HEADS + 1)
                    par = it % 2
                    dve.wait_ge(at_scores, item0 + (it + 1))
                    v.tensor_reduce(recips[:, it, 0:heads], ps[:, 4 + 2 * par:4 + 2 * par + heads, 0:n], AX, ALU.max)
                    dve.drain()
                    v.tensor_scalar(negmax[:, it, 0:heads], recips[:, it, 0:heads], -scale, None, ALU.mult)\
                        .then_inc(at_max, 1)

                def weight(it):
                    n = P * (it // HEADS + 1)
                    par = it % 2
                    dve.wait_ge(at_probs, item0 + (it + 1))
                    v.reciprocal(recips[:, it, 0:heads], sums[:, it, 0:heads])
                    dve.drain()
                    if it >= 1:
                        dve.wait_ge(at_turned, item0 + it)
                    if heads == 1:
                        v.tensor_scalar(weights[:, 0:n], probs[:, par, 0, 0:n], recips[:, it, 0:1], None, ALU.mult)\
                            .then_inc(at_weights, 1)
                        return
                    v.tensor_scalar(weights[:, 0:n], probs[:, par, 1, 0:n], recips[:, it, 1:2], lam[:, 0:1],
                                    ALU.mult, ALU.mult)
                    dve.drain()
                    v.scalar_tensor_tensor(out=weights[:, 0:n], in0=probs[:, par, 0, 0:n], scalar=recips[:, it, 0:1],
                                           in1=weights[:, 0:n], op0=ALU.mult, op1=ALU.add).then_inc(at_weights, 1)

                largest(0)
                for it in range(8):
                    if it < 7:
                        largest(it + 1)
                    weight(it)

            def y_rest(count, whole, pair):
                dve.wait_ge(y_hi_ready, count)
                sl = slice(2 * pair, 2 * pair + 2)
                lo_of(y_lo[:, sl, :], whole[:, sl, :], y_hi[:, sl, :]).then_inc(y_lo_ready, 1)

            def head_scales(call, bank, n, inv, eps, meanwhile=None):
                dve.wait_ge(hd_stats, call + 1)
                v.tensor_scalar(moment[:, 0:n], ps[:, bank, 0:n], inv, eps, ALU.mult, ALU.add).then_inc(hd_moment, 1)
                if meanwhile:
                    meanwhile()
                dve.wait_ge(hd_rstd, call + 1)

            v.memset(ones[:], 1.0)
            v.memset(zeros[:], 0.0)
            v.memset(vpad[:], 0.0)
            dve.drain().then_inc(const_dve, 1)
            dve.wait_ge(rows_turned, 1)
            v.tensor_copy(a_cols[:], ps[:, 0, 0:85])
            v.tensor_copy(b_cols[:, 0, :], ps[:, 0, 128:200])
            v.tensor_copy(b_cols[:, 1, :], ps[:, 0, 256:328])
            dve.drain().then_inc(cols_ready, 1)
            dve.wait_ge(const_ready, 1)
            v.tensor_copy(ident_b[:], ident[:])
            v.tensor_copy(cmask_b[:], cmask)
            v.tensor_copy(win[0][:, 0, :], count_i[:])
            dve.drain()
            v.reciprocal(win[1][:, 0, :], win[0][:, 0, :])
            dve.drain()
            for n, width in enumerate(WINDOWS):
                v.tensor_scalar(inv_count[:, n, :], win[1][:, 0, :], 1.0 / width, None, ALU.max)
            for m in range(KT):
                if m % 2 == 0:
                    dve.wait_ge(x_turned, m + 2)
                v.tensor_copy(x[:, m, :], acc(m)).then_inc(x_new, 1)
                add_squares(0, m)
            dve.wait_ge(c_ready, 1)
            for k in range(KT):
                ada_steps(0, k, range(2))
                if k == 4:
                    square_moments(0)
                elif k == 5:
                    square_scales(0)
            ahead(2)
            mod_finish(0)
            dve.wait_ge(params2_in, 9 * 16)
            v.tensor_tensor(lam_prod[:, 0:1], lam_in[:, 0:1], lam_in[:, 1:2], ALU.mult)
            v.tensor_tensor(lam_prod[:, 1:2], lam_in[:, 2:3], lam_in[:, 3:4], ALU.mult)
            v.tensor_scalar(sub_gain[:], a_cols[:, 48:49], 1.0 - LAM_INIT, None, ALU.mult)
            dve.drain().then_inc(lam_done, 1)

            norm_a(0)
            ffn(0, 0, 1)
            residual_a(0, 0, A_FFN[0] + FFN_CH - 1)
            norm_a(1)

            def mix_a0(b):
                for j in range(8):
                    ahead(b + j + 3)
                    if j == 5:
                        head_scales(0, 4, 32, 1.0 / QK_DIM, A_EPS)
                        v.tensor_copy(bc_half[:].rearrange("p i (s n) -> p (i s) n", s=2),
                                      bc(rstd[:].unsqueeze(2), (P, 32, 64))).then_inc(hd_diag, 1)
                dve.wait_ge(lam_exp, 1)
                v.tensor_tensor(lam[:, 3:4], lam[:, 2:3], lam[:, 1:2], ALU.subtract)
                dve.drain()
                v.tensor_scalar(lam[:, 0:1], lam[:, 3:4], -LAM_INIT, None, ALU.add)
                dve.wait_ge(hd_rows, 1)
                for i in range(4):
                    last = v.scalar_tensor_tensor(
                        out=qk[:, 2 * i:2 * i + 2, :], in0=qk[:, 2 * i:2 * i + 2, :], scalar=qk_gain[:, i // 2:i // 2 + 1],
                        in1=ps[:, 4 + i, :].rearrange("p (k n) -> p k n", k=2), op0=ALU.mult, op1=ALU.mult)
                last.then_inc(hd_scaled, 1)
                ahead(b + 11)
                attention(0, 2, QK_DIM ** -0.5)
                head_scales(1, 4, 8, 1.0 / P, A_EPS)
                make_diag(8, hd_diag)
                for i in range(2):
                    y_rest(i + 1, work, 2 + i)
                dve.wait_ge(hd_rows, 2)
                for i in range(2):
                    v.scalar_tensor_tensor(
                        out=work[:, 2 * i:2 * i + 2, :], in0=out_sb[:, 2 * i:2 * i + 2, :], scalar=sub_gain[:, 0:1],
                        in1=ps[:, 6 + i, :].rearrange("p (k n) -> p k n", k=2), op0=ALU.mult, op1=ALU.mult)\
                        .then_inc(y_made, 1)
                for i in range(2):
                    y_rest(i + 3, work, i)

            def rope_angles():
                dve.wait_ge(rope_pow, 1)
                dve.wait_ge(rope_in, 16)
                v.tensor_copy(angle, pos_i)
                dve.drain()
                v.tensor_scalar(angle, angle, inv_freq[:, 2:3], None, ALU.mult)
                dve.drain()
                v.tensor_scalar(rope_k[:], angle, 1.0 / (2 * math.pi), None, ALU.mult)
                dve.drain()
                v.tensor_copy(turns_f, rope_k[:])
                two_pi = 2 * math.pi
                part1 = 6.28125
                part2 = round((two_pi - part1) * 2 ** 21) / 2 ** 21
                for part in (part1, part2, two_pi - part1 - part2):
                    dve.drain()
                    v.scalar_tensor_tensor(out=angle, in0=turns_f, scalar=-part, in1=angle, op0=ALU.mult, op1=ALU.add)
                dve.drain()
                v.tensor_scalar(angle, angle, 3.1415925, -3.1415925, ALU.min, ALU.max).then_inc(rope_conv, 1)

            def rope_cosines():
                dve.wait_ge(rope_sin, 1)
                v.tensor_tensor(cos_t[:], cos_t[:], cos_t[:], ALU.mult)
                dve.drain()
                v.tensor_scalar(cos_t[:], cos_t[:], -2.0, 1.0, ALU.mult, ALU.add)

            def gated(n):
                return lambda m: v.scalar_tensor_tensor(
                    out=x[:, m, :], in0=acc(m), scalar=gate_col[:, n, m:m + 1], in1=x[:, m, :],
                    op0=ALU.mult, op1=ALU.add).then_inc(x_new, 1)

            def mix_a1(b):
                for j in range(4):
                    n = b + 3 * j
                    ahead(n + 4)
                    chunk_done(n + 1)
                    dve.wait_ge(c_copied, j + 1)
                    v.tensor_tensor(vpad[:, :, 2:T + 2], c_sb[:], ps[:, 1, :].rearrange("p (k n) -> p k n", k=2), ALU.mult)\
                        .then_inc(cx_read, 1)
                    dve.drain()
                    for tap in range(3):
                        for i in range(2):
                            t = 2 * j + i
                            col = a_cols[:, 53 + 8 * tap + t:54 + 8 * tap + t]
                            if tap == 0:
                                v.tensor_scalar(work[:, t, :], vpad[:, i, 0:T], col, None, ALU.mult)
                            else:
                                v.scalar_tensor_tensor(out=work[:, t, :], in0=vpad[:, i, tap:T + tap], scalar=col,
                                                       in1=work[:, t, :], op0=ALU.mult, op1=ALU.add)
                        dve.drain()
                    if j < 3:
                        ahead(n + 5)
                    chunk_done(n + 2)
                    v.tensor_tensor(work[:, 2 * j:2 * j + 2, :], work[:, 2 * j:2 * j + 2, :],
                                    ps[:, 2, :].rearrange("p (k n) -> p k n", k=2), ALU.mult).then_inc(y_made, 1)
                    if j < 3:
                        ahead(n + 6)
                    y_rest(4 + j + 1, work, j)
                    ahead(n + 6)
                    if j == 2:
                        rope_angles()
                    elif j == 3:
                        rope_cosines()

            ahead(A_MIX[0] + 3)
            mix_a0(A_MIX[0])
            residual_chunks(A_MIX[0] + 8, 2, gated(1))
            norm_a(2)
            ffn(A_FFN[1], 1, 2)
            residual_a(2, 1, A_FFN[1] + FFN_CH - 1)
            norm_a(3)
            ffn(A_FFN[2], 2, 3)
            residual_a(3, 2, A_FFN[2] + FFN_CH - 1)
            norm_a(4)
            ahead(A_MIX[1] + 3)
            mix_a1(A_MIX[1])
            residual_chunks(A_MIX[1] + 12, 5, gated(4))
            norm_a(5)
            ffn(A_FFN[3], 3)
            residual_a(5, 3, A_FFN[3] + FFN_CH - 1)
            x_lo_rest(6, x)

            def mix_b(l):
                n0 = B_MIX

                def evacuated(g):
                    dve.wait_ge(evac, call_e(l, g + 1))

                def log_decay():
                    dve.wait_ge(ab_exp, l + 1)
                    v.tensor_scalar(gl[:, 5, :], gl[:, 2, :], 2.0, None, ALU.add)
                    v.tensor_scalar(gl[:, 10, :], gl[:, 3, :], 1.0, None, ALU.add)
                    dve.drain()
                    v.reciprocal(gl[:, 6, :], gl[:, 5, :])
                    v.reciprocal(gl[:, 10, :], gl[:, 10, :])
                    dve.drain()
                    v.tensor_tensor(gl[:, 6, :], gl[:, 2, :], gl[:, 6, :], ALU.mult)
                    dve.drain()
                    v.tensor_tensor(gl[:, 7, :], gl[:, 6, :], gl[:, 6, :], ALU.mult)
                    dve.drain()
                    v.tensor_scalar(gl[:, 5, :], gl[:, 7, :], 1.0 / 15, None, ALU.mult)
                    for odd in (13, 11, 9, 7, 5, 3):
                        dve.drain()
                        v.scalar_tensor_tensor(out=gl[:, 5, :], in0=gl[:, 5, :], scalar=1.0 / odd, in1=gl[:, 7, :],
                                               op0=ALU.add, op1=ALU.mult)
                    dve.drain()
                    v.scalar_tensor_tensor(out=gl[:, 5, :], in0=gl[:, 5, :], scalar=1.0, in1=gl[:, 6, :],
                                           op0=ALU.add, op1=ALU.mult)
                    v.tensor_scalar(gl[:, 0, :], gl[:, 0, :], 0.0, None, ALU.max)
                    dve.drain()
                    v.scalar_tensor_tensor(out=gl[:, 5, :], in0=gl[:, 5, :], scalar=2.0, in1=gl[:, 0, :],
                                           op0=ALU.mult, op1=ALU.add)
                    dve.drain()
                    v.scalar_tensor_tensor(out=gl[:, 9, :].rearrange("p (t h) -> p t h", t=TT),
                                           in0=gl[:, 5, :].rearrange("p (t h) -> p t h", t=TT), scalar=-1.0,
                                           in1=bc(gl[:, 4, 0:4].unsqueeze(1), (P, TT, 4)), op0=ALU.mult, op1=ALU.mult)

                tap_at = [0]

                def taps(n):
                    for sh in range(tap_at[0], tap_at[0] + n):
                        j = TAPS - 1 - sh
                        for t in (0, 1):
                            wcol = cols3[:, 4 * j + t:4 * j + t + 1]
                            if sh == 0:
                                v.tensor_scalar(conv[:, t, :], glu[:, t, :], wcol, cols1[:, CB_DW + t:CB_DW + t + 1],
                                                ALU.mult, ALU.add)
                            else:
                                v.scalar_tensor_tensor(out=conv[:, t, sh:T], in0=glu[:, t, 0:T - sh], scalar=wcol,
                                                       in1=conv[:, t, sh:T], op0=ALU.mult, op1=ALU.add)
                        dve.drain()
                    tap_at[0] += n

                def level(s):
                    return v.scalar_tensor_tensor(out=bmat, in0=bc(levels[:].unsqueeze(1), (P, 8, P)), scalar=s + 1.0,
                                                  in1=amat, op0=ALU.is_equal, op1=ALU.mult)

                for g in range(6):
                    ahead(n0 + g + 3)
                    evacuated(g)
                    for tap in (2, 1, 0):
                        sh = 3 - tap
                        for i in range(2):
                            t = 2 * g + i
                            last = v.scalar_tensor_tensor(
                                out=qkv[:, t, sh:T], in0=stage[:, T * i:T * i + T - sh],
                                scalar=cols2[:, 12 * tap + t:12 * tap + t + 1], in1=qkv[:, t, sh:T],
                                op0=ALU.mult, op1=ALU.add)
                        if tap:
                            dve.drain()
                    last.then_inc(conv_done, 1)
                    if g == 3:
                        dve.wait_ge(ab_copied, l * 2 + 2)
                        v.tensor_tensor(gl[:, 0, :].rearrange("p (t h) -> p t h", t=TT), ab[:, :, 0:4],
                                        bc(head_par[:, 1, :].unsqueeze(1), (P, TT, 4)), ALU.add)
                        dve.drain()
                        v.tensor_scalar(gl[:, 1, :], gl[:, 0, :], -1.0, None, ALU.mult)
                        dve.drain()
                        v.tensor_tensor(gl[:, 1, :], gl[:, 0, :], gl[:, 1, :], ALU.min).then_inc(ab_in, 1)
                    if g == 5:
                        log_decay()
                ahead(n0 + 9)
                head_scales(call_h(l, 0), 3, 16, 1.0, 1e-6)
                v.tensor_scalar(rstd[:, 0:8], rstd[:, 0:8], P ** -0.5, None, ALU.mult)
                dve.drain()
                make_diag(16, hd_diag)
                ahead(n0 + 11)
                dve.wait_ge(hd_rows, call_h(l, 0) + 1)
                for i in range(4):
                    last = v.tensor_tensor(qkv[:, 2 * i:2 * i + 2, :], qkv[:, 2 * i:2 * i + 2, :],
                                           ps[:, 4 + i, :].rearrange("p (k n) -> p k n", k=2), ALU.mult)
                last.then_inc(qk_hat, 1)
                v.tensor_copy(diag[:, 0:8, :], bc(gl[:, 9, :].unsqueeze(2), (P, 8, P)))
                v.tensor_copy(diag[:, 8:16, :], bc(gl[:, 10, :].unsqueeze(2), (P, 8, P))).then_inc(g_ready, 1)
                ahead(n0 + 12)
                evacuated(9)
                v.tensor_tensor(glu[:, 0:2, :], glu[:, 0:2, :], sig[:], ALU.mult).then_inc(glu_ready, 1)
                ahead(n0 + 13)
                dve.wait_ge(g_mm, l + 1)
                v.tensor_copy(gcol[:], ps[:, 3, 64:72])
                dve.drain()
                for c in range(2):
                    v.tensor_tensor(emat[:, 4 * c:4 * c + 4, :], ps[:, 4 + c, :].rearrange("p (h n) -> p h n", n=P),
                                    bc(gcol[:, 4 * c:4 * c + 4].unsqueeze(2), (P, 4, P)), ALU.subtract)
                v.tensor_tensor(gl[:, 11, 0:4], ps[:, 4, :].rearrange("p (h n) -> p h n", n=P)[:, :, P - 1],
                                gcol[:, 0:4], ALU.subtract)
                dve.drain()
                v.tensor_scalar(emat[:], emat[:], 0.0, None, ALU.min).then_inc(dec_in, 1)
                ahead(n0 + 14)
                evacuated(11)
                v.tensor_tensor(glu[:, 2:4, :], glu[:, 2:4, :], sig[:], ALU.mult).then_inc(glu_ready, 1)
                dve.wait_ge(dec_exp, l + 1)
                v.tensor_tensor(emat[:], emat[:], bc(tri[:].unsqueeze(1), (P, 8, P)), ALU.mult)
                v.tensor_tensor(q_dec[:], q_dec[:], qkv[:, 0:4, P:T], ALU.mult)
                v.tensor_tensor(gl[:, 7, 0:4], gl[:, 10, 4:8], gl[:, 8, 0:4], ALU.mult)
                ahead(n0 + 15)
                dve.drain()
                dve.wait_ge(kk_mm, l + 1)
                for c in range(2):
                    cs = slice(4 * c, 4 * c + 4)
                    v.tensor_tensor(amat[:, cs, :], emat[:, cs, :], ps[:, 4 + c, :].rearrange("p (h n) -> p h n", n=P), ALU.mult)
                    v.tensor_tensor(qk_dec[:, cs, :], emat[:, cs, :], ps[:, 6 + c, :].rearrange("p (h n) -> p h n", n=P), ALU.mult)
                dve.drain()
                v.tensor_tensor(amat[:], amat[:], tmat[:], ALU.mult).then_inc(a_ready, 1)
                dve.drain()
                level(0)
                dve.drain()
                v.tensor_tensor(emat[:], bmat[:], bc(ident[:].unsqueeze(1), (P, 8, P)), ALU.add).then_inc(e_first, 1)
                dve.drain()
                level(1).then_inc(b_ready, 1)
                ahead(n0 + 17)
                dve.wait_ge(tok_mm, l + 1)
                for c in range(2):
                    col = gl[:, 8, 4:8] if c == 0 else gl[:, 7, 0:4]
                    v.tensor_tensor(k_tok[:, c, :].rearrange("p (h n) -> p h n", n=P),
                                    ps[:, 4 + c, :].rearrange("p (h n) -> p h n", n=P),
                                    bc(col.unsqueeze(2), (P, 4, P)), ALU.mult)
                    last = v.tensor_tensor(v_beta[:, c, :].rearrange("p (h n) -> p h n", n=P),
                                           ps[:, 6 + c, :].rearrange("p (h n) -> p h n", n=P),
                                           bc(gl[:, 10, 4 * c:4 * c + 4].unsqueeze(2), (P, 4, P)), ALU.mult)
                last.then_inc(tok_done, 1)
                ahead(n0 + 19)
                def d_out(value):
                    for h in range(2):
                        dve.wait_ge(d_mm, value + h)
                        v.tensor_copy(dmat[:, 4 * h:4 * h + 4, :], ps[:, 6 + h, :].rearrange("p (h n) -> p h n", n=P))\
                            .then_inc(d_copied, 1)

                d_out(l * HALVES + 1)
                for s in range(1, LEVELS):
                    if s + 1 < LEVELS:
                        dve.wait_ge(t_mm, l * HALVES + 2 * s)
                        level(s + 1).then_inc(b_ready, 1)
                        d_out(l * HALVES + (2 * s + 1))
                    taps(2)
                    if s == 1:
                        ahead(n0 + 20)
                taps(5)
                dve.wait_ge(s_mm, l + 1)
                v.tensor_copy(s_state[:], ps[:, 7, :].rearrange("p (h n) -> p h n", n=P)).then_inc(s_ready, 1)
                taps(1)
                dve.wait_ge(ws_mm, l + 1)
                v.tensor_tensor(u_sb[:, 4:8, :], u_sb[:, 4:8, :], ps[:, 4, :].rearrange("p (h n) -> p h n", n=P), ALU.subtract)\
                    .then_inc(v_new, 1)
                taps(4)
                ahead(n0 + 21)
                head_scales(call_h(l, 1), 3, 8, 1.0 / P, B_EPS, lambda: taps(2))
                make_diag(8, hd_diag)
                taps(1)
                ahead(n0 + 22)
                dve.wait_ge(hd_rows, call_h(l, 1) + 1)
                for i in range(2):
                    sl = slice(2 * i, 2 * i + 2)
                    v.scalar_tensor_tensor(out=work[:, sl, :], in0=out_sb[:, sl, :], scalar=cols1[:, CB_DN:CB_DN + 1],
                                           in1=ps[:, 4 + i, :].rearrange("p (k n) -> p k n", k=2),
                                           op0=ALU.mult, op1=ALU.mult)
                    dve.drain()
                    v.tensor_tensor(work[:, sl, :], work[:, sl, :], z_act[:, sl, :], ALU.mult).then_inc(y_made, 1)
                for i in range(2):
                    y_rest(call_y(l, i + 1), work, i)
                ahead(n0 + 23)
                taps(2)
                ahead(n0 + 24)
                taps(TAPS - tap_at[0])
                dve.drain().then_inc(cv_dve, 1)
                ahead(n0 + 25)
                chunk_done(n0 + 22)
                for i in range(4):
                    last = v.tensor_tensor(merged[:, 2 * i:2 * i + 2, :], gate[:, 2 * i:2 * i + 2, :],
                                           ps[:, 4 + i, :].rearrange("p (k n) -> p k n", k=2), ALU.mult)
                last.then_inc(branch_free, 1)
                ahead(n0 + 26)
                dve.wait_ge(hd_stats, call_h(l, 2) + 1)
                mean_moments(3, 512, B_EPS, hd_moment)
                ahead(n0 + 27)
                dve.wait_ge(hd_rstd, call_h(l, 2) + 1)
                mean_scales()
                make_diag(4, hd_diag)
                ahead(n0 + 28)
                dve.wait_ge(hd_rows, call_h(l, 2) + 1)
                for i in range(2):
                    pair = conv[:, 2 * i:2 * i + 2, :]
                    v.tensor_tensor(pair, pair, bc(ps[:, 3, 0:T].unsqueeze(1), (P, 2, T)), ALU.mult)
                    dve.drain()
                    v.tensor_tensor(pair, pair, bc(ps[:, 3, T:2 * T].unsqueeze(1), (P, 2, T)), ALU.add)\
                        .then_inc(cv_scaled, 1)
                for i in range(2):
                    y_rest(call_y(l, 3 + i), work, 2 + i)
                ahead(n0 + 30)
                chunk_done(n0 + 28)
                for m in range(KT):
                    v.scalar_tensor_tensor(out=gate[:, m, :], in0=acc(m), scalar=cols1[:, CB_PW2 + m:CB_PW2 + m + 1],
                                           in1=gate[:, m, :], op0=ALU.add, op1=ALU.mult)
                dve.drain()
                v.tensor_tensor(merged[:], merged[:], gate[:], ALU.add).then_inc(branch_free, 1)
                dve.wait_ge(hd_stats, call_h(l, 3) + 1)
                v.tensor_scalar(moment[:, 0:2], ps[:, 3, 0:2], 1.0 / 384, B_EPS, ALU.mult, ALU.add)
                v.tensor_scalar(moment[:, 2:4], ps[:, 3, 2:4], 1.0 / 256, B_EPS, ALU.mult, ALU.add).then_inc(hd_moment, 1)
                ahead(n0 + 31)
                dve.wait_ge(hd_rstd, call_h(l, 3) + 1)
                make_diag(4, hd_diag)
                ahead(n0 + 32)
                dve.wait_ge(hd_rows, call_h(l, 3) + 1)
                for i in range(5):
                    r = 0 if i < 3 else T
                    last = v.scalar_tensor_tensor(out=low[:, i, :], in0=low[:, i, :], scalar=cols1[:, CB_QN + i:CB_QN + i + 1],
                                                  in1=ps[:, 3, r:r + T], op0=ALU.mult, op1=ALU.mult)
                last.then_inc(hd_scaled, 1)
                ahead(n0 + 34)
                dve.wait_ge(rot_mm, l + 1)
                v.tensor_tensor(rot_q[:], ps[0:64, 4:6, :].rearrange("p b (k n) -> p (b k) n", k=2),
                                bc(sin_t[:].unsqueeze(1), (64, HEADS, T)), ALU.mult)
                v.tensor_tensor(rot_k, ps[0:64, 3, 0:T], sin_t[:], ALU.mult)
                v.tensor_tensor(q_rope[:], q_rope[:], bc(cos_t[:].unsqueeze(1), (64, HEADS, T)), ALU.mult)
                v.tensor_tensor(k_rope[:], k_rope[:], cos_t[:], ALU.mult)
                dve.drain()
                v.tensor_tensor(q_rope[:], q_rope[:], rot_q[:], ALU.add)
                v.tensor_tensor(k_rope[:], k_rope[:], rot_k, ALU.add).then_inc(rope_done, 1)
                ahead(n0 + 35)
                attention(l * 8 + 8, 1, 192 ** -0.5)
                for i in range(2):
                    y_rest(call_y(l, 5 + i), work, 2 + i)
                ahead(n0 + 36)
                for i in range(5):
                    if i == 0:
                        chunk_done(n0 + 33)
                    elif i == 2:
                        ahead(n0 + 37)
                        chunk_done(n0 + 34)
                    if i < 4:
                        sl = slice(2 * i, 2 * i + 2)
                        v.tensor_tensor(gate[:, sl, :], gate[:, sl, :], ps[:, 4 + i, :].rearrange("p (k n) -> p k n", k=2),
                                        ALU.mult)
                        dve.drain()
                        v.tensor_tensor(merged[:, sl, :], merged[:, sl, :], gate[:, sl, :], ALU.add).then_inc(y_made, 1)
                    if i:
                        y_rest(call_y(l, 6 + i), merged, i - 1)
                residual_chunks(n0 + 35, call_n(l, 1), lambda m: v.scalar_tensor_tensor(
                    out=x[:, m, :], in0=x[:, m, :], scalar=ALPHA, in1=acc(m), op0=ALU.mult, op1=ALU.add)
                    .then_inc(x_new, 1))

            assert at.n == limit[0]
            with dve.Fori(0, 2) as l:
                at.turns = l * LAYER_TURNS
                at.n = B0 + EARLY
                limit[0] = B0 + EARLY + B_LAYER_CH
                col = lambda c0: (lambda k: cols1[:, c0 + k:c0 + k + 1])

                def columns():
                    dve.wait_ge(lay_turned, l + 1)
                    v.tensor_copy(cols1[:], ps[:, 2, 0:106])
                    v.tensor_copy(cols2[:], ps[:, 2, 128:176])
                    v.tensor_copy(cols3[:], ps[:, 2, 256:380])
                    dve.drain().then_inc(lay_cols, 1)

                ffn(B0, l * 2 + 4, after_rest=columns)
                residual_b(2 * ALPHA, l * 2 + 4, B_FFN[0] + FFN_CH - 1, call_n(l, 0))
                norm_b(call_n(l, 0), call_x(l, 0), col(LN_G[0]), col(LN_B[0]), 4 * B_EPS)
                ahead(B_MIX + 3)
                mix_b(l)
                norm_b(call_n(l, 1), call_x(l, 1), col(LN_G[1]), col(LN_B[1]), B_EPS)
                ffn(B_FFN[1], l * 2 + 5)
                residual_b(2 * ALPHA, l * 2 + 5, B_FFN[1] + FFN_CH - 1, call_n(l, 2))
                norm_b(call_n(l, 2), call_x(l, 2), col(LN_G[2]), col(LN_B[2]), 4 * B_EPS)
                assert at.n == limit[0]


_OUT = ("out_0_dram", (1, 256, 1024))


def kernel(**inputs):
    import numpy as _np
    import concourse.bacc as _bacc
    from concourse import mybir as _mybir
    from concourse.bass_utils import run_bass_kernel_spmd as _run

    nc = _bacc.Bacc("TRN2", target_bir_lowering=False, num_devices=1)
    arrays, args = {}, {}
    for name in inputs:
        v = _np.ascontiguousarray(inputs[name])
        arrays[f"in_{name}_dram"] = v
        args[name] = nc.dram_tensor(f"in_{name}_dram", v.shape, _mybir.dt.from_np(v.dtype), kind="ExternalInput").ap()
    out = nc.dram_tensor(_OUT[0], _OUT[1], _mybir.dt.float32, kind="ExternalOutput").ap()
    block_kernel(nc, args, out)
    r = _run(nc, [arrays], core_ids=[0])
    return r.results[0][_OUT[0]]
```
